# Optimizing a Trainium2 kernel written in Bass

```python
import math
import jax, jax.numpy as jnp
from jax import lax
import numpy as np

D_MODEL = 1024
BATCH = 1
SEQ = 512
DEPTH = 4
DEC_BATCH = 8
DEC_SEQ = 4
PAST_LEN = 512
PAGE_SIZE = 128

A_GROUPS = ((128, 1), (512, 4), (2048, 16))
N_GROUPS_A = len(A_GROUPS)
HG_A = 6
HD_A = 64
ROPE_THETA = 10000.0
A_PROJ = N_GROUPS_A * 3 * HG_A * HD_A
A_OUT = N_GROUPS_A * HG_A * HD_A
H_B = D_MODEL // 128
DK_B = 128
DV_B = 128
CONV_W = 4
CHUNK_B = 64
B_QKV = 3 * H_B * DK_B
B_PROJ = B_QKV + H_B * DV_B + 2 * H_B
POOL_WINDOWS = (2, 4, 8, 16)
POOL_CG = D_MODEL // len(POOL_WINDOWS)
POOL_BUF = max(POOL_WINDOWS) - 1
D_FF = 4 * D_MODEL
N_A = (DEPTH + 2) // 3
N_B = (DEPTH + 1) // 3
N_C = DEPTH // 3
RMS_EPS = 1e-6

kernel_name = 'hybrid_dilated_delta_pool_step'

def rmsnorm(x, g):
    xf = x.astype(jnp.float32)
    y = xf * lax.rsqrt(jnp.mean(xf * xf, axis=-1, keepdims=True) + RMS_EPS)
    return (y * g.astype(jnp.float32)).astype(x.dtype)

def l2norm(x):
    return x * lax.rsqrt(jnp.sum(x * x, axis=-1, keepdims=True) + 1e-6)

def rope(x, pos):
    half = x.shape[-1] // 2
    inv = ROPE_THETA ** (-jnp.arange(half, dtype=jnp.float32) / half)
    ang = pos.astype(jnp.float32)[:, None] * inv[None, :]
    cos = jnp.cos(ang)[:, None, :]
    sin = jnp.sin(ang)[:, None, :]
    xf = x.astype(jnp.float32)
    x1, x2 = xf[..., :half], xf[..., half:]
    return jnp.concatenate([x1 * cos - x2 * sin, x2 * cos + x1 * sin], axis=-1)

def dilated_window_prompt(q, k, v, window, dil):
    B, S, H, hd = q.shape
    n = S // dil
    blk = window // dil
    nb = -(-n // blk)
    npad = nb * blk

    def to_blocks(x):
        x = x.astype(jnp.float32).reshape(B, n, dil, H, hd).transpose(0, 2, 1, 3, 4)
        x = jnp.pad(x, ((0, 0), (0, 0), (0, npad - n), (0, 0), (0, 0)))
        return x.reshape(B, dil, nb, blk, H, hd)

    def with_prev(x):
        prev = jnp.concatenate([jnp.zeros_like(x[:, :, :1]), x[:, :, :-1]], axis=2)
        return jnp.concatenate([prev, x], axis=3)

    qb = to_blocks(q)
    kk = with_prev(to_blocks(k))
    vv = with_prev(to_blocks(v))
    s = jnp.einsum('brnqhd,brnkhd->brnhqk', qb, kk) * (hd ** -0.5)
    qi = jnp.arange(blk)[:, None]
    kj = jnp.arange(2 * blk)[None, :]
    dist = blk + qi - kj
    band = (dist >= 0) & (dist <= blk)
    has_prev = (jnp.arange(nb)[:, None, None] > 0) | (kj[None] >= blk)
    mask = band[None] & has_prev
    s = jnp.where(mask[None, None, :, None], s, -jnp.inf)
    m = jnp.max(s, axis=-1)
    p = jnp.exp(s - m[..., None])
    l = jnp.sum(p, axis=-1)
    o = jnp.einsum('brnhqk,brnkhd->brnqhd', p, vv) / jnp.swapaxes(l, -1, -2)[..., None]
    lse = jnp.swapaxes(m + jnp.log(l), -1, -2)

    def from_blocks(x):
        x = x.reshape((B, dil, npad) + x.shape[4:])[:, :, :n]
        x = jnp.swapaxes(x, 1, 2)
        return x.reshape((B, S) + x.shape[3:])

    return from_blocks(o), from_blocks(lse)

def dilated_window_sample(q, k, v, buf, window, dil):
    T = q.shape[1]
    L = buf.shape[1]
    hd = q.shape[-1]
    kc = jnp.concatenate([buf[:, :, 0].astype(jnp.float32), k], axis=1)
    vc = jnp.concatenate([buf[:, :, 1].astype(jnp.float32), v], axis=1)
    offs = jnp.arange(window // dil + 1) * dil
    idx = L + jnp.arange(T)[:, None] - offs[None, :]
    valid = idx >= 0
    idx = jnp.maximum(idx, 0)
    kg = kc[:, idx]
    vg = vc[:, idx]
    s = jnp.einsum('bthd,btmhd->bthm', q.astype(jnp.float32), kg) * (hd ** -0.5)
    s = jnp.where(valid[None, :, None, :], s, -jnp.inf)
    m = jnp.max(s, axis=-1)
    p = jnp.exp(s - m[..., None])
    l = jnp.sum(p, axis=-1)
    o = jnp.einsum('bthm,btmhd->bthd', p, vg) / l[..., None]
    new_buf = jnp.stack([kc[:, T:], vc[:, T:]], axis=2)
    return o, m + jnp.log(l), new_buf

def mixer_a(h, w_in, w_out, pos, bufs):
    B, T, _ = h.shape
    qkv = (h @ w_in).reshape(B, T, N_GROUPS_A, 3, HG_A, HD_A)
    outs, lses, new_bufs = [], [], []
    for g, (window, dil) in enumerate(A_GROUPS):
        q = rope(qkv[:, :, g, 0], pos)
        k = rope(qkv[:, :, g, 1], pos)
        v = qkv[:, :, g, 2].astype(jnp.float32)
        if bufs is None:
            o, lse = dilated_window_prompt(q, k, v, window, dil)
            keep = min(window, T)
            nbuf = jnp.stack([k[:, T - keep:], v[:, T - keep:]], axis=2)
        else:
            o, lse, nbuf = dilated_window_sample(q, k, v, bufs[g], window, dil)
        outs.append(o)
        lses.append(lse)
        new_bufs.append(nbuf)
    wts = jax.nn.softmax(jnp.stack(lses, axis=2), axis=2)
    o = (jnp.stack(outs, axis=2) * wts[..., None]).reshape(B, T, A_OUT)
    return o.astype(h.dtype) @ w_out, new_bufs

def gated_delta_chunked(q, k, v, g, beta, s0):
    B, T, H, dk = q.shape
    dv = v.shape[-1]
    C = min(CHUNK_B, T)
    N = -(-T // C)
    pad = N * C - T

    def prep(x):
        x = jnp.pad(x.astype(jnp.float32), [(0, 0), (0, pad)] + [(0, 0)] * (x.ndim - 2))
        x = x.reshape((B, N, C, H) + x.shape[3:])
        return jnp.moveaxis(x, 3, 1)

    q, k, v, g, beta = prep(q), prep(k), prep(v), prep(g), prep(beta)
    G = jnp.cumsum(g, axis=-1)
    tri = jnp.tril(jnp.ones((C, C), bool))
    stri = jnp.tril(jnp.ones((C, C), bool), -1)
    dec = jnp.exp(jnp.where(tri, G[..., :, None] - G[..., None, :], -jnp.inf))
    kb = k * beta[..., None]
    A = jnp.where(stri, jnp.einsum('bhncd,bhnsd->bhncs', kb, k) * dec, 0.0)
    eye = jnp.eye(C, dtype=jnp.float32)
    Tm = lax.linalg.triangular_solve(eye + A, jnp.broadcast_to(eye, A.shape), left_side=True, lower=True)
    u = jnp.einsum('bhncs,bhnse->bhnce', Tm, v * beta[..., None])
    w = jnp.einsum('bhncs,bhnsd->bhncd', Tm, kb * jnp.exp(G)[..., None])
    attn = jnp.einsum('bhncd,bhnsd->bhncs', q, k) * dec
    qe = q * jnp.exp(G)[..., None]
    Gl = G[..., -1:]
    kd = k * jnp.exp(Gl - G)[..., None]
    dl = jnp.exp(Gl[..., 0])

    def step(S, xs):
        qe_i, u_i, w_i, attn_i, kd_i, dl_i = xs
        v_new = u_i - jnp.einsum('bhcd,bhde->bhce', w_i, S)
        o_i = jnp.einsum('bhcd,bhde->bhce', qe_i, S) + jnp.einsum('bhcs,bhse->bhce', attn_i, v_new)
        S = S * dl_i[..., None, None] + jnp.einsum('bhcd,bhce->bhde', kd_i, v_new)
        return S, o_i

    xs = tuple(jnp.moveaxis(x, 2, 0) for x in (qe, u, w, attn, kd, dl))
    S, o = lax.scan(step, s0.astype(jnp.float32), xs)
    o = jnp.moveaxis(jnp.moveaxis(o, 0, 2), 1, 3).reshape(B, N * C, H, dv)[:, :T]
    return o, S

def mixer_b(h, conv_buf, s0, w_in, conv_w, a_log, dt_bias, norm_w, w_out):
    B, T, _ = h.shape
    proj = h @ w_in
    o1 = B_QKV + H_B * DV_B
    xqkv = proj[..., :B_QKV]
    z = proj[..., B_QKV:o1].reshape(B, T, H_B, DV_B).astype(jnp.float32)
    a = proj[..., o1:o1 + H_B].astype(jnp.float32)
    b = proj[..., o1 + H_B:].astype(jnp.float32)
    xp = jnp.concatenate([conv_buf.astype(xqkv.dtype), xqkv], axis=1)
    c = xp[:, 0:T] * conv_w[0]
    for j in range(1, CONV_W):
        c = c + xp[:, j:j + T] * conv_w[j]
    c = jax.nn.silu(c.astype(jnp.float32))
    q = l2norm(c[..., :H_B * DK_B].reshape(B, T, H_B, DK_B)) * (DK_B ** -0.5)
    k = l2norm(c[..., H_B * DK_B:2 * H_B * DK_B].reshape(B, T, H_B, DK_B))
    v = c[..., 2 * H_B * DK_B:].reshape(B, T, H_B, DV_B)
    beta = jax.nn.sigmoid(b)
    g = -jnp.exp(a_log.astype(jnp.float32)) * jax.nn.softplus(a + dt_bias.astype(jnp.float32))
    o, s_new = gated_delta_chunked(q, k, v, g, beta, s0)
    o = rmsnorm(o, norm_w) * jax.nn.silu(z)
    y = o.reshape(B, T, H_B * DV_B).astype(h.dtype) @ w_out
    return y, xp[:, xp.shape[1] - (CONV_W - 1):], s_new

def mixer_c(h, prefix, n_valid, w_grp, scale):
    B, T, D = h.shape
    P = prefix.shape[1]
    xp = jnp.concatenate([prefix.astype(h.dtype), h], axis=1)
    xpf = xp.astype(jnp.float32)
    cs = jnp.concatenate([jnp.zeros((B, 1, D), jnp.float32), jnp.cumsum(xpf, axis=1)], axis=1)
    t = jnp.arange(T)
    end = P + t + 1
    hf = xpf[:, P:]
    diffs = []
    for gi, w in enumerate(POOL_WINDOWS):
        lo, hi = gi * POOL_CG, (gi + 1) * POOL_CG
        tot = cs[:, end, lo:hi] - cs[:, end - w, lo:hi]
        cnt = jnp.minimum(w, t + 1 + n_valid).astype(jnp.float32)
        diffs.append(tot / cnt[None, :, None] - hf[..., lo:hi])
    d = jnp.stack(diffs, axis=2)
    y = jnp.einsum('btgc,gce->btge', d, w_grp.astype(jnp.float32)).reshape(B, T, D) * scale.astype(jnp.float32)
    return y.astype(h.dtype), xp[:, T:]

def sq_relu_mlp(h, w1, w2):
    return jnp.square(jax.nn.relu(h @ w1)) @ w2

def setup_inputs(seed: int = 0) -> dict:
    key = jax.random.key(seed)
    ks = iter(jax.random.split(key, 32))

    def nrm(shape, scale=1.0):
        return jax.random.normal(next(ks), shape, jnp.float32) * scale

    x_prompt = nrm((BATCH, SEQ, D_MODEL))
    x_sample = nrm((DEC_BATCH, DEC_SEQ, D_MODEL))
    cache_a_kv1 = nrm((N_A, DEC_BATCH, min(A_GROUPS[0][0], PAST_LEN), 2, HG_A, HD_A))
    cache_a_kv2 = nrm((N_A, DEC_BATCH, min(A_GROUPS[1][0], PAST_LEN), 2, HG_A, HD_A))
    cache_a_kv3 = nrm((N_A, DEC_BATCH, min(A_GROUPS[2][0], PAST_LEN), 2, HG_A, HD_A))
    state_b_s = nrm((N_B, DEC_BATCH, H_B, DK_B, DV_B), 0.1)
    state_b_conv = nrm((N_B, DEC_BATCH, CONV_W - 1, B_QKV))
    state_c_pool = nrm((N_C, DEC_BATCH, min(POOL_BUF, PAST_LEN), D_MODEL))
    norm1 = 1.0 + nrm((DEPTH, D_MODEL), 0.02)
    norm2 = 1.0 + nrm((DEPTH, D_MODEL), 0.02)
    norm_f = 1.0 + nrm((D_MODEL,), 0.02)
    a_w_in = nrm((N_A, D_MODEL, A_PROJ), D_MODEL ** -0.5)
    a_w_out = nrm((N_A, A_OUT, D_MODEL), A_OUT ** -0.5)
    b_w_in = nrm((N_B, D_MODEL, B_PROJ), D_MODEL ** -0.5)
    b_conv = nrm((N_B, CONV_W, B_QKV), CONV_W ** -0.5)
    b_a_log = jnp.log(jax.random.uniform(next(ks), (N_B, H_B), jnp.float32, 1.0, 16.0))
    dt = jnp.exp(jax.random.uniform(next(ks), (N_B, H_B), jnp.float32) * (math.log(0.1) - math.log(0.001)) + math.log(0.001))
    b_dt_bias = dt + jnp.log(-jnp.expm1(-dt))
    b_norm = 1.0 + nrm((N_B, DV_B), 0.02)
    b_w_out = nrm((N_B, H_B * DV_B, D_MODEL), (H_B * DV_B) ** -0.5)
    c_w = nrm((N_C, len(POOL_WINDOWS), POOL_CG, POOL_CG), POOL_CG ** -0.5)
    c_scale = 1.0 + nrm((N_C, D_MODEL), 0.1)
    mlp_w1 = nrm((DEPTH, D_MODEL, D_FF), D_MODEL ** -0.5)
    mlp_w2 = nrm((DEPTH, D_FF, D_MODEL), D_FF ** -0.5)
    return {'x_prompt': x_prompt, 'x_sample': x_sample,
            'cache_a_kv1': cache_a_kv1, 'cache_a_kv2': cache_a_kv2, 'cache_a_kv3': cache_a_kv3,
            'state_b_s': state_b_s, 'state_b_conv': state_b_conv, 'state_c_pool': state_c_pool,
            'norm1': norm1, 'norm2': norm2, 'norm_f': norm_f,
            'a_w_in': a_w_in, 'a_w_out': a_w_out,
            'b_w_in': b_w_in, 'b_conv': b_conv, 'b_a_log': b_a_log, 'b_dt_bias': b_dt_bias,
            'b_norm': b_norm, 'b_w_out': b_w_out,
            'c_w': c_w, 'c_scale': c_scale,
            'mlp_w1': mlp_w1, 'mlp_w2': mlp_w2}

def reference(x_prompt, x_sample, cache_a_kv1, cache_a_kv2, cache_a_kv3, state_b_s, state_b_conv, state_c_pool,
              norm1, norm2, norm_f, a_w_in, a_w_out, b_w_in, b_conv, b_a_log, b_dt_bias, b_norm, b_w_out,
              c_w, c_scale, mlp_w1, mlp_w2):
    xp, xs = x_prompt, x_sample
    Bp, Sp = xp.shape[0], xp.shape[1]
    Ts = xs.shape[1]
    pos_p = jnp.arange(Sp)
    pos_s = PAST_LEN + jnp.arange(Ts)
    a_p, a_s, b_p, b_s, c_p, c_s = [], [], [], [], [], []
    for i in range(DEPTH):
        kind, j = i % 3, i // 3
        hp = rmsnorm(xp, norm1[i])
        hs = rmsnorm(xs, norm1[i])
        if kind == 0:
            yp, kv_p = mixer_a(hp, a_w_in[j], a_w_out[j], pos_p, None)
            ys, kv_s = mixer_a(hs, a_w_in[j], a_w_out[j], pos_s, (cache_a_kv1[j], cache_a_kv2[j], cache_a_kv3[j]))
            a_p.append(kv_p)
            a_s.append(kv_s)
        elif kind == 1:
            conv0 = jnp.zeros((Bp, CONV_W - 1, B_QKV), hp.dtype)
            s0 = jnp.zeros((Bp, H_B, DK_B, DV_B), jnp.float32)
            yp, cb_p, sb_p = mixer_b(hp, conv0, s0, b_w_in[j], b_conv[j], b_a_log[j], b_dt_bias[j], b_norm[j], b_w_out[j])
            ys, cb_s, sb_s = mixer_b(hs, state_b_conv[j], state_b_s[j], b_w_in[j], b_conv[j], b_a_log[j], b_dt_bias[j], b_norm[j], b_w_out[j])
            b_p.append((sb_p, cb_p))
            b_s.append((sb_s, cb_s))
        else:
            yp, pool_p = mixer_c(hp, jnp.zeros((Bp, POOL_BUF, D_MODEL), hp.dtype), 0, c_w[j], c_scale[j])
            ys, pool_s = mixer_c(hs, state_c_pool[j], state_c_pool.shape[2], c_w[j], c_scale[j])
            c_p.append(pool_p)
            c_s.append(pool_s)
        xp = xp + yp
        xs = xs + ys
        xp = xp + sq_relu_mlp(rmsnorm(xp, norm2[i]), mlp_w1[i], mlp_w2[i])
        xs = xs + sq_relu_mlp(rmsnorm(xs, norm2[i]), mlp_w1[i], mlp_w2[i])
    y_prompt = rmsnorm(xp, norm_f)
    y_sample = rmsnorm(xs, norm_f)
    new_a_kv1_p = jnp.stack([e[0] for e in a_p])
    new_a_kv2_p = jnp.stack([e[1] for e in a_p])
    new_a_kv3_p = jnp.stack([e[2] for e in a_p])
    new_b_s_p = jnp.stack([e[0] for e in b_p])
    new_b_conv_p = jnp.stack([e[1] for e in b_p])
    new_c_pool_p = jnp.stack(c_p)
    new_a_kv1_s = jnp.stack([e[0] for e in a_s])
    new_a_kv2_s = jnp.stack([e[1] for e in a_s])
    new_a_kv3_s = jnp.stack([e[2] for e in a_s])
    new_b_s_s = jnp.stack([e[0] for e in b_s])
    new_b_conv_s = jnp.stack([e[1] for e in b_s])
    new_c_pool_s = jnp.stack(c_s)
    return (y_prompt, y_sample, new_a_kv1_p, new_a_kv2_p, new_a_kv3_p, new_b_s_p, new_b_conv_p, new_c_pool_p, new_a_kv1_s, new_a_kv2_s, new_a_kv3_s, new_b_s_s, new_b_conv_s, new_c_pool_s)


_drawn_inputs = setup_inputs


def setup_inputs(seed=0):
    import zlib

    import numpy as np

    out = dict(_drawn_inputs(seed))
    spreads = {}
    factors = {}
    for name, (base, spread) in spreads.items():
        noise = np.random.default_rng([zlib.crc32(name.encode()), seed]).standard_normal(out[name].shape)
        drawn = base * np.exp(spread * noise) if base else spread * noise
        out[name] = __import__('jax').numpy.asarray(drawn.astype(out[name].dtype))
    for name, factor in factors.items():
        out[name] = (out[name] * factor).astype(out[name].dtype)
    return out
```

```python
from contextlib import ExitStack

import numpy as np
import concourse.bass as bass
from concourse import mybir

F32 = mybir.dt.float32
F32R = mybir.dt.float32r
ALU = mybir.AluOpType
ACT = mybir.ActivationFunctionType
AX = mybir.AxisListType.X

P = 128
D = 1024
KD = D // P
SEQ = 512
DEC_B = 8
DEC_T = 4
NS = DEC_B * DEC_T
TOK = SEQ + NS
HALF = TOK // 2
QT = SEQ // P
DEPTH = 4
FF = 4 * D
FQ = 4
EPS = 1e-6
SLOTS = 4
RAW = 2
KMAX = 9


COPY_PIECES = [(g, 127 * i, 127) for g in (2, 3) for i in range(4)] + [(1, 0, 124)]
COPIES = len(COPY_PIECES)


def build_step(nc, aps):
    layers = range(DEPTH)
    phases = []
    for l in layers:
        if l % 3 == 0:
            phases += [("a_in", l, 27), ("a_out", l, 8)]
        elif l % 3 == 1:
            phases += [("b_in", l, 32), ("b_out", l, 8)]
        phases.append(("mlp", l, 64))
    base, used = {}, {}
    total, per_slot = 0, [0] * RAW
    order = []
    raw_last = [None] * RAW
    found = {}
    for name, l, tiles in phases:
        base[name, l], used[name, l] = total, list(per_slot)
        found[name, l] = list(raw_last)
        order.append((name, l, tiles))
        for pos in range(tiles):
            per_slot[pos % RAW] += 1
            raw_last[pos % RAW] = total + pos
        total += tiles

    class WeightTile:

        def __init__(self, name, l, pos, q=0):
            tiles = dict(((a, b), c) for a, b, c in order)[name, l]
            if isinstance(q, int) and pos + 16 * q >= tiles:
                at = [(a, b) for a, b, _ in order].index((name, l)) + 1
                pos, q = pos + 16 * q - tiles, 0
                name, l = order[at][:2] if at < len(order) else (None, None)
            self.name, self.l, self.pos, self.q = name, l, pos, q
            if name is None:
                return
            self.slot = pos % SLOTS
            self.n = base[name, l] + pos + 16 * q
            self.first = base[name, l] + pos
            self.raw = pos % RAW
            self.landed = 16 * (used[name, l][self.raw] + pos // RAW + 1 + 8 * q)
            before = found[name, l][self.raw]
            self.raw_free = self.n - RAW + 1 if pos >= RAW else None if before is None else before + 1
            self.kt = KMAX if name == "a_out" else KD

    norms = [2 * l + s for l in layers for s in (0, 1)] + [2 * DEPTH]
    norm_no = {m: i for i, m in enumerate(norms)}
    split_norms = [m for m in norms if m != 2 * DEPTH and not (m % 2 == 0 and (m // 2) % 3 == 2)]
    split_no = {m: i for i, m in enumerate(split_norms)}

    with ExitStack() as ctx:
        def sb(name, shape, dt=F32):
            return ctx.enter_context(nc.sbuf_tensor(name, shape, dt))

        def sem(name):
            return ctx.enter_context(nc.semaphore(name))

        x = sb("x", [P, KD, TOK])
        w_raw = sb("w_raw", [P, RAW, KMAX, P])
        w_hi = sb("w_hi", [P, SLOTS, KMAX, P], F32R)
        w_lo = sb("w_lo", [P, SLOTS, KMAX, P], F32R)
        work = {}
        with ExitStack() as place:
            for name in ("e1", "e2", "eg", "kbe", "kd", "vb", "T", "U", "Z"):
                work[f"b_{name}"] = place.enter_context(nc.sbuf_tensor(f"b_{name}", [P, 2, 4, P], F32))
            work["b_dmask"] = place.enter_context(nc.sbuf_tensor("b_dmask", [P, 4, P], F32))
        act_hi = sb("act_hi", [P, KMAX, TOK], F32R)
        act_lo = sb("act_lo", [P, KMAX, TOK], F32R)
        R = sb("R", [P, TOK])
        ident = sb("ident", [P, P])
        ones = sb("ones", [P, P])
        gains = sb("gains", [P, 2 * DEPTH + 2, KD])
        gain_rows = sb("gain_rows", [(2 * DEPTH + 2) * KD, P])
        sumsq = sb("sumsq", [P, TOK])
        sq = sb("sq", [P, TOK])
        std = sb("std", [P, QT + 1])
        rstd = sb("rstd", [P, QT + 1])
        diag = sb("diag", [P, QT + 1, P])
        eps_col = sb("eps_col", [P, 1])
        with ExitStack() as local:
            def lsb(name, shape, dt=F32):
                return local.enter_context(nc.sbuf_tensor(name, shape, dt))
            h_hi = lsb("h_hi", [P, KD, TOK], F32R)
            h_lo = lsb("h_lo", [P, KD, TOK], F32R)
            relu_t = lsb("relu_t", [P, 2, TOK])
            h32 = lsb("h32", [P, 2, TOK])
        with ExitStack() as local:
            x_in = lsb("x_in", [P, QT + 1, D])
        with ExitStack() as local:
            y_T = lsb("y_T", [P, 2, TOK])
            y_out = lsb("y_out", [P, QT + 1, D])

        acc = ctx.enter_context(nc.psum_tensor("acc", [P, 2, 2, 512], F32))
        misc = [ctx.enter_context(nc.psum_tensor(f"misc{i}", [P, 512], F32)) for i in range(4)]

        w_landed = [sem(f"w_landed{i}") for i in range(RAW)]
        w_hi_done, w_split, acc_ready, evac_done = sem("w_hi_done"), sem("w_split"), sem("acc_ready"), sem("evac_done")
        const_in, x_landed, gain_T, gains_done, consts_set = (
            sem("const_in"), sem("x_landed"), sem("gain_T"), sem("gains_done"), sem("consts_set"))
        x_T, pool_x = sem("x_T"), sem("pool_x")
        x_ready, xg_hi, xg_ready = sem("x_ready"), sem("xg_hi"), sem("xg_ready")
        sq_done, norm_sum = sem("sq_done"), sem("norm_sum")
        std_ready, rstd_ready, diag_ready, rbc_ready, r_ready = (
            sem("std_ready"), sem("rstd_ready"), sem("diag_ready"), sem("rbc_ready"), sem("r_ready"))
        h_hi_done, h32_done, h_ready = sem("h_hi_done"), sem("h32_done"), sem("h_ready")
        y_ready, y_T_done, y_copied, stored = sem("y_ready"), sem("y_T_done"), sem("y_copied"), sem("stored")
        caches_copied = sem("caches_copied")

        def weights_of(t):
            if t.name == "mlp":
                if t.pos % 16 < 8:
                    col = (t.pos // 16 * 8 + t.pos % 16) * P
                    w = aps["mlp_w1"][t.l].rearrange("(k p) n -> p k n", p=P)
                    return w[:, :, bass.ds(t.q * D + col, P)]
                w = aps["mlp_w2"][t.l].rearrange("(f k p) n -> p f k n", p=P, k=KD)
                qq = t.q + t.pos // 16
                return w[:, bass.ds(qq, 1), :, (t.pos % 16 - 8) * P:(t.pos % 16 - 7) * P].rearrange("p f k n -> p (f k) n")
            w = aps[t.name[0] + "_w_" + t.name[2:]][t.l // 3]
            return w.rearrange("(k p) n -> p k n", p=P)[:, :, t.pos * P:(t.pos + 1) * P]

        def sp_weights(sp, t):
            if t.name is None:
                return
            if t.raw_free is not None:
                sp.wait_ge(w_split, t.raw_free)
            sp.dma_start(w_raw[:, t.raw, 0:t.kt, :], weights_of(t)).then_inc(w_landed[t.raw], 16)

        def act_split(act, t):
            if t.name is None:
                return
            act.wait_ge(w_landed[t.raw], t.landed)
            if t.first >= SLOTS - 1:
                act.wait_ge(acc_ready, t.n - 2)
            nc.scalar.activation(w_hi[:, t.slot, 0:t.kt, :], w_raw[:, t.raw, 0:t.kt, :], ACT.Copy).then_inc(w_hi_done, 1)

        def dve_split(dve, t):
            if t.name is None:
                return
            dve.wait_ge(w_hi_done, t.n + 1)
            nc.vector.tensor_tensor(w_lo[:, t.slot, 0:t.kt, :], w_raw[:, t.raw, 0:t.kt, :],
                                    w_hi[:, t.slot, 0:t.kt, :].bitcast(F32), ALU.subtract).then_inc(w_split, 1)

        def pe_tile(pe, t, hi, lo, k_ready=None, between=None):
            pe.wait_ge(w_split, t.n + 1)
            if t.first >= 2:
                pe.wait_ge(evac_done, t.n - 1)
            for k in range(t.kt):
                if k_ready is not None:
                    pe.wait_ge(k_ready[0], k_ready[1] + k + 1)
                if k == 3 and between is not None:
                    between()
                for i, (w, a) in enumerate(((w_hi, hi), (w_hi, lo), (w_lo, hi))):
                    for s in range(2):
                        last = nc.tensor.matmul(acc[:, t.first % 2, s, 0:HALF], w[:, t.slot, k, :],
                                                a[:, k, s * HALF:(s + 1) * HALF],
                                                start=(k == 0 and i == 0), stop=(k == t.kt - 1 and i == 2))
            last.then_inc(acc_ready, 1)

        def acc_of(t):
            return acc[:, t.first % 2, :, 0:HALF]

        def halves(ap):
            return ap.rearrange("p (s n) -> p s n", s=2)

        def gain_row(m):
            return m if m == 2 * DEPTH else m // 2 + DEPTH * (m % 2)

        def x_from(m):
            if m == norms[0]:
                return x_ready, 0
            l = layers[(norm_no[m] - 1) // 2]
            if m % 2 == 0:
                return evac_done, base["mlp", l] + 56
            if l % 3 == 2:
                return pool_x, 0
            return evac_done, base["ab"[l % 3] + "_out", l]

        def act_gain(act, m, k):
            act.wait_ge(x_from(m)[0], x_from(m)[1] + k + 1)
            nc.scalar.activation(act_hi[:, k, :], x[:, k, :], ACT.Copy, scale=gains[:, gain_row(m), k:k + 1]).then_inc(xg_hi, 1)

        def dve_gain(dve, m, k):
            dve.wait_ge(xg_hi, 8 * split_no[m] + k + 1)
            nc.vector.scalar_tensor_tensor(act_lo[:, k, :], x[:, k, :], gains[:, gain_row(m), k:k + 1],
                                           act_hi[:, k, :].bitcast(F32), ALU.mult, ALU.subtract).then_inc(xg_ready, 1)

        def pool_sumsq(pool, m, k):
            i = norm_no[m]
            pool.wait_ge(x_from(m)[0], x_from(m)[1] + k + 1)
            if k == 0:
                if i > 0:
                    pool.wait_ge(norm_sum, i)
                nc.gpsimd.tensor_tensor(sumsq[:, :], x[:, 0, :], x[:, 0, :], ALU.mult).then_inc(sq_done, 1)
                return
            n = 15 * i + 2 * k - 1
            pool.wait_ge(sq_done, n)
            nc.gpsimd.tensor_tensor(sq[:, :], x[:, k, :], x[:, k, :], ALU.mult).then_inc(sq_done, 1)
            pool.wait_ge(sq_done, n + 1)
            last = nc.gpsimd.tensor_tensor(sumsq[:, :], sumsq[:, :], sq[:, :], ALU.add)
            last.then_inc(sq_done, 1)

        def pe_norm_sum(pe, m):
            i = norm_no[m]
            pe.wait_ge(sq_done, 15 * (i + 1))
            if i > 0:
                pe.wait_ge(r_ready, i)
            for j in range(QT + 1):
                rows = P if j < QT else NS
                last = nc.tensor.matmul(misc[0][0:rows, j:j + 1], sumsq[:, j * P:j * P + rows], ones[:, 0:1],
                                        start=True, stop=True)
            last.then_inc(norm_sum, 1)

        def act_norm_std(act, m):
            i = norm_no[m]
            act.wait_ge(norm_sum, i + 1)
            if i > 0:
                act.wait_ge(rstd_ready, i)
            nc.scalar.activation(std[:, 0:QT], misc[0][:, 0:QT], ACT.Sqrt, scale=1.0 / D, bias=eps_col[:, 0:1])
            nc.scalar.activation(std[0:NS, QT:QT + 1], misc[0][0:NS, QT:QT + 1], ACT.Sqrt, scale=1.0 / D,
                                 bias=eps_col[0:NS, 0:1]).then_inc(std_ready, 1)

        def dve_norm_diag(dve, m):
            i = norm_no[m]
            dve.wait_ge(std_ready, i + 1)
            nc.vector.reciprocal(rstd[:, :], std[:, :]).then_inc(rstd_ready, 1)
            dve.wait_ge(rstd_ready, i + 1)
            if i > 0:
                dve.wait_ge(rbc_ready, i)
            nc.vector.tensor_tensor(diag[:, :, :], ident[:, :].unsqueeze(1).to_broadcast([P, QT + 1, P]),
                                    rstd[:, :].unsqueeze(2).to_broadcast([P, QT + 1, P]), ALU.mult).then_inc(diag_ready, 1)

        def pe_norm_bcast(pe, m):
            pe.wait_ge(diag_ready, norm_no[m] + 1)
            for j in range(QT):
                nc.tensor.matmul(misc[1][:, j * P:(j + 1) * P], ones[:, :], diag[:, j, :], start=True, stop=True)
            nc.tensor.matmul(misc[0][:, 64:64 + NS], ones[0:NS, :], diag[0:NS, QT, 0:NS], start=True, stop=True).then_inc(rbc_ready, 1)

        def act_norm_R(act, m):
            act.wait_ge(rbc_ready, norm_no[m] + 1)
            nc.scalar.activation(R[:, 0:SEQ], misc[1][:, :], ACT.Copy)
            nc.scalar.activation(R[:, SEQ:TOK], misc[0][:, 64:64 + NS], ACT.Copy).then_inc(r_ready, 1)

        def mlp_positions(eng, step):
            step(0, 0)
            step(1, 0)
            with eng.Fori(0, FQ - 1) as q:
                for p in range(2, 18):
                    step(p, q)
            for p in range(2, 16):
                step(p, FQ - 1)

        def mlp_no(l):
            return l

        def cache_copy(sp, l, p, q):
            c = (p - 2) // 2 if p % 2 == 0 else COPIES - 1 if p == 17 else None
            if c is None:
                return
            a, b = mlp_no(l) // 2, DEC_B // 2 * (mlp_no(l) % 2) + q
            g, first, rows = COPY_PIECES[c]
            old = aps[f"cache_a_kv{g}"][a].rearrange("b l s h d -> b l (s h d)")
            new = aps[f"new_a_kv{g}_s"][a].rearrange("b l s h d -> b l (s h d)")
            sp.dma_start(new[bass.ds(b, 1), first:first + rows, :],
                         old[bass.ds(b, 1), first + DEC_T:first + DEC_T + rows, :]).then_inc(caches_copied, 16)

        def sp_mlp(sp, l):
            def step(p, q):
                sp_weights(sp, WeightTile("mlp", l, p, q))
                cache_copy(sp, l, p, q)
            with sp.Fori(0, FQ - 1) as q:
                for p in range(2, 18):
                    step(p, q)
            for p in range(2, 18):
                step(p, FQ - 1)

        def h_count(l, p, q):
            return 32 * mlp_no(l) + 8 * q + (p // 16) * 8 + p % 16

        def pe_mlp(pe, l):
            m = 2 * l + 1

            def step(p, q):
                t = WeightTile("mlp", l, p, q)
                if p % 16 < 8:
                    first = p == 0 and isinstance(q, int)
                    between = (lambda: pe_norm_bcast(pe, m)) if p == 1 and isinstance(q, int) else None
                    pe_tile(pe, t, act_hi, act_lo, k_ready=(xg_ready, 8 * split_no[m]) if first else None, between=between)
                    if first:
                        pe_norm_sum(pe, m)
                else:
                    pe_tile(pe, t, h_hi, h_lo, k_ready=(h_ready, 32 * mlp_no(l) + 8 * q) if p == 8 else None)
            mlp_positions(pe, step)

        def act_mlp(act, l, m_next):
            m = 2 * l + 1

            def step(p, q):
                act_split(act, WeightTile("mlp", l, p + 2, q))
                t = WeightTile("mlp", l, p, q)
                if p == 0 and isinstance(q, int):
                    act_norm_std(act, m)
                    act_norm_R(act, m)
                if p % 16 < 8:
                    act.wait_ge(evac_done, t.n + 1)
                    nc.scalar.activation(h_hi[:, p % 16, :], relu_t[:, p % 2, :], ACT.Square).then_inc(h_hi_done, 1)
                elif isinstance(q, int) and m_next in split_norms:
                    act_gain(act, m_next, p % 16 - 8)
            mlp_positions(act, step)

        def dve_mlp(dve, l, m_next):
            m = 2 * l + 1

            def step(p, q):
                dve_split(dve, WeightTile("mlp", l, p + 2, q))
                t = WeightTile("mlp", l, p, q)
                if p == 0 and isinstance(q, int):
                    dve_norm_diag(dve, m)
                    dve.wait_ge(r_ready, norm_no[m] + 1)
                dve.wait_ge(acc_ready, t.n + 1)
                if p % 16 < 8:
                    if mlp_no(l) or p >= 2:
                        dve.wait_ge(h_ready, h_count(l, p, q) - 1)
                    nc.vector.scalar_tensor_tensor(halves(relu_t[:, p % 2, :]), acc_of(t), 0.0, halves(R[:, :]),
                                                   ALU.max, ALU.mult).then_inc(evac_done, 1)
                    return
                k = p % 16 - 8
                nc.vector.tensor_tensor(halves(x[:, k, :]), acc_of(t), halves(x[:, k, :]), ALU.add).then_inc(evac_done, 1)
                if isinstance(q, int) and m_next in split_norms:
                    dve_gain(dve, m_next, k)
            mlp_positions(dve, step)

        def pool_mlp(pool, l, m_next):
            def step(p, q):
                t = WeightTile("mlp", l, p, q)
                if p % 16 < 8:
                    n = h_count(l, p, q)
                    pool.wait_ge(evac_done, t.n + 1)
                    if mlp_no(l) or p >= 2:
                        pool.wait_ge(h_ready, n - 1)
                    nc.gpsimd.tensor_tensor(h32[:, p % 2, :], relu_t[:, p % 2, :], relu_t[:, p % 2, :], ALU.mult).then_inc(h32_done, 1)
                    pool.wait_ge(h32_done, n + 1)
                    pool.wait_ge(h_hi_done, n + 1)
                    nc.gpsimd.tensor_tensor(h_lo[:, p % 16, :], h32[:, p % 2, :], h_hi[:, p % 16, :].bitcast(F32),
                                            ALU.subtract).then_inc(h_ready, 1)
                elif isinstance(q, int):
                    pool_sumsq(pool, m_next, p % 16 - 8)
            mlp_positions(pool, step)

        mixers = {}
        dve_steps, act_steps, pool_steps = sem("dve_steps"), sem("act_steps"), sem("pool_steps")
        c_stored = sem("c_stored")
        steps = {"dve": 0, "act": 0, "pool": 0}

        def chain(eng, ins, name="dve"):
            s = {"dve": dve_steps, "act": act_steps, "pool": pool_steps}[name]
            ins.then_inc(s, 1)
            steps[name] += 1
            eng.wait_ge(s, steps[name])

        def lsb(name, shape, dt=F32):
            return local.enter_context(nc.sbuf_tensor(name, shape, dt))

        def place_free(eng, l):
            if l == layers[0]:
                eng.wait_ge(x_T, KD)
                eng.wait_ge(x_ready, KD)
            else:
                eng.wait_ge(evac_done, base["mlp", l - 1] + 64)

        WINDOWS = (2, 4, 8, 16)
        PRE = 15
        CP = PRE + SEQ
        CS = PRE + DEC_T
        CW = CP + DEC_B * CS
        PREV_ROWS = DEC_B * PRE
        TAIL = PRE + NS
        with ExitStack() as local:
            c_x = lsb("c_x", [P, KD, CW])
            c_sum = lsb("c_sum", [P, 2, CW])
            c_d = lsb("c_d", [P, 2, TOK])
            c_w_raw = lsb("c_w_raw", [P, KD, 256])
            c_w_hi = lsb("c_w_hi", [P, KD, 256], F32R)
            c_w_lo = lsb("c_w_lo", [P, KD, 256], F32R)
            c_prev = lsb("c_prev", [PREV_ROWS, D])
            c_inv = lsb("c_inv", [P, len(WINDOWS), 16])
            c_tail = lsb("c_tail", [TAIL, D])
        c_landed, c_zero, c_prev_T, c_prev_done = sem("c_landed"), sem("c_zero"), sem("c_prev_T"), sem("c_prev_done")
        c_h, c_wh, c_d_done, c_d_hi, c_d_ready, c_w_ready = (sem("c_h"), sem("c_wh"), sem("c_d_done"), sem("c_d_hi"),
                                                             sem("c_d_ready"), sem("c_w_ready"))
        c_y, c_tail_T, c_tail_done = sem("c_y"), sem("c_tail_T"), sem("c_tail_done")

        class MixC:

            @staticmethod
            def sp(sp, l):
                place_free(sp, l)
                sp.dma_start(c_prev[:, :], aps["state_c_pool"][0].rearrange("b j d -> (b j) d")).then_inc(c_landed, 16)
                sp.dma_start(c_inv[:, :, :], aps["c_pool_inv"]).then_inc(c_landed, 16)
                sp.dma_start(c_w_raw[:, :, :], aps["c_w"][0].rearrange("g (k p) e -> p (g k) e", p=P)).then_inc(c_landed, 16)
                sp.dma_start(aps["new_c_pool_s"][0, :, 0:PRE - DEC_T, :], aps["state_c_pool"][0, :, DEC_T:PRE, :]).then_inc(c_stored, 16)
                sp.wait_ge(c_tail_done, 2)
                sp.dma_start(aps["new_c_pool_p"][0, 0], c_tail[0:PRE, :]).then_inc(c_stored, 16)
                for b in range(DEC_B):
                    sp.dma_start(aps["new_c_pool_s"][0, b, PRE - DEC_T:PRE, :],
                                 c_tail[PRE + b * DEC_T:PRE + (b + 1) * DEC_T, :]).then_inc(c_stored, 16)
                sp.wait_ge(c_stored, 16 * (2 + DEC_B))

            @staticmethod
            def pool(pool, l):
                place_free(pool, l)
                nc.gpsimd.memset(c_x[:, :, 0:PRE], 0.0).then_inc(c_zero, 1)
                nc.gpsimd.memset(c_sum[:, :, 0:PRE + 1], 0.0).then_inc(c_zero, 1)
                for k in range(KD):
                    pool_sumsq(pool, 2 * l + 1, k)

            @staticmethod
            def pe(pe, l):
                pe_norm_sum(pe, 2 * l)
                pe.wait_ge(c_landed, 48)
                for k in range(KD):
                    place_free(pe, l)
                    nc.tensor.transpose(acc[:, k // 4, 0, (k % 4) * P:(k % 4) * P + PREV_ROWS], c_prev[:, k * P:(k + 1) * P],
                                        ident[0:PREV_ROWS, 0:PREV_ROWS]).then_inc(c_prev_T, 1)
                pe_norm_bcast(pe, 2 * l)
                for k in range(KD):
                    pe.wait_ge(c_h, k + 1)
                    nc.tensor.transpose(misc[2 + k // 4][0:TAIL, (k % 4) * P:(k % 4 + 1) * P],
                                        c_d[:, k % 2, 0:TAIL], ident[:, :]).then_inc(c_tail_T, 1)
                for o in range(KD):
                    g = o // 2
                    pe.wait_ge(c_w_ready, KD)
                    if o == 0:
                        pe.wait_ge(c_prev_done, KD)
                    if o >= 2:
                        pe.wait_ge(pool_x, o - 1)
                    for k in (2 * g, 2 * g + 1):
                        pe.wait_ge(c_d_ready, k + 1)
                        for i, (w, a) in enumerate(((c_w_hi, act_hi), (c_w_hi, act_lo), (c_w_lo, act_hi))):
                            for s in range(2):
                                last = nc.tensor.matmul(acc[:, (base["mlp", l] + o) % 2, s, 0:HALF], w[:, k, (o % 2) * P:(o % 2 + 1) * P],
                                                        a[:, k, s * HALF:(s + 1) * HALF],
                                                        start=(k == 2 * g and i == 0), stop=(k == 2 * g + 1 and i == 2))
                    last.then_inc(c_y, 1)
                pe.wait_ge(pool_x, KD - 1)

            @staticmethod
            def act(act, l):
                act_norm_std(act, 2 * l)
                act.wait_ge(c_landed, 48)
                for k in range(KD):
                    act.wait_ge(c_prev_T, 4 * (k // 4) + 4)
                    nc.scalar.activation(c_x[:, k, CP:].rearrange("p (b j) -> p b j", j=CS)[:, :, 0:PRE],
                                         acc[:, k // 4, 0, (k % 4) * P:(k % 4) * P + PREV_ROWS].rearrange("p (b j) -> p b j", j=PRE),
                                         ACT.Copy).then_inc(c_prev_done, 1)
                act_norm_R(act, 2 * l)
                for k in range(KD):
                    nc.scalar.activation(c_w_hi[:, k, :], c_w_raw[:, k, :], ACT.Copy).then_inc(c_wh, 1)
                for k in range(KD):
                    act.wait_ge(c_d_done, k + 1)
                    nc.scalar.activation(act_hi[:, k, :], c_d[:, k % 2, :], ACT.Copy).then_inc(c_d_hi, 1)
                for half in range(2):
                    act.wait_ge(c_tail_T, 4 * half + 4)
                    nc.scalar.activation(c_tail[:, half * 512:(half + 1) * 512], misc[2 + half][0:TAIL, :], ACT.Copy).then_inc(c_tail_done, 1)
                for k in range(KD):
                    act.wait_ge(c_y, 2 * (k // 2) + 2)
                    act_gain(act, 2 * l + 1, k)

            @staticmethod
            def dve(dve, l):
                dve_norm_diag(dve, 2 * l)
                dve.wait_ge(r_ready, norm_no[2 * l] + 1)
                dve.wait_ge(c_zero, 2)
                dve.wait_ge(c_prev_done, KD)
                row = gain_row(2 * l)
                for k in range(KD):
                    g, b = k // 2, k % 2
                    cur = c_x[:, k, :]
                    if k >= 2:
                        dve.wait_ge(c_d_ready, k - 1)
                    nc.vector.scalar_tensor_tensor(cur[:, PRE:CP], x[:, k, 0:SEQ], gains[:, row, k:k + 1], R[:, 0:SEQ],
                                                   ALU.mult, ALU.mult)
                    chain(dve, nc.vector.scalar_tensor_tensor(
                        cur[:, CP:].rearrange("p (b j) -> p b j", j=CS)[:, :, PRE:], x[:, k, SEQ:TOK].rearrange("p (b t) -> p b t", t=DEC_T),
                        gains[:, row, k:k + 1], R[:, SEQ:TOK].rearrange("p (b t) -> p b t", t=DEC_T), ALU.mult, ALU.mult))
                    nc.vector.tensor_copy(c_d[:, b, 0:PRE], cur[:, CP - PRE:CP])
                    nc.vector.tensor_copy(c_d[:, b, PRE:TAIL].rearrange("p (b t) -> p b t", t=DEC_T),
                                          cur[:, CP:].rearrange("p (b j) -> p b j", j=CS)[:, :, PRE:]).then_inc(c_h, 1)
                    src = cur
                    for i in range(g + 1):
                        step = 1 << i
                        dst = c_sum[:, i % 2, :]
                        chain(dve, nc.vector.tensor_tensor(dst[:, 2 * step - 1:CW], src[:, 2 * step - 1:CW],
                                                           src[:, step - 1:CW - step], ALU.add))
                        src = dst
                    dve.wait_ge(c_tail_T, k + 1)
                    w = WINDOWS[g]
                    nc.vector.scalar_tensor_tensor(c_d[:, b, 16:SEQ], src[:, PRE + 16:CP], 1.0 / w, cur[:, PRE + 16:CP],
                                                   ALU.mult, ALU.subtract)
                    nc.vector.scalar_tensor_tensor(c_d[:, b, SEQ:TOK].rearrange("p (b t) -> p b t", t=DEC_T),
                                                   src[:, CP:].rearrange("p (b j) -> p b j", j=CS)[:, :, PRE:], 1.0 / w,
                                                   cur[:, CP:].rearrange("p (b j) -> p b j", j=CS)[:, :, PRE:], ALU.mult, ALU.subtract)
                    chain(dve, nc.vector.tensor_tensor(c_d[:, b, 0:16], src[:, PRE:PRE + 16], c_inv[:, g, :], ALU.mult))
                    nc.vector.tensor_tensor(c_d[:, b, 0:16], c_d[:, b, 0:16], cur[:, PRE:PRE + 16], ALU.subtract).then_inc(c_d_done, 1)
                    if k == 0:
                        for j in range(KD):
                            dve.wait_ge(c_wh, j + 1)
                            nc.vector.tensor_tensor(c_w_lo[:, j, :], c_w_raw[:, j, :], c_w_hi[:, j, :].bitcast(F32), ALU.subtract).then_inc(c_w_ready, 1)
                    dve.wait_ge(c_d_hi, k + 1)
                    nc.vector.tensor_tensor(act_lo[:, k, :], c_d[:, b, :], act_hi[:, k, :].bitcast(F32), ALU.subtract).then_inc(c_d_ready, 1)
                for o in range(KD):
                    dve.wait_ge(c_y, o + 1)
                    nc.vector.scalar_tensor_tensor(halves(x[:, o, :]), acc[:, (base["mlp", l] + o) % 2, :, 0:HALF],
                                                   gains[:, 2 * DEPTH + 1, o:o + 1], halves(x[:, o, :]), ALU.mult, ALU.add).then_inc(pool_x, 1)
                    dve_gain(dve, 2 * l + 1, o)

        mixers[2] = MixC

        NG, HG, HD = 3, 6, 64
        PAIRS = HG // 2
        GW = HG * HD
        FT = NG * PAIRS
        A_TILES = 3 * PAIRS
        CACHE = (128, 512, 512)
        SCALE = HD ** -0.5
        BATCH = DEC_B // 2
        S_OFF, S_LEN = (0, 160, 704), (128, 512, 128)
        S_ALL = 864
        with ExitStack() as local:
            a_o = lsb("a_o", [P, NG, QT, GW])
            a_qbd = lsb("a_qbd", [P, FT, DEC_B, 32])
            a_kn = lsb("a_kn", [P, FT, NS])
            a_vn = lsb("a_vn", [NS, NG, GW])
            a_st = lsb("a_st", [P, NG, QT, 2 * HG])
            a_stx0 = lsb("a_stx0", [P, QT, 2 * HG])
            a_stx1 = lsb("a_stx1", [P, QT, 4 * HG])
            a_e = lsb("a_e", [P, 3, NG, QT * HG])
            a_t = lsb("a_t", [P, 3, QT * HG])
            a_f = lsb("a_f", [P, 3, NG, QT * HG])
            a_sst = lsb("a_sst", [P, 2, NG, 2])
            outer = local
            with ExitStack() as local:
                a_qk = lsb("a_qk", [P, 2 * PAIRS, TOK])
                a_v = lsb("a_v", [P, PAIRS, TOK])
                a_vtok = lsb("a_vtok", [P, QT, GW])
                a_ktok = lsb("a_ktok", [P, 2, GW])
                a_cos = lsb("a_cos", [P, TOK])
                a_sin = lsb("a_sin", [P, TOK])
                a_sw = lsb("a_sw", [P, TOK])
                a_rc = lsb("a_rc", [P, TOK])
                a_p = lsb("a_p", [P, 2, QT, 2 * P])
                a_pt = lsb("a_pt", [P, 2, QT, P])
                a_mask = lsb("a_mask", [P, 3, P])
            with ExitStack() as local:
                s_kv = lsb("s_kv", [P, 2, 4, GW])
                s_kT = lsb("s_kT", [P, 2, PAIRS, 512])
                s_p = lsb("s_p", [P, 2, S_ALL])
                s_pt = lsb("s_pt", [P, 2, 9, P])
                s_mask = lsb("s_mask", [P, 2, S_ALL])
        a_landed, a_zero, a_swapped, a_rope, a_vready = sem("a_landed"), sem("a_zero"), sem("a_swapped"), sem("a_rope"), sem("a_vready")
        a_kT, a_vT, a_kcopy, a_vcopy = sem("a_kT"), sem("a_vT"), sem("a_kcopy"), sem("a_vcopy")
        a_kout, a_vout, a_nout = [sem("a_kout0"), sem("a_kout1")], sem("a_vout"), sem("a_nout")
        a_scores, a_masked, a_nb, a_probs, a_ptT, a_ptc, a_pv, a_ocopy = (
            sem("a_scores"), sem("a_masked"), sem("a_nb"), sem("a_probs"), sem("a_ptT"), sem("a_ptc"), sem("a_pv"), sem("a_ocopy"))
        a_qcopy, a_bounce, a_back = sem("a_qcopy"), sem("a_bounce"), sem("a_back")
        a_dif, a_exp, a_scaled, a_oT, a_ohi, a_olo = sem("a_dif"), sem("a_exp"), sem("a_scaled"), sem("a_oT"), sem("a_ohi"), sem("a_olo")
        s_landed, s_mlanded = [sem("s_landed0"), sem("s_landed1")], sem("s_mlanded")
        s_kTp, s_kTc, s_unit, s_scores, s_masked, s_nb, s_probs, s_pscaled = (
            sem("s_kTp"), sem("s_kTc"), sem("s_unit"), sem("s_scores"), sem("s_masked"), sem("s_nb"), sem("s_probs"), sem("s_pscaled"))
        s_ptT, s_ptc, s_pv, s_hi, s_lo = sem("s_ptT"), sem("s_ptc"), sem("s_pv"), sem("s_hi"), sem("s_lo")

        a_layers = [l for l in layers if l % 3 == 0]
        K_ITEMS = [(g, b) for g in range(NG) for b in range(QT + 1) if g > 0 or b >= QT - 1]
        def units_of(g, batch):
            bs = list(range(BATCH * batch, BATCH * (batch + 1)))
            return [(g, batch, [b]) for b in bs] if g == 1 else [(g, batch, bs)]
        K_UNITS = [u for g in range(NG) for batch in range(2) for u in units_of(g, batch)]
        V_UNITS = [u for batch in range(2) for g in range(NG) for u in units_of(g, batch)]
        UNITS = [(0, u) for u in K_UNITS] + [(1, u) for u in V_UNITS]
        unit_landed = [[], []]
        for n, (_, u) in enumerate(UNITS * len(a_layers)):
            unit_landed[n % 2].append((unit_landed[n % 2][-1] if unit_landed[n % 2] else 0) + (64 if u[0] == 2 else 16))
        scratch0 = nc.dram_tensor("scratch0", [2, SEQ, 2 * HG], F32, kind="Internal").ap()
        scratch1 = nc.dram_tensor("scratch1", [2, SEQ, 4 * HG], F32, kind="Internal").ap()

        def cols(g, b):
            if b == QT:
                return slice(SEQ, TOK)
            return slice(b * P, (b + 1) * P) if g == 0 else slice(b, SEQ, QT)

        def a_no(l):
            return a_layers.index(l)

        class MixA:

            @staticmethod
            def sp(sp, l):
                a, n = l // 3, a_no(l)
                place_free(sp, l)
                sp.dma_start(a_cos[:, :], aps["c_cos"]).then_inc(a_landed, 16)
                sp.dma_start(a_sin[:, :], aps["c_sin"]).then_inc(a_landed, 16)
                sp.dma_start(a_mask[:, :, :], aps["c_mask"]).then_inc(a_landed, 16)
                for g in range(NG):
                    for p in range(A_TILES * g + 2, A_TILES * (g + 1) + 2):
                        sp_weights(sp, WeightTile("a_in", l, p))
                    new_p, new_s = aps[f"new_a_kv{g + 1}_p"], aps[f"new_a_kv{g + 1}_s"]
                    L = CACHE[g]
                    for b in range(QT + 1):
                        rows = P if b < QT else NS
                        if b == QT:
                            dst = new_s[a, :, L - DEC_T:L].rearrange("b t c h d -> b t c (h d)")
                        elif g == 0:
                            dst = new_p[a, 0].rearrange("i c h d -> i c (h d)")
                        else:
                            dst = new_p[a, 0].rearrange("(i r) c h d -> r i c (h d)", r=QT)[b]
                        if (g, b) in K_ITEMS:
                            i = K_ITEMS.index((g, b))
                            sp.wait_ge(a_kcopy, n * len(K_ITEMS) + i + 1)
                            if b < QT:
                                sp.dma_start(dst[:, 0, :], a_ktok[:, i % 2, :]).then_inc(a_kout[i % 2], 16)
                            else:
                                for s in range(DEC_B):
                                    sp.dma_start(dst[s, :, 0, :], a_ktok[s * DEC_T:(s + 1) * DEC_T, i % 2, :]).then_inc(a_kout[i % 2], 16)
                        sp.wait_ge(a_vcopy, 5 * (3 * n + g) + b + 1)
                        if b == QT:
                            for s in range(DEC_B):
                                sp.dma_start(dst[s, :, 1, :], a_vn[s * DEC_T:(s + 1) * DEC_T, g, :]).then_inc(a_nout, 16)
                        elif g > 0 or b == QT - 1:
                            sp.dma_start(dst[:, 1, :], a_vtok[:, b, :]).then_inc(a_vout, 16)
                sp.wait_ge(a_probs, 18 * (n + 1))
                sp.dma_start(scratch0[a].rearrange("(b p) c -> p b c", p=P), a_st[:, 0, :, :]).then_inc(a_bounce, 16)
                for g in (1, 2):
                    sp.dma_start(scratch1[a].rearrange("(i r) c -> i r c", r=QT)[:, :, (g - 1) * 12:g * 12], a_st[:, g, :, :]).then_inc(a_bounce, 16)
                sp.wait_ge(a_bounce, 48 * (n + 1))
                sp.dma_start(a_stx0[:, :, :], scratch0[a].rearrange("(i r) c -> i r c", r=QT)).then_inc(a_back, 16)
                sp.dma_start(a_stx1[:, :, :], scratch1[a].rearrange("(b p) c -> p b c", p=P)).then_inc(a_back, 16)
                for p in range(2, 10):
                    sp_weights(sp, WeightTile("a_out", l, p))
                sp.wait_ge(a_nout, 16 * 3 * DEC_B * (n + 1))

            @staticmethod
            def pool(pool, l):
                a, n = l // 3, a_no(l)
                place_free(pool, l)
                nc.gpsimd.memset(a_qbd[:, :, :, :], 0.0).then_inc(a_zero, 1)
                nc.gpsimd.memset(a_p[:, :, 0, 0:P], -1e30).then_inc(a_zero, 1)
                pool.wait_ge(a_ocopy, 18 * (n + 1))
                pool.wait_ge(a_vout, 16 * 9 * (n + 1))
                for i in range(2):
                    pool.wait_ge(a_kout[i], K_OUT_TOTAL[i] * (n + 1))
                pool.dma_start(s_mask[:, :, :], aps["c_smask"]).then_inc(s_mlanded, 16)
                for i, (kv, (g, batch, bs)) in enumerate(UNITS):
                    u = n * len(UNITS) + i
                    if i >= 2:
                        pool.wait_ge(s_unit, u - 1)
                    cache = aps[f"cache_a_kv{g + 1}"][a]
                    dst = s_kv[:, i % 2, :, :]
                    if g == 0:
                        pool.dma_start(dst, cache[bs[0]:bs[-1] + 1, :, kv].rearrange("b k h d -> k b (h d)")).then_inc(s_landed[i % 2], 16)
                    elif g == 1:
                        pool.dma_start(dst, cache[bs[0], :, kv].rearrange("(p j) h d -> p j (h d)", j=4)).then_inc(s_landed[i % 2], 16)
                    else:
                        src = cache[bs[0]:bs[-1] + 1, :, kv].rearrange("b (k r) h d -> r k b (h d)", r=16)
                        for r in range(DEC_T):
                            pool.dma_start(dst[32 * r:32 * r + 32], src[r]).then_inc(s_landed[i % 2], 16)
                for k in range(KD):
                    pool_sumsq(pool, 2 * l + 1, k)

            @staticmethod
            def pe(pe, l):
                n, m = a_no(l), 2 * l
                for g in range(NG):
                    G = 3 * n + g
                    for j in range(A_TILES):
                        t = WeightTile("a_in", l, A_TILES * g + j)
                        first = t.pos == 0
                        pe_tile(pe, t, act_hi, act_lo, k_ready=(xg_ready, 8 * split_no[m]) if first else None,
                                between=(lambda: pe_norm_bcast(pe, m)) if t.pos == 1 else None)
                        if first:
                            pe_norm_sum(pe, m)
                    pe.wait_ge(evac_done, base["a_in", l] + A_TILES * (g + 1))
                    pe.wait_ge(a_rope, 6 * (G + 1))
                    for b in range(QT + 1):
                        rows = P if b < QT else NS
                        if (g, b) in K_ITEMS:
                            i = K_ITEMS.index((g, b))
                            if i + n * len(K_ITEMS) >= 2:
                                pe.wait_ge(a_kcopy, n * len(K_ITEMS) + i - 1)
                            for p in range(PAIRS):
                                last = nc.tensor.transpose(acc[0:rows, i % 2, 0, p * P:(p + 1) * P], a_qk[:, PAIRS + p, cols(g, b)], ident[:, :])
                            last.then_inc(a_kT, 1)
                        v = 5 * G + b
                        if v >= 2:
                            pe.wait_ge(a_vcopy, v - 1)
                        for p in range(PAIRS):
                            last = nc.tensor.transpose(acc[0:rows, v % 2, 1, p * P:(p + 1) * P], a_v[:, p, cols(g, b)], ident[:, :])
                        last.then_inc(a_vT, 1)
                    pe.wait_ge(a_kcopy, n * len(K_ITEMS) + K_ITEMS.index((g, QT)) + 1)
                    pe.wait_ge(a_vcopy, 5 * (G + 1))

                    def scores(h):
                        H = 6 * G + h
                        r = slice((h % 2) * HD, (h % 2 + 1) * HD)
                        if h >= 2:
                            pe.wait_ge(a_masked, H - 1)
                        for b in range(QT):
                            last = nc.tensor.matmul(acc[:, h % 2, 0, b * P:(b + 1) * P], a_qk[r, h // 2, cols(g, b)],
                                                    a_qk[r, PAIRS + h // 2, cols(g, b)], start=True, stop=True)
                        if g == 0:
                            for b in range(1, QT):
                                last = nc.tensor.matmul(acc[:, h % 2, 1, b * P:(b + 1) * P], a_qk[r, h // 2, cols(g, b)],
                                                        a_qk[r, PAIRS + h // 2, cols(g, b - 1)], start=True, stop=True)
                        last.then_inc(a_scores, 1)

                    def turn(h):
                        H = 6 * G + h
                        pe.wait_ge(a_probs, H + 1)
                        if H >= 1:
                            pe.wait_ge(a_ptc, H)
                        for b in range(QT):
                            last = nc.tensor.transpose(misc[2][:, b * P:(b + 1) * P], a_p[:, h % 2, b, P:2 * P], ident[:, :])
                        if g == 0:
                            for b in range(1, QT):
                                last = nc.tensor.transpose(misc[3][:, b * P:(b + 1) * P], a_p[:, h % 2, b, 0:P], ident[:, :])
                        last.then_inc(a_ptT, 1)

                    def values(h):
                        H = 6 * G + h
                        pe.wait_ge(a_ptc, H + 1)
                        if H >= 2:
                            pe.wait_ge(a_ocopy, H - 1)
                        hc = slice(h * HD, (h + 1) * HD)
                        for b in range(QT):
                            prev = g == 0 and b > 0
                            out = misc[h % 2][:, b * HD:(b + 1) * HD]
                            if prev:
                                nc.tensor.matmul(out, a_pt[:, 1, b, :], a_vtok[:, b - 1, hc], start=True, stop=False)
                            last = nc.tensor.matmul(out, a_pt[:, 0, b, :], a_vtok[:, b, hc], start=not prev, stop=True)
                        last.then_inc(a_pv, 1)

                    for i in range(HG + 2):
                        if i < HG:
                            scores(i)
                        if 1 <= i <= HG:
                            turn(i - 1)
                        if i >= 2:
                            values(i - 2)
                pe.wait_ge(a_qcopy, 7 * 3 * (n + 1))
                pe.wait_ge(a_ocopy, 18 * (n + 1))
                pe.wait_ge(a_zero, 2 * (n + 1))

                def unit_wait(i):
                    u = n * len(UNITS) + i
                    pe.wait_ge(s_landed[i % 2], unit_landed[i % 2][u // 2])

                def turn_keys(i):
                    unit_wait(i)
                    if i + n >= 1:
                        pe.wait_ge(s_kTc, 3 * (12 * n + i))
                    for p in range(PAIRS):
                        for j in range(4):
                            last = nc.tensor.transpose(misc[1 + p][:, j * P:(j + 1) * P], s_kv[:, i % 2, j, p * P:(p + 1) * P], ident[:, :])
                        last.then_inc(s_kTp, 1)

                def sample_scores(i):
                    g, batch, bs = K_UNITS[i]
                    pe.wait_ge(s_kTc, 3 * (12 * n + i + 1))
                    k = 2 * g + batch
                    if bs[0] == BATCH * batch and g > 0:
                        pe.wait_ge(s_masked, 6 * n + k - 1)
                    for b in bs:
                        rows = slice(32 * (b % BATCH), 32 * (b % BATCH) + 32)
                        keys = slice(0, 512) if g == 1 else slice((b % BATCH) * P, (b % BATCH + 1) * P)
                        for p in range(PAIRS):
                            nc.tensor.matmul(acc[rows, batch, 0, 0:S_LEN[g]], a_qbd[:, 3 * g + p, b, :], s_kT[:, i % 2, p, keys],
                                             start=(p == 0), stop=(p == PAIRS - 1))
                        for p in range(PAIRS):
                            last = nc.tensor.matmul(acc[rows, batch, 1, 0:NS], a_qbd[:, 3 * g + p, b, :], a_kn[:, 3 * g + p, :],
                                                    start=(p == 0), stop=(p == PAIRS - 1))
                    last.then_inc(s_unit, 1)

                turn_keys(0)
                for i in range(12):
                    if i < 11:
                        turn_keys(i + 1)
                    sample_scores(i)
                for batch in range(2):
                    pe.wait_ge(s_pscaled, 2 * n + batch + 1)
                    if batch + n:
                        pe.wait_ge(s_ptc, 2 * n + batch)
                    if batch == 0:
                        pe.wait_ge(s_kTc, 36 * (n + 1))
                    starts = [0] + [S_OFF[1] + j * P for j in range(4)] + [S_OFF[2]]
                    for j, c in enumerate(starts):
                        nc.tensor.transpose(misc[1 + j // 4][:, (j % 4) * P:(j % 4 + 1) * P], s_p[:, batch, c:c + P], ident[:, :])
                    for g in range(NG):
                        j = 6 + g
                        c = S_OFF[g] + S_LEN[g]
                        last = nc.tensor.transpose(misc[1 + j // 4][0:NS, (j % 4) * P:(j % 4 + 1) * P], s_p[:, batch, c:c + NS], ident[:, :])
                    last.then_inc(s_ptT, 1)
                for i, (g, batch, bs) in enumerate(V_UNITS):
                    unit_wait(12 + i)
                    pe.wait_ge(s_ptc, 2 * n + batch + 1)
                    for b in bs:
                        bb = b % BATCH
                        for p in range(PAIRS):
                            f = 3 * g + p
                            pc = slice(bb * 32 + 8 * p, bb * 32 + 8 * p + 8)
                            out = acc[:, batch, 0, (f * BATCH + bb) * 8:(f * BATCH + bb + 1) * 8]
                            tiles = [(j, 1 + j) for j in range(4)] if g == 1 else [(bb, 0 if g == 0 else 5)]
                            for q, (src, pt) in enumerate(tiles):
                                nc.tensor.matmul(out, s_kv[:, i % 2, src, p * P:(p + 1) * P], s_pt[:, batch, pt, pc], start=(q == 0), stop=False)
                            last = nc.tensor.matmul(out, a_vn[0:NS, g, p * P:(p + 1) * P], s_pt[0:NS, batch, 6 + g, pc], start=False, stop=True)
                    last.then_inc(s_unit, 1)
                for f in range(FT):
                    pe.wait_ge(a_scaled, 3 * n + f // 3 + 1)
                    if f + n >= 1:
                        pe.wait_ge(a_olo, 9 * n + f)
                    for b in range(QT):
                        last = nc.tensor.transpose(misc[0][:, b * P:(b + 1) * P], a_o[:, f // 3, b, (f % 3) * P:(f % 3 + 1) * P], ident[:, :])
                    last.then_inc(a_oT, 1)
                pe.wait_ge(a_olo, 9 * (n + 1))
                pe.wait_ge(s_lo, 4 * (n + 1))
                for o in range(KD):
                    pe_tile(pe, WeightTile("a_out", l, o), act_hi, act_lo)

            @staticmethod
            def act(act, l):
                n, m = a_no(l), 2 * l
                for g in range(NG):
                    G = 3 * n + g
                    for j in range(A_TILES):
                        t = WeightTile("a_in", l, A_TILES * g + j)
                        act_split(act, WeightTile("a_in", l, t.pos + 2))
                        if t.pos == 0:
                            act_norm_std(act, m)
                            act_norm_R(act, m)
                        if j < 2 * PAIRS:
                            act.wait_ge(acc_ready, t.n + 1)
                            if t.n >= 1:
                                act.wait_ge(evac_done, t.n)
                            for q in range(4):
                                last = nc.scalar.activation(halves(a_sw[32 * (q ^ 1):32 * (q ^ 1) + 32, :]),
                                                            acc[32 * q:32 * q + 32, t.first % 2, :, 0:HALF], ACT.Copy)
                            last.then_inc(a_swapped, 1)
                    for b in range(QT + 1):
                        if (g, b) not in K_ITEMS:
                            continue
                        i = K_ITEMS.index((g, b))
                        rows = P if b < QT else NS
                        act.wait_ge(a_kT, n * len(K_ITEMS) + i + 1)
                        if i + n * len(K_ITEMS) >= 2:
                            act.wait_ge(a_kout[i % 2], K_OUT[i] + K_OUT_TOTAL[i % 2] * n)
                        nc.scalar.activation(a_ktok[0:rows, i % 2, :], acc[0:rows, i % 2, 0, 0:GW], ACT.Copy).then_inc(a_kcopy, 1)
                    for i in range(HG + 1):
                        H = 6 * G + i
                        if i < HG:
                            act.wait_ge(a_nb, H + 1)
                            for b in range(QT):
                                lo = 0 if g == 0 and b > 0 else P
                                last = nc.scalar.activation(a_p[:, i % 2, b, lo:2 * P], a_p[:, i % 2, b, lo:2 * P], ACT.Exp, scale=SCALE,
                                                            bias=a_st[:, g, b, i:i + 1], accum_out=a_st[:, g, b, HG + i:HG + i + 1])
                            last.then_inc(a_probs, 1)
                        if i >= 1:
                            act.wait_ge(a_ptT, H)
                            if H >= 2:
                                act.wait_ge(a_pv, H - 1)
                            last = nc.scalar.activation(a_pt[:, 0, :, :], misc[2][:, :].rearrange("p (b n) -> p b n", n=P), ACT.Copy)
                            if g == 0:
                                last = nc.scalar.activation(a_pt[:, 1, 1:QT, :], misc[3][:, P:].rearrange("p (b n) -> p b n", n=P), ACT.Copy)
                            last.then_inc(a_ptc, 1)

                def sample_exp(k):
                    g, batch = k // 2, k % 2
                    act.wait_ge(s_nb, 6 * n + k + 1)
                    part = s_p[:, batch, S_OFF[g]:S_OFF[g] + S_LEN[g] + NS]
                    nc.scalar.activation(part, part, ACT.Exp, scale=SCALE, bias=a_sst[:, 0, g, batch:batch + 1],
                                         accum_out=a_sst[:, 1, g, batch:batch + 1]).then_inc(s_probs, 1)

                def last_of(i):
                    return i == 11 or K_UNITS[i + 1][:2] != K_UNITS[i][:2]

                for i in range(13):
                    if i < 12:
                        for p in range(PAIRS):
                            act.wait_ge(s_kTp, 3 * (12 * n + i) + p + 1)
                            if i >= 2:
                                act.wait_ge(s_unit, 24 * n + i - 1)
                            nc.scalar.activation(s_kT[:, i % 2, p, :], misc[1 + p][:, :], ACT.Copy).then_inc(s_kTc, 1)
                    if i >= 1 and last_of(i - 1):
                        sample_exp(2 * K_UNITS[i - 1][0] + K_UNITS[i - 1][1])

                def combine_exp(c, w):
                    act.wait_ge(a_dif, 3 * n + c + 1)
                    nc.scalar.activation(a_e[:, c, :, 0:w], a_e[:, c, :, 0:w], ACT.Exp).then_inc(a_exp, 1)

                combine_exp(0, 2)
                for batch in range(2):
                    act.wait_ge(s_ptT, 2 * n + batch + 1)
                    nc.scalar.activation(s_pt[:, batch, 0:4, :], misc[1][:, :].rearrange("p (j n) -> p j n", n=P), ACT.Copy)
                    nc.scalar.activation(s_pt[:, batch, 4:6, :], misc[2][:, 0:2 * P].rearrange("p (j n) -> p j n", n=P), ACT.Copy)
                    nc.scalar.activation(s_pt[0:NS, batch, 6:8, :], misc[2][0:NS, 2 * P:4 * P].rearrange("p (j n) -> p j n", n=P), ACT.Copy)
                    nc.scalar.activation(s_pt[0:NS, batch, 8, :], misc[3][0:NS, 0:P], ACT.Copy).then_inc(s_ptc, 1)
                combine_exp(1, QT * HG)
                combine_exp(2, QT * HG)
                for batch in range(2):
                    act.wait_ge(s_unit, 24 * n + 12 + 6 * (batch + 1))
                    for s in range(2):
                        r = slice(HD * s, HD * (s + 1))
                        nc.scalar.activation(sample_cols(act_hi, r, batch), sample_out(r, batch, s), ACT.Copy).then_inc(s_hi, 1)
                for f in range(FT):
                    act.wait_ge(a_oT, 9 * n + f + 1)
                    nc.scalar.activation(prompt_cols(act_hi, f), misc[0][:, :].rearrange("p (b i) -> p b i", i=P), ACT.Copy).then_inc(a_ohi, 1)
                for o in range(KD):
                    act_split(act, WeightTile("a_out", l, o + 2))
                act.wait_ge(evac_done, base["a_out", l] + KD)
                for k in range(KD):
                    act_gain(act, 2 * l + 1, k)

            @staticmethod
            def dve(dve, l):
                n, m = a_no(l), 2 * l
                for g in range(NG):
                    G = 3 * n + g
                    for j in range(A_TILES):
                        t = WeightTile("a_in", l, A_TILES * g + j)
                        dve_split(dve, WeightTile("a_in", l, t.pos + 2))
                        if t.pos == 0:
                            dve_norm_diag(dve, m)
                            dve.wait_ge(r_ready, norm_no[m] + 1)
                            dve.wait_ge(a_landed, 48 * (n + 1))
                            chain(dve, nc.vector.tensor_tensor(a_cos[:, :], a_cos[:, :], R[:, :], ALU.mult))
                            chain(dve, nc.vector.tensor_tensor(a_sin[:, :], a_sin[:, :], R[:, :], ALU.mult))
                        dve.wait_ge(acc_ready, t.n + 1)
                        if j < 2 * PAIRS:
                            dve.wait_ge(a_swapped, 6 * G + j + 1)
                            nc.vector.tensor_tensor(halves(a_rc[:, :]), acc_of(t), halves(a_cos[:, :]), ALU.mult)
                            nc.vector.tensor_tensor(a_qk[:, j, :], a_sw[:, :], a_sin[:, :], ALU.mult).then_inc(evac_done, 1)
                            dve.wait_ge(evac_done, t.n + 1)
                            nc.vector.tensor_tensor(a_qk[:, j, :], a_qk[:, j, :], a_rc[:, :], ALU.add).then_inc(a_rope, 1)
                            dve.wait_ge(a_rope, 6 * G + j + 1)
                        else:
                            nc.vector.tensor_tensor(halves(a_v[:, j - 2 * PAIRS, :]), acc_of(t), halves(R[:, :]), ALU.mult).then_inc(evac_done, 1)
                    for b in range(QT + 1):
                        v = 5 * G + b
                        dve.wait_ge(a_vT, v + 1)
                        if b == 0 and 0 < g:
                            dve.wait_ge(a_vout, 16 * (9 * n + (1, 5)[g - 1]))
                        if b < QT:
                            nc.vector.tensor_copy(a_vtok[:, b, :], acc[:, v % 2, 1, 0:GW]).then_inc(a_vcopy, 1)
                        else:
                            nc.vector.tensor_copy(a_vn[0:NS, g, :], acc[0:NS, v % 2, 1, 0:GW]).then_inc(a_vcopy, 1)
                    dve.wait_ge(a_zero, 2 * (n + 1))
                    for p in range(PAIRS):
                        for s in range(2):
                            r = slice(HD * s, HD * (s + 1))
                            c = (2 * p + s) * DEC_T
                            nc.vector.tensor_copy(a_qbd[r, 3 * g + p, :, c:c + DEC_T],
                                                  a_qk[r, p, SEQ:TOK].rearrange("p (b t) -> p b t", t=DEC_T)).then_inc(a_qcopy, 1)
                    nc.vector.tensor_copy(a_kn[:, 3 * g:3 * g + 3, :], a_qk[:, PAIRS:2 * PAIRS, SEQ:TOK]).then_inc(a_qcopy, 1)
                    mask = a_mask[:, (0, 0, 2)[g], :].unsqueeze(1)
                    for i in range(HG + 2):
                        H = 6 * G + i
                        if i < HG:
                            dve.wait_ge(a_scores, H + 1)
                            if H >= 2:
                                dve.wait_ge(a_ptT, H - 1)
                            last = nc.vector.tensor_tensor(a_p[:, i % 2, :, P:2 * P], acc[:, i % 2, 0, :].rearrange("p (b k) -> p b k", k=P),
                                                           mask.to_broadcast([P, QT, P]), ALU.add)
                            if g == 0:
                                last = nc.vector.tensor_tensor(a_p[:, i % 2, 1:QT, 0:P], acc[:, i % 2, 1, P:].rearrange("p (b k) -> p b k", k=P),
                                                               a_mask[:, 1, :].unsqueeze(1).to_broadcast([P, QT - 1, P]), ALU.add)
                            last.then_inc(a_masked, 1)
                            dve.wait_ge(a_masked, H + 1)
                            chain(dve, nc.vector.tensor_reduce(a_t[:, 0, 0:QT], a_p[:, i % 2, :, (0 if g == 0 else P):2 * P], AX, ALU.max))
                            nc.vector.tensor_scalar(a_st[:, g, :, i], a_t[:, 0, 0:QT], -SCALE, None, ALU.mult).then_inc(a_nb, 1)
                            dve.wait_ge(a_nb, H + 1)
                        if i >= 2:
                            dve.wait_ge(a_pv, H - 1)
                            h = i - 2
                            nc.vector.tensor_copy(a_o[:, g, :, h * HD:(h + 1) * HD],
                                                  misc[h % 2][:, 0:QT * HD].rearrange("p (b d) -> p b d", d=HD)).then_inc(a_ocopy, 1)
                for k in range(6):
                    g, batch = k // 2, k % 2
                    units = [i for i, u in enumerate(K_UNITS) if u[:2] == (g, batch)]
                    dve.wait_ge(s_unit, 24 * n + units[-1] + 1)
                    if k == 0:
                        dve.wait_ge(s_mlanded, 16 * (n + 1))
                    o, L = S_OFF[g], S_LEN[g]
                    nc.vector.tensor_tensor(s_p[:, batch, o:o + L], acc[:, batch, 0, 0:L], s_mask[:, batch, o:o + L], ALU.add)
                    nc.vector.tensor_tensor(s_p[:, batch, o + L:o + L + NS], acc[:, batch, 1, 0:NS], s_mask[:, batch, o + L:o + L + NS],
                                            ALU.add).then_inc(s_masked, 1)
                    dve.wait_ge(s_masked, 6 * n + k + 1)
                    chain(dve, nc.vector.tensor_reduce(a_t[:, 0, 0:1], s_p[:, batch, o:o + L + NS], AX, ALU.max))
                    nc.vector.tensor_scalar(a_sst[:, 0, g, batch:batch + 1], a_t[:, 0, 0:1], -SCALE, None, ALU.mult).then_inc(s_nb, 1)
                    dve.wait_ge(s_nb, 6 * n + k + 1)

                def combine(c, w, nb, l_sum, shape):
                    lowest, den = shape(a_t[:, c, 0:w]), shape(a_t[:, (c + 1) % 3, 0:w])
                    e = [shape(a_e[:, c, g, 0:w]) for g in range(NG)]
                    f = [shape(a_f[:, c, g, 0:w]) for g in range(NG)]
                    chain(dve, nc.vector.tensor_tensor(lowest, nb[0], nb[1], ALU.min))
                    chain(dve, nc.vector.tensor_tensor(lowest, lowest, nb[2], ALU.min))
                    for g in range(NG):
                        last = nc.vector.tensor_tensor(e[g], lowest, nb[g], ALU.subtract)
                    last.then_inc(a_dif, 1)
                    dve.wait_ge(a_exp, 3 * n + c + 1)
                    for g in range(NG):
                        last = nc.vector.tensor_tensor(f[g], e[g], l_sum[g], ALU.mult)
                    chain(dve, last)
                    chain(dve, nc.vector.tensor_tensor(den, f[0], f[1], ALU.add))
                    chain(dve, nc.vector.tensor_tensor(den, den, f[2], ALU.add))
                    chain(dve, nc.vector.reciprocal(den, den))
                    for g in range(NG):
                        last = nc.vector.tensor_tensor(f[g], e[g], den, ALU.mult)
                    chain(dve, last)

                dve.wait_ge(s_probs, 6 * (n + 1))
                combine(0, 2, [a_sst[:, 0, g, :] for g in range(NG)], [a_sst[:, 1, g, :] for g in range(NG)], lambda ap: ap)
                for batch in range(2):
                    for g in range(NG):
                        part = s_p[:, batch, S_OFF[g]:S_OFF[g] + S_LEN[g] + NS]
                        last = nc.vector.tensor_scalar(part, part, a_f[:, 0, g, batch:batch + 1], None, ALU.mult)
                    last.then_inc(s_pscaled, 1)
                dve.wait_ge(a_back, 32 * (n + 1))
                grid = lambda ap: ap.rearrange("p (b h) -> p b h", h=HG)
                st = [[a_st[:, g, :, s * HG:(s + 1) * HG] for g in range(NG)] for s in range(2)]
                x0 = [a_stx0[:, :, s * HG:(s + 1) * HG] for s in range(2)]
                x1 = [[a_stx1[:, :, (2 * g + s) * HG:(2 * g + s + 1) * HG] for g in range(2)] for s in range(2)]
                combine(1, QT * HG, [st[0][0]] + x1[0], [st[1][0]] + x1[1], grid)
                combine(2, QT * HG, [x0[0]] + st[0][1:], [x0[1]] + st[1][1:], grid)
                for g in range(NG):
                    o = a_o[:, g, :, :].rearrange("p b (h d) -> p (b h) d", d=HD)
                    nc.vector.tensor_tensor(o, o, a_f[:, 1 if g == 0 else 2, g, :].unsqueeze(2).to_broadcast([P, QT * HG, HD]),
                                            ALU.mult).then_inc(a_scaled, 1)
                for batch in range(2):
                    for s in range(2):
                        dve.wait_ge(s_hi, 4 * n + 2 * batch + s + 1)
                        r = slice(HD * s, HD * (s + 1))
                        nc.vector.tensor_tensor(sample_cols(act_lo, r, batch), sample_out(r, batch, s),
                                                sample_cols(act_hi, r, batch).bitcast(F32), ALU.subtract).then_inc(s_lo, 1)
                for f in range(FT):
                    dve.wait_ge(a_ohi, 9 * n + f + 1)
                    nc.vector.tensor_tensor(prompt_cols(act_lo, f), misc[0][:, :].rearrange("p (b i) -> p b i", i=P),
                                            prompt_cols(act_hi, f).bitcast(F32), ALU.subtract).then_inc(a_olo, 1)
                for o in range(KD):
                    t = WeightTile("a_out", l, o)
                    dve_split(dve, WeightTile("a_out", l, o + 2))
                    dve.wait_ge(acc_ready, t.n + 1)
                    nc.vector.tensor_tensor(halves(x[:, o, :]), acc_of(t), halves(x[:, o, :]), ALU.add).then_inc(evac_done, 1)
                for k in range(KD):
                    dve_gain(dve, 2 * l + 1, k)

        def sample_out(r, batch, s):
            return acc[r, batch, 0, 0:FT * BATCH * 8].rearrange("p (f b s t) -> p s f b t", f=FT, b=BATCH, s=2)[:, s]

        def sample_cols(buf, r, batch):
            c = SEQ + batch * BATCH * DEC_T
            return buf[r, 0:FT, c:c + BATCH * DEC_T].rearrange("p f (b t) -> p f b t", t=DEC_T)

        def prompt_cols(buf, f):
            if f < PAIRS:
                return buf[:, f, 0:SEQ].rearrange("p (b i) -> p b i", i=P)
            return buf[:, f, 0:SEQ].rearrange("p (i b) -> p b i", b=QT)

        K_OUT, K_OUT_TOTAL = [], [0, 0]
        for i, (g, b) in enumerate(K_ITEMS):
            K_OUT.append(K_OUT_TOTAL[i % 2])
            K_OUT_TOTAL[i % 2] += 16 * (DEC_B if b == QT else 1)
        mixers[0] = MixA

        HB_, CHUNK, CONV = 8, 64, 4
        QKV = 3 * HB_
        XS = CONV - 1 + DEC_T
        XP = CONV - 1 + SEQ
        XW = XP + DEC_B * XS
        XF = XW - (CONV - 1)
        LEVELS = 6
        TAILB = (CONV - 1) * (1 + DEC_B)
        with ExitStack() as local:
            b_qkv = lsb("b_qkv", [P, QKV, TOK])
            b_z = lsb("b_z", [P, HB_, TOK])
            b_ab = lsb("b_ab", [P, QT + 1, 2 * HB_])
            b_g = lsb("b_g", [P, QT + 1, HB_])
            b_beta = lsb("b_beta", [P, QT + 1, HB_])
            b_G = lsb("b_G", [P, QT + 1, HB_])
            b_be = lsb("b_be", [P, QT + 1, HB_])
            b_kdf = lsb("b_kdf", [P, QT + 1, HB_])
            b_tmp = lsb("b_tmp", [P, 2, QT + 1, HB_])
            b_dl = lsb("b_dl", [P, 2 * QT + DEC_B, HB_])
            b_gm = lsb("b_gm", [NS, DEC_B, HB_])
            b_par = lsb("b_par", [P, 2 * HB_])
            b_rn = lsb("b_rn", [P, QT + 1, 2 * HB_])
            b_cw = lsb("b_cw", [P, CONV * QKV + 1])
            b_tri = lsb("b_tri", [P, 4, P])
            b_bmask = lsb("b_bmask", [NS, DEC_B])
            eps_l2 = lsb("eps_l2", [P, 1])
            outer_b = local
            with ExitStack() as local:
                b_xp = lsb("b_xp", [P, 2, XW])
                b_xc = lsb("b_xc", [P, 2, XW])
                b_cst = lsb("b_cst", [P, QKV, DEC_B, CONV - 1])
                b_state = lsb("b_state", [DEC_B * (CONV - 1), 4, P])
                b_rows = lsb("b_rows", [CONV * QKV + 1, P])
                b_tail = lsb("b_tail", [P, 2, TAILB])
                b_tailT = lsb("b_tailT", [TAILB, 2, 512])
                b_sq = lsb("b_sq", [P, TOK])
                b_wab = lsb("b_wab", [P, KD, 2 * HB_])
                b_wab_hi = lsb("b_wab_hi", [P, KD, 2 * HB_], F32R)
                b_wab_lo = lsb("b_wab_lo", [P, KD, 2 * HB_], F32R)
            with ExitStack() as local:
                b_S = lsb("b_S", [P, 2, HB_, P])
                b_M = lsb("b_M", [P, 2, 2, 4, P])
                b_lvl = lsb("b_lvl", [P, LEVELS, P])
            with ExitStack() as local:
                b_h32 = lsb("b_h32", [P, 2, TOK])
                b_osq = lsb("b_osq", [P, 2, TOK])
        names = ("e1", "e2", "eg", "kbe", "kd", "vb", "T", "U", "Z")
        b_w = {nm: work[f"b_{nm}"] for nm in names}
        b_dmask = work["b_dmask"]
        b_vmask = b_M[0:NS, :, :, :, :].rearrange("p a c h n -> p (a c h n)")[:, 0:DEC_B * P]
        b_h32v = b_w["e1"][:, 0, 0, 0:NS]
        b_landed, b_clanded, b_zero = sem("b_landed"), sem("b_clanded"), sem("b_zero")
        b_stT, b_stc, b_cwT, b_cwc = sem("b_stT"), sem("b_stc"), sem("b_cwT"), sem("b_cwc")
        b_pre, b_conv, b_tailc, b_silu, b_sqd, b_sum = sem("b_pre"), sem("b_conv"), sem("b_tailc"), sem("b_silu"), sem("b_sqd"), sem("b_sum")
        b_tlT, b_tlc, b_tlout = sem("b_tlT"), sem("b_tlc"), [sem("b_tlout0"), sem("b_tlout1")]
        b_wabh, b_wabr = sem("b_wabh"), sem("b_wabr")
        b_gate_pe, b_gate_act, b_gate_dve = sem("b_gate_pe"), sem("b_gate_act"), sem("b_gate_dve")
        b_bc, b_qk = sem("b_bc"), sem("b_qk")
        b_kvT, b_kv, b_kk, b_e, b_ex, b_a, b_att = (
            sem("b_kvT"), sem("b_kv"), sem("b_kk"), sem("b_e"), sem("b_ex"), sem("b_a"), sem("b_att"))
        b_m, b_zp, b_zc, b_delta, b_tu, b_wT, b_wc = (
            sem("b_m"), sem("b_zp"), sem("b_zc"), sem("b_delta"), sem("b_tu"), sem("b_wT"), sem("b_wc"))
        b_vn, b_vnc, b_ob, b_s, b_oc = sem("b_vn"), sem("b_vnc"), sem("b_ob"), sem("b_s"), sem("b_oc")
        b_sin, b_sout, b_pout = [sem("b_sin0"), sem("b_sin1")], [sem("b_sout0"), sem("b_sout1")], sem("b_pout")
        b_vT, b_vTc, b_vm, b_su, b_sd = sem("b_vT"), sem("b_vTc"), sem("b_vm"), sem("b_su"), sem("b_sd")
        b_osqd, b_os, b_obc, b_on, b_og, b_ohi, b_olo = (
            sem("b_osqd"), sem("b_os"), sem("b_obc"), sem("b_on"), sem("b_og"), sem("b_ohi"), sem("b_olo"))

        def width(i):
            return P if i < QT else NS

        def tcols(i):
            return slice(i * P, i * P + width(i))

        def levels_of(i):
            return LEVELS if i < QT else 2

        def lev(i, k, hb):
            return 12 * i + 2 * k + hb

        def heads(ap):
            return ap.rearrange("p (h n) -> p h n", h=4)

        class MixB:

            @staticmethod
            def sp(sp, l):
                place_free(sp, l)
                sp.dma_start(b_rows[0:CONV * QKV, :], aps["b_conv"][0].rearrange("j (k p) -> (j k) p", p=P)).then_inc(b_landed, 16)
                sp.dma_start(b_rows[CONV * QKV:, :], aps["b_norm"]).then_inc(b_landed, 16)
                sp.dma_start(b_par[:, 0:HB_], aps["b_dt_bias"].partition_broadcast(P)).then_inc(b_landed, 16)
                sp.dma_start(b_par[:, HB_:], aps["b_a_log"].partition_broadcast(P)).then_inc(b_landed, 16)
                sp.dma_start(b_tri[:, :, :], aps["c_tri"]).then_inc(b_landed, 16)
                sp.dma_start(b_bmask[:, :], aps["c_bmask"]).then_inc(b_landed, 16)
                sp.dma_start(b_wab[:, :, :], aps["b_w_in"][0].rearrange("(k p) n -> p k n", p=P)[:, :, 4 * HB_ * P:]).then_inc(b_landed, 16)
                for c in range(6):
                    if c:
                        sp.wait_ge(b_stT, 4 * c)
                    sp.dma_start(b_state[:, :, :], aps["state_b_conv"][0].rearrange("b j (k p) -> (b j) k p", p=P)[:, 4 * c:4 * c + 4, :]).then_inc(b_clanded, 16)
                for j in range(32):
                    sp_weights(sp, WeightTile("b_in", l, j + 2))
                    if j >= 4 and j % 4 == 2 and j < 28:
                        c = j // 4 - 1
                        sp.wait_ge(b_tlc, c + 1)
                        cs = slice(c * 512, (c + 1) * 512)
                        sp.dma_start(aps["new_b_conv_p"][0, 0, :, cs], b_tailT[0:3, c % 2, :]).then_inc(b_tlout[c % 2], 16)
                        sp.dma_start(aps["new_b_conv_s"][0].rearrange("b j c -> (b j) c")[:, cs], b_tailT[3:TAILB, c % 2, :]).then_inc(b_tlout[c % 2], 16)
                sp.wait_ge(b_gate_dve, 7)
                for i in range(2):
                    sp.wait_ge(b_tlout[i], 96)
                sp.wait_ge(b_qk, 16)
                sp.dma_start(b_lvl[:, :, :], aps["c_lvl"]).then_inc(b_clanded, 16)
                sp.dma_start(b_dmask[:, :, :], aps["c_dmask"]).then_inc(b_clanded, 16)
                states = aps["state_b_s"][0].rearrange("b h d e -> h d b e")
                new_states = aps["new_b_s_s"][0].rearrange("b h d e -> h d b e")
                sp.dma_start(b_S[:, 1, :, :], states[0]).then_inc(b_sin[1], 16)
                sp.wait_ge(b_s, 16)
                sp.dma_start(aps["new_b_s_p"][0, 0].rearrange("h d e -> d h e"), b_S[:, 0, :, :]).then_inc(b_pout, 16)
                sp.wait_ge(b_pout, 16)
                for h in range(1, HB_ + 1):
                    slot = (h + 1) % 2
                    if h < HB_:
                        if h >= 2:
                            sp.wait_ge(b_sout[slot], 16 * (h // 2))
                        sp.dma_start(b_S[:, slot, :, :], states[h]).then_inc(b_sin[slot], 16)
                    sp.wait_ge(b_sd, h)
                    sp.dma_start(new_states[h - 1], b_S[:, h % 2, :, :]).then_inc(b_sout[h % 2], 16)
                for i in range(2):
                    sp.wait_ge(b_sout[i], 64)
                for p in range(2, 10):
                    sp_weights(sp, WeightTile("b_out", l, p))

            @staticmethod
            def pool(pool, l):
                place_free(pool, l)
                for i in range(2):
                    nc.gpsimd.memset(b_xp[:, i, 0:CONV - 1], 0.0).then_inc(b_zero, 1)
                nc.gpsimd.memset(eps_l2[:, :], 1e-6).then_inc(b_zero, 1)
                for j in range(2 * HB_):
                    pool.wait_ge(b_silu, j + 1)
                    if j >= 1:
                        pool.wait_ge(b_sum, j)
                    nc.gpsimd.tensor_tensor(b_sq[:, :], b_qkv[:, j, :], b_qkv[:, j, :], ALU.mult).then_inc(b_sqd, 1)
                pool.wait_ge(b_qk, 16)
                pool.wait_ge(b_gate_dve, 7)
                for i in range(2):
                    pool.wait_ge(b_tlout[i], 96)
                nc.gpsimd.memset(b_S[:, 0, :, :], 0.0).then_inc(b_zero, 1)
                pool.wait_ge(b_clanded, 16 * 8)
                for i in range(QT + 1):
                    w = width(i)
                    for k in range(levels_of(i)):
                        for hb in range(2):
                            pool.wait_ge(b_a, 2 * i + hb + 1)
                            if k >= 2:
                                pool.wait_ge(b_tu, lev(i, k - 2, hb) + 1)
                            nc.gpsimd.tensor_tensor(b_M[0:w, hb, k % 2, :, 0:w], b_w["e1"][0:w, hb, :, 0:w],
                                                    b_lvl[0:w, k, 0:w].unsqueeze(1).to_broadcast([w, 4, w]), ALU.mult).then_inc(b_m, 1)
                for k in range(KD):
                    pool_sumsq(pool, 2 * l + 1, k)

            @staticmethod
            def pe(pe, l):
                m = 2 * l
                pe.wait_ge(b_landed, 7 * 16)
                nc.tensor.transpose(misc[1][:, 0:CONV * QKV + 1], b_rows[:, :], ident[0:CONV * QKV + 1, 0:CONV * QKV + 1]).then_inc(b_cwT, 1)
                R24 = DEC_B * (CONV - 1)
                for j in range(QKV):
                    pe.wait_ge(b_clanded, 16 * (j // 4 + 1))
                    nc.tensor.transpose(misc[2 + j // 12][:, (j % 12) * R24:(j % 12 + 1) * R24], b_state[:, j % 4, :], ident[0:R24, 0:R24]).then_inc(b_stT, 1)

                def tail(j):
                    pe.wait_ge(b_tailc, j + 1)
                    if j == 0:
                        pe.wait_ge(b_stc, 2)
                    if j >= 8:
                        pe.wait_ge(b_tlc, j // 4 - 1)
                    nc.tensor.transpose(misc[2 + (j // 4) % 2][0:TAILB, (j % 4) * P:(j % 4 + 1) * P], b_tail[:, j % 2, :], ident[:, :]).then_inc(b_tlT, 1)

                def sums(sq, first, bank, col):
                    for i in range(QT + 1):
                        last = nc.tensor.matmul(bank[0:width(i), first + i * 2 * HB_ + col:first + i * 2 * HB_ + col + 1],
                                                sq[:, tcols(i)], ones[:, 0:1], start=True, stop=True)
                    return last

                for j in range(32):
                    t = WeightTile("b_in", l, j)
                    pe_tile(pe, t, act_hi, act_lo, k_ready=(xg_ready, 8 * split_no[m]) if j == 0 else None,
                            between=(lambda: (pe.wait_ge(b_cwc, 1), pe_norm_bcast(pe, m))) if j == 1 else None)
                    if j == 0:
                        pe_norm_sum(pe, m)
                    if 1 <= j <= QKV:
                        tail(j - 1)
                    if 2 <= j < 2 * HB_ + 2:
                        pe.wait_ge(b_sqd, j - 1)
                        sums(b_sq, 128, misc[0], j - 2).then_inc(b_sum, 1)
                pe.wait_ge(b_wabr, 1)
                for i in range(QT + 1):
                    for k in range(KD):
                        for q, (a, w) in enumerate(((act_hi, b_wab_hi), (act_lo, b_wab_hi), (act_hi, b_wab_lo))):
                            last = nc.tensor.matmul(misc[1][0:width(i), i * 2 * HB_:(i + 1) * 2 * HB_], a[:, k, tcols(i)], w[:, k, :],
                                                    start=(k == 0 and q == 0), stop=(k == KD - 1 and q == 2))
                last.then_inc(b_gate_pe, 1)
                pe.wait_ge(b_gate_dve, 1)
                pe.wait_ge(evac_done, base["b_in", l] + 32)
                for j in range(2 * HB_):
                    if j >= 2:
                        pe.wait_ge(b_qk, j - 1)
                    for i in range(QT + 1):
                        w = width(i)
                        last = nc.tensor.matmul(acc[:, j % 2, i // QT, (i % QT) * P:(i % QT) * P + w],
                                                b_rn[0:w, i, j:j + 1].to_broadcast([w, P]), ident[0:w, 0:w], start=True, stop=True)
                    last.then_inc(b_bc, 1)
                pe.wait_ge(b_gate_dve, 4)
                pe.wait_ge(b_gate_dve, 5)
                pe.wait_ge(b_tlc, 6)
                for i in range(QT + 1):
                    w, o = width(i), 0 if i < QT else 2
                    for s in range(2):
                        nc.tensor.matmul(misc[2][0:w, (s * 5 + i) * HB_:(s * 5 + i + 1) * HB_], b_tri[0:w, o + s, 0:w], b_g[0:w, i, :],
                                         start=True, stop=True)
                    if i < QT:
                        for s in range(2):
                            nc.tensor.matmul(misc[2][:, 128 + (2 * i + s) * HB_:128 + (2 * i + s + 1) * HB_],
                                             b_tri[:, 1, CHUNK * s:CHUNK * s + 1].to_broadcast([P, P]), b_g[:, i, :], start=True, stop=True)
                nc.tensor.matmul(misc[2][:, 192:256], ones[0:NS, :], b_gm[:, :, :].rearrange("p b h -> p (b h)"), start=True, stop=True).then_inc(b_gate_pe, 1)
                pe.wait_ge(b_gate_dve, 7)
                pe.wait_ge(b_qk, 16)
                pe.wait_ge(b_zero, 4)
                for i in range(QT + 1):
                    w, tc = width(i), tcols(i)
                    for hb in range(2):
                        u = 2 * i + hb
                        if i >= 1:
                            pe.wait_ge(b_oc, 4 * (i - 1) + 2 + hb + 1)
                            pe.wait_ge(b_s, 4 * (i - 1) + 2 + hb + 1)
                        for h in range(4):
                            nc.tensor.transpose(acc[0:w, hb, 0, h * P:(h + 1) * P], b_qkv[:, HB_ + 4 * hb + h, tc], ident[:, :])
                        for h in range(4):
                            last = nc.tensor.transpose(acc[0:w, hb, 1, h * P:(h + 1) * P], b_qkv[:, 2 * HB_ + 4 * hb + h, tc], ident[:, :])
                        last.then_inc(b_kvT, 1)
                    for hb in range(2):
                        u = 2 * i + hb
                        for h in range(4):
                            kT = b_qkv[:, HB_ + 4 * hb + h, tc]
                            nc.tensor.matmul(misc[2 * hb][0:w, h * P:h * P + w], kT, kT, start=True, stop=True)
                        for h in range(4):
                            nc.tensor.matmul(misc[2 * hb + 1][0:w, h * P:h * P + w], b_qkv[:, HB_ + 4 * hb + h, tc],
                                             b_qkv[:, 4 * hb + h, tc], start=True, stop=True)
                        pe.wait_ge(b_kv, u + 1)
                        for h in range(4):
                            hh = 4 * hb + h
                            last = nc.tensor.matmul(acc[:, hb, 0, h * P:h * P + w], b_g[0:w, i, hh:hh + 1].to_broadcast([w, P]),
                                                    b_tri[0:w, 0 if i < QT else 2, 0:w], start=True, stop=True)
                        last.then_inc(b_kk, 1)
                    for k in range(levels_of(i)):
                        for hb in range(2):
                            pe.wait_ge(b_m, lev(i, k, hb) + 1)
                            if k == 0:
                                pe.wait_ge(b_att, 2 * i + hb + 1)
                            else:
                                pe.wait_ge(b_tu, lev(i, k - 1, hb) + 1)
                            for h in range(4):
                                last = nc.tensor.matmul(misc[2 * hb][0:w, h * P:h * P + w], b_M[0:w, hb, k % 2, h, 0:w],
                                                        ident[0:w, 0:w] if k == 0 else b_w["U"][0:w, hb, h, 0:w], start=True, stop=True)
                            last.then_inc(b_zp, 1)
                        if k == 0:
                            continue
                        for hb in range(2):
                            pe.wait_ge(b_zc, lev(i, k, hb) + 1)
                            for h in range(4):
                                last = nc.tensor.matmul(misc[2 * hb + 1][0:w, h * P:h * P + w], b_w["T"][0:w, hb, h, 0:w],
                                                        b_w["Z"][0:w, hb, h, 0:w], start=True, stop=True)
                            if k < levels_of(i) - 1:
                                for h in range(4):
                                    last = nc.tensor.matmul(acc[0:w, hb, 0, h * P:h * P + w], b_w["Z"][0:w, hb, h, 0:w],
                                                            b_w["T"][0:w, hb, h, 0:w], start=True, stop=True)
                            last.then_inc(b_delta, 1)
                    for hb in range(2):
                        pe.wait_ge(b_tu, lev(i, levels_of(i) - 1, hb) + 1)
                        for h in range(4):
                            last = nc.tensor.matmul(misc[2 * hb][:, h * P:h * P + w], b_w["kbe"][0:w, hb, h, :], b_w["U"][0:w, hb, h, 0:w],
                                                    start=True, stop=True)
                        last.then_inc(b_wT, 1)
                    if i < QT:
                        for n in range(2):
                            c = 4 * i + 2 * n
                            r = slice(CHUNK * n, CHUNK * (n + 1))
                            for hb in range(2):
                                pe.wait_ge(b_wc, 2 * i + hb + 1)
                                if c >= 2:
                                    pe.wait_ge(b_s, c - 2 + hb + 1)
                                for h in range(4):
                                    out = misc[2 * hb + 1][r, h * P:(h + 1) * P]
                                    nc.tensor.matmul(out, b_w["U"][:, hb, h, r], b_w["vb"][:, hb, h, :], start=True, stop=False)
                                    last = nc.tensor.matmul(out, b_w["Z"][:, hb, h, r], b_S[:, 0, 4 * hb + h, :], start=False, stop=True)
                                last.then_inc(b_vn, 1)
                            for hb in range(2):
                                pe.wait_ge(b_vnc, c + hb + 1)
                                if n == 1:
                                    pe.wait_ge(b_oc, c - 2 + hb + 1)
                                for h in range(4):
                                    out = acc[:, hb, 0, h * CHUNK:(h + 1) * CHUNK]
                                    nc.tensor.matmul(out, b_S[:, 0, 4 * hb + h, :], b_w["eg"][:, hb, h, r], start=True, stop=False)
                                    nc.tensor.matmul(out, b_w["T"][r, hb, h, :], b_w["e2"][r, hb, h, r], start=False, stop=True)
                                for h in range(4):
                                    last = nc.tensor.matmul(acc[:, hb, 1, h * P:(h + 1) * P], b_w["kd"][r, hb, h, :], b_w["T"][r, hb, h, :],
                                                            start=True, stop=True)
                                last.then_inc(b_ob, 1)
                for h in range(HB_):
                    hb, hh = h // 4, h % 4
                    pe.wait_ge(b_wc, 2 * QT + 2)
                    pe.wait_ge(b_sin[(h + 1) % 2], 16 * (h // 2 + 1))
                    S = b_S[:, (h + 1) % 2, :, :]
                    if h >= 1:
                        pe.wait_ge(b_sd, h)
                    out = acc[:, 0, 0, 0:NS]
                    nc.tensor.matmul(out, b_w["vb"][0:NS, hb, hh, :], b_w["U"][0:NS, hb, hh, 0:NS], start=True, stop=False)
                    for b in range(DEC_B):
                        c = slice(DEC_T * b, DEC_T * (b + 1))
                        last = nc.tensor.matmul(acc[:, 0, 0, c], S[:, b, :], b_w["Z"][:, hb, hh, c], start=False, stop=(b == DEC_B - 1))
                    last.then_inc(b_vn, 1)
                    pe.wait_ge(b_vTc, 2 * h + 1)
                    nc.tensor.transpose(acc[0:NS, 0, 1, 0:P], b_h32v[:, :], ident[:, :]).then_inc(b_vT, 1)
                    pe.wait_ge(b_vTc, 2 * h + 2)
                    nc.tensor.matmul(acc[:, 1, 0, 0:NS], b_w["T"][0:NS, hb, hh, :], b_w["e2"][0:NS, hb, hh, 0:NS], start=True, stop=False)
                    for b in range(DEC_B):
                        c = slice(DEC_T * b, DEC_T * (b + 1))
                        last = nc.tensor.matmul(acc[:, 1, 0, c], S[:, b, :], b_w["eg"][:, hb, hh, c], start=False, stop=(b == DEC_B - 1))
                    last.then_inc(b_ob, 1)
                    pe.wait_ge(b_vm, h + 1)
                    for s in range(2):
                        last = nc.tensor.matmul(misc[s][:, :], b_w["kd"][0:NS, hb, hh, :], b_vmask[:, s * 512:(s + 1) * 512], start=True, stop=True)
                    last.then_inc(b_su, 1)
                for h in range(HB_):
                    pe.wait_ge(b_osqd, h + 1)
                    sums(b_osq[:, h % 2, :], 0, misc[2], h).then_inc(b_os, 1)
                pe.wait_ge(b_gate_dve, 8)
                for h in range(HB_):
                    if h >= 2:
                        pe.wait_ge(b_on, h - 1)
                    for i in range(QT + 1):
                        w = width(i)
                        last = nc.tensor.matmul(acc[:, h % 2, i // QT, (i % QT) * P:(i % QT) * P + w],
                                                b_rn[0:w, i, h:h + 1].to_broadcast([w, P]), ident[0:w, 0:w], start=True, stop=True)
                    last.then_inc(b_obc, 1)
                pe.wait_ge(b_on, HB_)
                for o in range(KD):
                    pe_tile(pe, WeightTile("b_out", l, o), act_hi, act_lo, k_ready=(b_olo, 0) if o == 0 else None)

            @staticmethod
            def act(act, l):
                m = 2 * l
                act.wait_ge(b_cwT, 1)
                nc.scalar.activation(b_cw[:, :], misc[1][:, 0:CONV * QKV + 1], ACT.Copy).then_inc(b_cwc, 1)
                for s in range(2):
                    act.wait_ge(b_stT, 12 * (s + 1))
                    nc.scalar.activation(b_cst[:, 12 * s:12 * s + 12, :, :],
                                         misc[2 + s][:, 0:288].rearrange("p (k b j) -> p k b j", k=12, b=DEC_B), ACT.Copy).then_inc(b_stc, 1)
                act.wait_ge(b_landed, 7 * 16)
                nc.scalar.activation(b_wab_hi[:, :, :], b_wab[:, :, :], ACT.Copy).then_inc(b_wabh, 1)
                act.wait_ge(b_stc, 2)

                def sample_of(ap, lo, hi):
                    return ap[:, XP:XW].rearrange("p (b j) -> p b j", j=XS)[:, :, lo:hi]

                for j in range(32):
                    act_split(act, WeightTile("b_in", l, j + 2))
                    if j == 0:
                        act_norm_std(act, m)
                        act_norm_R(act, m)
                    if j < QKV:
                        xp = b_xp[:, j % 2, :]
                        if j >= 2:
                            act.wait_ge(b_conv, j - 1)
                        nc.scalar.activation(sample_of(xp, 0, CONV - 1), b_cst[:, j, :, :], ACT.Copy).then_inc(b_pre, 1)
                        act.wait_ge(evac_done, base["b_in", l] + j + 1)
                        if j >= 2:
                            act.wait_ge(b_tlT, j - 1)
                        nc.scalar.activation(b_tail[:, j % 2, 0:3], xp[:, SEQ:XP], ACT.Copy)
                        nc.scalar.activation(b_tail[:, j % 2, 3:].rearrange("p (b j) -> p b j", b=DEC_B), sample_of(xp, DEC_T, XS), ACT.Copy).then_inc(b_tailc, 1)
                        act.wait_ge(b_conv, j + 1)
                        xc = b_xc[:, j % 2, :]
                        nc.scalar.activation(b_qkv[:, j, 0:SEQ], xc[:, 0:SEQ], ACT.Silu)
                        nc.scalar.activation(b_qkv[:, j, SEQ:].rearrange("p (b t) -> p b t", t=DEC_T), sample_of(xc, 0, DEC_T), ACT.Silu).then_inc(b_silu, 1)
                        if j % 4 == 0 and j:
                            tail_out(act, j // 4 - 1)
                    else:
                        if j == QKV:
                            tail_out(act, 5)
                        act.wait_ge(evac_done, base["b_in", l] + j + 1)
                        nc.scalar.activation(b_z[:, j - QKV, :], b_z[:, j - QKV, :], ACT.Silu)
                act.wait_ge(b_sum, 16)
                act.wait_ge(b_zero, 3)
                for i in range(QT + 1):
                    w = width(i)
                    last = nc.scalar.activation(b_rn[0:w, i, :], misc[0][0:w, 128 + 16 * i:144 + 16 * i], ACT.Sqrt, bias=eps_l2[0:w, 0:1])
                last.then_inc(b_gate_act, 1)
                act.wait_ge(b_gate_dve, 2)
                nc.scalar.activation(b_tmp[:, :, :, :], b_tmp[:, :, :, :], ACT.Exp)
                nc.scalar.activation(b_par[:, HB_:], b_par[:, HB_:], ACT.Exp).then_inc(b_gate_act, 1)
                act.wait_ge(b_gate_dve, 3)
                nc.scalar.activation(b_tmp[:, 0, :, :], b_tmp[:, 0, :, :], ACT.Ln).then_inc(b_gate_act, 1)
                act.wait_ge(b_gate_pe, 2)
                nc.scalar.activation(b_dl[:, :, :], misc[2][:, 128:256].rearrange("p (c h) -> p c h", h=HB_), ACT.Exp)
                nc.scalar.activation(b_tmp[:, 1, 0:QT, :], misc[2][:, 40:72].rearrange("p (i h) -> p i h", h=HB_), ACT.Copy)
                nc.scalar.activation(b_tmp[0:NS, 1, QT, :], misc[2][0:NS, 72:80], ACT.Copy)
                nc.scalar.activation(b_G[:, 0:QT, :], misc[2][:, 0:32].rearrange("p (i h) -> p i h", h=HB_), ACT.Copy)
                nc.scalar.activation(b_G[0:NS, QT, :], misc[2][0:NS, 32:40], ACT.Copy).then_inc(b_gate_act, 1)
                act.wait_ge(b_gate_dve, 6)
                act.wait_ge(b_gate_act, 4)
                nc.scalar.activation(b_kdf[:, :, :], b_tmp[:, 1, :, :], ACT.Exp)
                nc.scalar.activation(b_be[:, :, :], b_G[:, :, :], ACT.Exp).then_inc(b_gate_act, 1)
                for i in range(QT + 1):
                    w = width(i)
                    for hb in range(2):
                        u = 2 * i + hb
                        act.wait_ge(b_e, 2 * u + 1)
                        nc.scalar.activation(b_w["e1"][0:w, hb, :, 0:w], b_w["e1"][0:w, hb, :, 0:w], ACT.Exp, scale=-1.0).then_inc(b_ex, 1)
                        act.wait_ge(b_e, 2 * u + 2)
                        nc.scalar.activation(b_w["e2"][0:w, hb, :, 0:w], b_w["e2"][0:w, hb, :, 0:w], ACT.Exp).then_inc(b_ex, 1)
                        nc.scalar.activation(b_w["eg"][:, hb, :, 0:w], heads(acc[:, hb, 0, :])[:, :, 0:w], ACT.Exp).then_inc(b_ex, 1)
                    for k in range(levels_of(i)):
                        for hb in range(2):
                            act.wait_ge(b_zp, lev(i, k, hb) + 1)
                            nc.scalar.activation(b_w["Z"][0:w, hb, :, 0:w], heads(misc[2 * hb][0:w, :])[:, :, 0:w], ACT.Copy).then_inc(b_zc, 1)
                    for hb in range(2):
                        act.wait_ge(b_wT, 2 * i + hb + 1)
                        nc.scalar.activation(b_w["Z"][:, hb, :, 0:w], heads(misc[2 * hb][:, :])[:, :, 0:w], ACT.Copy, scale=-1.0).then_inc(b_wc, 1)
                    if i < QT:
                        for n in range(2):
                            c = 4 * i + 2 * n
                            r = slice(CHUNK * n, CHUNK * (n + 1))
                            for hb in range(2):
                                act.wait_ge(b_vn, c + hb + 1)
                                nc.scalar.activation(b_w["T"][r, hb, :, :], heads(misc[2 * hb + 1][r, :]), ACT.Copy).then_inc(b_vnc, 1)
                            for hb in range(2):
                                act.wait_ge(b_ob, c + hb + 1)
                                o = i * P + n * CHUNK
                                nc.scalar.activation(b_qkv[:, 4 * hb:4 * hb + 4, o:o + CHUNK],
                                                     acc[:, hb, 0, 0:4 * CHUNK].rearrange("p (h c) -> p h c", h=4), ACT.Copy).then_inc(b_oc, 1)
                for h in range(HB_):
                    hb, hh = h // 4, h % 4
                    act.wait_ge(b_vn, 16 + h + 1)
                    nc.scalar.activation(b_h32v[:, :], acc[:, 0, 0, 0:NS], ACT.Copy).then_inc(b_vTc, 1)
                    act.wait_ge(b_vT, h + 1)
                    nc.scalar.activation(b_w["T"][0:NS, hb, hh, :], acc[0:NS, 0, 1, 0:P], ACT.Copy).then_inc(b_vTc, 1)
                    act.wait_ge(b_ob, 16 + h + 1)
                    nc.scalar.activation(b_qkv[:, h, SEQ:TOK], acc[:, 1, 0, 0:NS], ACT.Copy).then_inc(b_oc, 1)
                act.wait_ge(b_oc, 16 + HB_)
                for s in range(2):
                    act.wait_ge(b_sout[s], 64)
                for h in range(HB_):
                    if h >= 2:
                        act.wait_ge(b_os, h - 1)
                    nc.scalar.activation(b_osq[:, h % 2, :], b_qkv[:, h, :], ACT.Square).then_inc(b_osqd, 1)
                act.wait_ge(b_os, HB_)
                for i in range(QT + 1):
                    w = width(i)
                    last = nc.scalar.activation(b_rn[0:w, i, 0:HB_], misc[2][0:w, 16 * i:16 * i + HB_], ACT.Sqrt, scale=1.0 / P, bias=eps_l2[0:w, 0:1])
                last.then_inc(b_gate_act, 1)
                for h in range(HB_):
                    act.wait_ge(b_og, h + 1)
                    nc.scalar.activation(act_hi[:, h, :], b_h32[:, h % 2, :], ACT.Copy).then_inc(b_ohi, 1)
                for o in range(KD):
                    act_split(act, WeightTile("b_out", l, o + 2))
                act.wait_ge(evac_done, base["b_out", l] + KD)
                for k in range(KD):
                    act_gain(act, 2 * l + 1, k)

            @staticmethod
            def dve(dve, l):
                m = 2 * l
                sub = lambda ap, lo, hi: ap[:, XP:XW].rearrange("p (b j) -> p b j", j=XS)[:, :, lo:hi]
                for j in range(32):
                    t = WeightTile("b_in", l, j)
                    dve_split(dve, WeightTile("b_in", l, j + 2))
                    if j == 0:
                        dve_norm_diag(dve, m)
                        dve.wait_ge(r_ready, norm_no[m] + 1)
                        dve.wait_ge(b_wabh, 1)
                        nc.vector.tensor_tensor(b_wab_lo[:, :, :], b_wab[:, :, :], b_wab_hi[:, :, :].bitcast(F32), ALU.subtract).then_inc(b_wabr, 1)
                        dve.wait_ge(b_cwc, 1)
                        dve.wait_ge(b_zero, 3)
                    dve.wait_ge(acc_ready, t.n + 1)
                    if j >= QKV:
                        nc.vector.tensor_tensor(halves(b_z[:, j - QKV, :]), acc_of(t), halves(R[:, :]), ALU.mult).then_inc(evac_done, 1)
                        continue
                    xp, xc = b_xp[:, j % 2, :], b_xc[:, j % 2, :]
                    if j >= 2:
                        dve.wait_ge(b_tailc, j - 1)
                        dve.wait_ge(b_silu, j - 1)
                    pre = CONV - 1
                    nc.vector.tensor_tensor(xp[:, pre:pre + HALF], acc[:, t.first % 2, 0, 0:HALF], R[:, 0:HALF], ALU.mult)
                    nc.vector.tensor_tensor(xp[:, pre + HALF:XP], acc[:, t.first % 2, 1, 0:SEQ - HALF], R[:, HALF:SEQ], ALU.mult)
                    nc.vector.tensor_tensor(sub(xp, pre, XS), acc[:, t.first % 2, 1, SEQ - HALF:HALF].rearrange("p (b t) -> p b t", t=DEC_T),
                                            R[:, SEQ:TOK].rearrange("p (b t) -> p b t", t=DEC_T), ALU.mult).then_inc(evac_done, 1)
                    dve.wait_ge(evac_done, t.n + 1)
                    dve.wait_ge(b_pre, j + 1)
                    chain(dve, nc.vector.tensor_scalar(xc[:, 0:XF], xp[:, 0:XF], b_cw[:, j:j + 1], None, ALU.mult))
                    for q in range(1, CONV):
                        ins = nc.vector.scalar_tensor_tensor(xc[:, 0:XF], xp[:, q:q + XF], b_cw[:, QKV * q + j:QKV * q + j + 1], xc[:, 0:XF],
                                                             ALU.mult, ALU.add)
                        if q < CONV - 1:
                            chain(dve, ins)
                    ins.then_inc(b_conv, 1)
                dve.wait_ge(b_gate_act, 1)
                chain(dve, nc.vector.memset(b_tmp[:, :, :, :], 0.0))
                for i in range(QT + 1):
                    w = width(i)
                    last = nc.vector.reciprocal(b_rn[0:w, i, :], b_rn[0:w, i, :])
                chain(dve, last)
                chain(dve, nc.vector.memset(b_ab[:, :, :], 0.0))
                for i in range(QT + 1):
                    w = width(i)
                    last = nc.vector.tensor_scalar(b_rn[0:w, i, 0:HB_], b_rn[0:w, i, 0:HB_], float(P) ** -0.5, None, ALU.mult)
                last.then_inc(b_gate_dve, 1)
                dve.wait_ge(b_gate_pe, 1)
                for i in range(QT + 1):
                    w = width(i)
                    last = nc.vector.tensor_scalar(b_ab[0:w, i, :], misc[1][0:w, 16 * i:16 * i + 16], rstd[0:w, i:i + 1], None, ALU.mult)
                chain(dve, last)
                a5, b5 = b_ab[:, :, 0:HB_], b_ab[:, :, HB_:]
                chain(dve, nc.vector.tensor_tensor(a5, a5, b_par[:, 0:HB_].unsqueeze(1).to_broadcast([P, QT + 1, HB_]), ALU.add))
                nc.vector.scalar_tensor_tensor(b_tmp[:, 0, :, :], a5, -1.0, a5, ALU.mult, ALU.min)
                nc.vector.tensor_scalar(b_tmp[:, 1, :, :], b5, -1.0, None, ALU.mult).then_inc(b_gate_dve, 1)
                dve.wait_ge(b_gate_act, 2)
                chain(dve, nc.vector.tensor_scalar(b_tmp[:, :, :, :], b_tmp[:, :, :, :], 1.0, None, ALU.add))
                nc.vector.reciprocal(b_beta[:, :, :], b_tmp[:, 1, :, :]).then_inc(b_gate_dve, 1)
                dve.wait_ge(b_gate_act, 3)
                chain(dve, nc.vector.scalar_tensor_tensor(b_g[:, :, :], a5, 0.0, b_tmp[:, 0, :, :], ALU.max, ALU.add))
                chain(dve, nc.vector.scalar_tensor_tensor(b_g[:, :, :], b_g[:, :, :], -1.0,
                                                          b_par[:, HB_:].unsqueeze(1).to_broadcast([P, QT + 1, HB_]), ALU.mult, ALU.mult))
                nc.vector.tensor_tensor(b_gm[:, :, :], b_g[0:NS, QT, :].unsqueeze(1).to_broadcast([NS, DEC_B, HB_]),
                                        b_bmask[:, :].unsqueeze(2).to_broadcast([NS, DEC_B, HB_]), ALU.mult).then_inc(b_gate_dve, 1)
                dve.wait_ge(b_gate_dve, 4)
                nc.vector.memset(b_G[:, :, :], 0.0).then_inc(b_gate_dve, 1)
                for j in range(2 * HB_):
                    dve.wait_ge(b_bc, j + 1)
                    nc.vector.tensor_tensor(b_qkv[:, j, 0:SEQ], b_qkv[:, j, 0:SEQ], acc[:, j % 2, 0, :], ALU.mult)
                    nc.vector.tensor_tensor(b_qkv[:, j, SEQ:TOK], b_qkv[:, j, SEQ:TOK], acc[:, j % 2, 1, 0:NS], ALU.mult).then_inc(b_qk, 1)
                dve.wait_ge(b_gate_act, 4)
                nc.vector.tensor_tensor(b_tmp[:, 1, :, :], b_tmp[:, 1, :, :], b_G[:, :, :], ALU.subtract).then_inc(b_gate_dve, 1)
                dve.wait_ge(b_gate_act, 5)
                nc.vector.tensor_tensor(b_be[:, :, :], b_be[:, :, :], b_beta[:, :, :], ALU.mult).then_inc(b_gate_dve, 1)
                dve.wait_ge(b_gate_dve, 7)
                dve.wait_ge(b_clanded, 16 * 8)
                for i in range(QT + 1):
                    w = width(i)
                    o = 0 if i < QT else 2
                    for hb in range(2):
                        u = 2 * i + hb
                        hs = slice(4 * hb, 4 * hb + 4)
                        dve.wait_ge(b_kvT, u + 1)
                        per = lambda f: f[0:w, i, hs].unsqueeze(2).to_broadcast([w, 4, P])
                        nc.vector.tensor_tensor(b_w["kbe"][0:w, hb], heads(acc[0:w, hb, 0, :]), per(b_be), ALU.mult)
                        nc.vector.tensor_tensor(b_w["kd"][0:w, hb], heads(acc[0:w, hb, 0, :]), per(b_kdf), ALU.mult)
                        nc.vector.tensor_tensor(b_w["vb"][0:w, hb], heads(acc[0:w, hb, 1, :]), per(b_beta), ALU.mult).then_inc(b_kv, 1)
                    for hb in range(2):
                        dve.wait_ge(b_kk, 2 * i + hb + 1)
                        for h in range(4):
                            last = nc.vector.scalar_tensor_tensor(b_w["e1"][0:w, hb, h, 0:w], acc[0:w, hb, 0, h * P:h * P + w],
                                                                  b_G[0:w, i, 4 * hb + h:4 * hb + h + 1], b_dmask[0:w, o, 0:w], ALU.subtract, ALU.add)
                        last.then_inc(b_e, 1)
                        for h in range(4):
                            last = nc.vector.scalar_tensor_tensor(b_w["e2"][0:w, hb, h, 0:w], acc[0:w, hb, 0, h * P:h * P + w],
                                                                  b_G[0:w, i, 4 * hb + h:4 * hb + h + 1], b_dmask[0:w, o + 1, 0:w], ALU.subtract, ALU.add)
                        last.then_inc(b_e, 1)
                    for hb in range(2):
                        u = 2 * i + hb
                        dve.wait_ge(b_ex, 3 * u + 1)
                        for h in range(4):
                            last = nc.vector.scalar_tensor_tensor(b_w["e1"][0:w, hb, h, 0:w], misc[2 * hb][0:w, h * P:h * P + w],
                                                                  b_beta[0:w, i, 4 * hb + h:4 * hb + h + 1], b_w["e1"][0:w, hb, h, 0:w],
                                                                  ALU.mult, ALU.mult)
                        last.then_inc(b_a, 1)
                        dve.wait_ge(b_ex, 3 * u + 3)
                        nc.vector.tensor_tensor(b_w["e2"][0:w, hb, :, 0:w], heads(misc[2 * hb + 1][0:w, :])[:, :, 0:w],
                                                b_w["e2"][0:w, hb, :, 0:w], ALU.mult)
                        nc.vector.tensor_tensor(b_w["eg"][:, hb, :, 0:w], b_qkv[:, 4 * hb:4 * hb + 4, tcols(i)],
                                                b_w["eg"][:, hb, :, 0:w], ALU.mult).then_inc(b_att, 1)
                    eye = ident[0:w, 0:w].unsqueeze(1).to_broadcast([w, 4, w])
                    for k in range(levels_of(i)):
                        for hb in range(2):
                            T, U, Z = (b_w[nm][0:w, hb, :, 0:w] for nm in "TUZ")
                            if k == 0:
                                dve.wait_ge(b_zc, lev(i, k, hb) + 1)
                                dve.wait_ge(b_m, lev(i, k, hb) + 1)
                                nc.vector.tensor_tensor(U, eye, Z, ALU.subtract)
                                nc.vector.tensor_tensor(T, eye, b_M[0:w, hb, 0, :, 0:w], ALU.subtract).then_inc(b_tu, 1)
                            else:
                                dve.wait_ge(b_delta, 10 * i + 2 * (k - 1) + hb + 1)
                                if k == 1:
                                    dve.wait_ge(b_tu, lev(i, k, hb) - 1)
                                last = nc.vector.tensor_tensor(U, U, heads(misc[2 * hb + 1][0:w, :])[:, :, 0:w], ALU.subtract)
                                if k < levels_of(i) - 1:
                                    last = nc.vector.tensor_tensor(T, T, heads(acc[0:w, hb, 0, :])[:, :, 0:w], ALU.subtract)
                                last.then_inc(b_tu, 1)
                    if i < QT:
                        for n in range(2):
                            for hb in range(2):
                                c = 4 * i + 2 * n + hb
                                dve.wait_ge(b_ob, c + 1)
                                for h in range(4):
                                    S = b_S[:, 0, 4 * hb + h, :]
                                    last = nc.vector.scalar_tensor_tensor(S, S, b_dl[:, 2 * i + n, 4 * hb + h:4 * hb + h + 1],
                                                                          acc[:, hb, 1, h * P:(h + 1) * P], ALU.mult, ALU.add)
                                last.then_inc(b_s, 1)
                for h in range(HB_):
                    hb, hh = h // 4, h % 4
                    dve.wait_ge(b_vTc, 2 * h + 2)
                    if h >= 1:
                        dve.wait_ge(b_su, h)
                    nc.vector.tensor_tensor(b_vmask[:, :].rearrange("p (b e) -> p b e", b=DEC_B),
                                            b_w["T"][0:NS, hb, hh, :].unsqueeze(1).to_broadcast([NS, DEC_B, P]),
                                            b_bmask[:, :].unsqueeze(2).to_broadcast([NS, DEC_B, P]), ALU.mult).then_inc(b_vm, 1)
                    dve.wait_ge(b_su, h + 1)
                    for b in range(DEC_B):
                        S = b_S[:, (h + 1) % 2, b, :]
                        last = nc.vector.scalar_tensor_tensor(S, S, b_dl[:, 2 * QT + b, h:h + 1], misc[b // 4][:, (b % 4) * P:(b % 4 + 1) * P],
                                                              ALU.mult, ALU.add)
                    last.then_inc(b_sd, 1)
                dve.wait_ge(b_gate_act, 6)
                for i in range(QT + 1):
                    w = width(i)
                    last = nc.vector.reciprocal(b_rn[0:w, i, 0:HB_], b_rn[0:w, i, 0:HB_])
                last.then_inc(b_gate_dve, 1)
                nw = b_cw[:, CONV * QKV:CONV * QKV + 1]
                for h in range(HB_):
                    dve.wait_ge(b_obc, h + 1)
                    if h >= 2:
                        dve.wait_ge(b_olo, h - 1)
                    o32 = b_h32[:, h % 2, :]
                    nc.vector.scalar_tensor_tensor(o32[:, 0:SEQ], b_qkv[:, h, 0:SEQ], nw, acc[:, h % 2, 0, :], ALU.mult, ALU.mult)
                    nc.vector.scalar_tensor_tensor(o32[:, SEQ:TOK], b_qkv[:, h, SEQ:TOK], nw, acc[:, h % 2, 1, 0:NS], ALU.mult, ALU.mult).then_inc(b_on, 1)
                    dve.wait_ge(b_on, h + 1)
                    nc.vector.tensor_tensor(o32, o32, b_z[:, h, :], ALU.mult).then_inc(b_og, 1)
                    dve.wait_ge(b_ohi, h + 1)
                    nc.vector.tensor_tensor(act_lo[:, h, :], o32, act_hi[:, h, :].bitcast(F32), ALU.subtract).then_inc(b_olo, 1)
                for o in range(KD):
                    t = WeightTile("b_out", l, o)
                    dve_split(dve, WeightTile("b_out", l, o + 2))
                    dve.wait_ge(acc_ready, t.n + 1)
                    nc.vector.tensor_tensor(halves(x[:, o, :]), acc_of(t), halves(x[:, o, :]), ALU.add).then_inc(evac_done, 1)
                for k in range(KD):
                    dve_gain(dve, 2 * l + 1, k)

        def tail_out(act, c):
            act.wait_ge(b_tlT, 4 * c + 4)
            if c >= 2:
                act.wait_ge(b_tlout[c % 2], 32 * (c // 2))
            nc.scalar.activation(b_tailT[:, c % 2, :], misc[2 + c % 2][0:TAILB, :], ACT.Copy).then_inc(b_tlc, 1)

        mixers[1] = MixB

        block = ctx.enter_context(nc.Block())
        first_norm = norms[0]

        def next_norm(l):
            return 2 * (l + 1)

        @block.sync
        def _(sp):
            sp.dma_start(ident[:, :], aps["c_ident"]).then_inc(const_in, 16)
            sp.dma_start(gain_rows[0:DEPTH * KD, :], aps["norm1"].rearrange("l (k p) -> (l k) p", p=P)).then_inc(const_in, 16)
            sp.dma_start(gain_rows[DEPTH * KD:2 * DEPTH * KD, :], aps["norm2"].rearrange("l (k p) -> (l k) p", p=P)).then_inc(const_in, 16)
            sp.dma_start(gain_rows[2 * DEPTH * KD:(2 * DEPTH + 1) * KD, :], aps["norm_f"].rearrange("(k p) -> k p", p=P)).then_inc(const_in, 16)
            sp.dma_start(gain_rows[(2 * DEPTH + 1) * KD:, :], aps["c_scale"][0].rearrange("(k p) -> k p", p=P)).then_inc(const_in, 16)
            for j in range(QT):
                sp.dma_start(x_in[:, j, :], aps["x_prompt"][0, j * P:(j + 1) * P, :]).then_inc(x_landed, 16)
            sp.dma_start(x_in[0:NS, QT, :], aps["x_sample"].rearrange("b t d -> (b t) d")).then_inc(x_landed, 16)
            for p in range(2):
                sp_weights(sp, WeightTile(order[0][0], order[0][1], p))
            for l in layers:
                mixers[l % 3].sp(sp, l)
                sp_mlp(sp, l)
            sp.wait_ge(y_copied, 2 * KD)
            for j in range(QT):
                sp.dma_start(aps["y_prompt"][0, j * P:(j + 1) * P, :], y_out[:, j, :]).then_inc(stored, 16)
            sp.dma_start(aps["y_sample"].rearrange("b t d -> (b t) d"), y_out[0:NS, QT, :]).then_inc(stored, 16)
            sp.wait_ge(stored, 16 * (QT + 1))
            sp.wait_ge(caches_copied, 16 * COPIES * FQ * len(layers))

        @block.gpsimd
        def _(pool):
            nc.gpsimd.memset(ones[:, :], 1.0)
            nc.gpsimd.memset(std[:, :], 1.0)
            nc.gpsimd.memset(eps_col[:, :], EPS).then_inc(consts_set, 1)
            for k in range(KD):
                pool_sumsq(pool, first_norm, k)
            for l in layers:
                mixers[l % 3].pool(pool, l)
                pool_mlp(pool, l, next_norm(l))

        @block.scalar
        def _(act):
            act.wait_ge(gain_T, 1)
            nc.scalar.activation(gains[:, :, :], misc[2][:, 0:(2 * DEPTH + 2) * KD].rearrange("p (m k) -> p m k", k=KD),
                                 ACT.Copy).then_inc(gains_done, 1)
            act.wait_ge(gains_done, 1)
            act.wait_ge(consts_set, 1)
            for k in range(KD):
                if first_norm in split_norms:
                    act_gain(act, first_norm, k)
                if k < 2:
                    act_split(act, WeightTile(order[0][0], order[0][1], k))
            for l in layers:
                mixers[l % 3].act(act, l)
                act_mlp(act, l, next_norm(l))
            act_norm_std(act, 2 * DEPTH)
            act_norm_R(act, 2 * DEPTH)
            for k in range(KD):
                act.wait_ge(y_T_done, k + 1)
                nc.scalar.activation(y_out[:, 0:QT, k * P:(k + 1) * P],
                                     acc[:, k % 2, 0, :].rearrange("p (j n) -> p j n", n=P), ACT.Copy).then_inc(y_copied, 1)
                nc.scalar.activation(y_out[0:NS, QT, k * P:(k + 1) * P], acc[0:NS, k % 2, 1, 0:P], ACT.Copy).then_inc(y_copied, 1)

        @block.vector
        def _(dve):
            dve.wait_ge(gains_done, 1)
            for k in range(KD):
                dve.wait_ge(x_T, k + 1)
                nc.vector.tensor_copy(x[:, k, 0:SEQ], acc[:, k % 2, 0, :])
                nc.vector.tensor_copy(x[:, k, SEQ:TOK], acc[:, k % 2, 1, 0:NS]).then_inc(x_ready, 1)
                if first_norm in split_norms:
                    dve_gain(dve, first_norm, k)
                if k < 2:
                    dve_split(dve, WeightTile(order[0][0], order[0][1], k))
            for l in layers:
                mixers[l % 3].dve(dve, l)
                dve_mlp(dve, l, next_norm(l))
            dve_norm_diag(dve, 2 * DEPTH)
            dve.wait_ge(r_ready, len(norms))
            for k in range(KD):
                if k >= 2:
                    dve.wait_ge(y_T_done, k - 1)
                nc.vector.scalar_tensor_tensor(y_T[:, k % 2, :], x[:, k, :], gains[:, 2 * DEPTH, k:k + 1], R[:, :],
                                               ALU.mult, ALU.mult).then_inc(y_ready, 1)

        @block.tensor
        def _(pe):
            pe.wait_ge(const_in, 80)
            rows = (2 * DEPTH + 2) * KD
            nc.tensor.transpose(misc[2][:, 0:rows], gain_rows[:, :], ident[0:rows, 0:rows]).then_inc(gain_T, 1)
            pe.wait_ge(x_landed, 16 * (QT + 1))
            for k in range(KD):
                if k >= 2:
                    pe.wait_ge(x_ready, k - 1)
                for j in range(QT):
                    nc.tensor.transpose(acc[:, k % 2, 0, j * P:(j + 1) * P], x_in[:, j, k * P:(k + 1) * P], ident[:, :])
                nc.tensor.transpose(acc[:, k % 2, 1, 0:NS], x_in[0:NS, QT, k * P:(k + 1) * P],
                                    ident[0:NS, 0:NS]).then_inc(x_T, 1)
            pe.wait_ge(consts_set, 1)
            pe.wait_ge(x_ready, KD)
            for l in layers:
                mixers[l % 3].pe(pe, l)
                pe_mlp(pe, l)
            pe_norm_sum(pe, 2 * DEPTH)
            pe_norm_bcast(pe, 2 * DEPTH)
            pe.wait_ge(evac_done, total)
            for k in range(KD):
                pe.wait_ge(y_ready, k + 1)
                if k >= 2:
                    pe.wait_ge(y_copied, 2 * (k - 1))
                for j in range(QT):
                    nc.tensor.transpose(acc[:, k % 2, 0, j * P:(j + 1) * P], y_T[:, k % 2, j * P:(j + 1) * P], ident[:, :])
                nc.tensor.transpose(acc[0:NS, k % 2, 1, 0:P], y_T[:, k % 2, SEQ:TOK], ident[:, :]).then_inc(y_T_done, 1)


def constants():
    f = np.float32
    c = {"c_ident": np.eye(P, dtype=f)}
    inv = [[f(1) / f(min(w, t + 1)) for t in range(16)] for w in (2, 4, 8, 16)]
    c["c_pool_inv"] = np.broadcast_to(np.array(inv, f), (P, 4, 16)).copy()
    pos = np.concatenate([np.arange(SEQ), np.tile(SEQ + np.arange(DEC_T), DEC_B)]).astype(f)
    half = 32
    freq = (f(10000.0) ** (-np.arange(half, dtype=f) / f(half))).astype(f)
    ang = (pos[None, :] * freq[:, None]).astype(f)
    cos, sin = np.cos(ang).astype(f), np.sin(ang).astype(f)
    c["c_cos"] = np.tile(cos, (4, 1))
    c["c_sin"] = np.tile(np.concatenate([-sin, sin]), (2, 1))
    i, j = np.arange(P)[:, None], np.arange(P)[None, :]
    allowed = np.stack([j <= i, j >= i, (j <= i) & (i % 4 == j % 4)], axis=1)
    c["c_mask"] = np.where(allowed, f(0), f(-1e30)).astype(f)
    row = np.arange(P)
    t, real = row % 4, row % 32 < 24
    k = np.arange(P)
    cached = [k[None, :] >= t[:, None],
              np.repeat(np.arange(4), P)[None, :] == t[:, None],
              (k // 32)[None, :] == t[:, None]]
    new = np.arange(NS)
    both = []
    for batch in range(2):
        mine = (new // 4)[None, :] == (4 * batch + row // 32)[:, None]
        parts = []
        for g in range(3):
            when = (new % 4)[None, :] <= t[:, None] if g == 0 else (new % 4)[None, :] == t[:, None]
            parts += [cached[g], mine & when]
        both.append(np.concatenate(parts, axis=1) | ~real[:, None])
    c["c_smask"] = np.where(np.stack(both, axis=1), f(0), f(-1e30)).astype(f)
    s, q = np.arange(P)[:, None], np.arange(P)[None, :]
    tri, dmask = [], []
    for n in (64, DEC_T):
        same = s // n == q // n
        tri += [same & (s <= q), same]
        dmask += [np.where(same & (q < s), f(0), f(1e30)), np.where(same & (s <= q), f(0), f(-1e30))]
    c["c_tri"] = np.stack(tri, axis=1).astype(f)
    c["c_dmask"] = np.stack(dmask, axis=1).astype(f)
    lvl = [(s // (2 << k) == q // (2 << k)) & (s // (1 << k) % 2 == 1) & (q // (1 << k) % 2 == 0) for k in range(6)]
    c["c_lvl"] = np.stack(lvl, axis=1).astype(f)
    c["c_bmask"] = (np.arange(NS)[:, None] // DEC_T == np.arange(DEC_B)[None, :]).astype(f)
    return c


INPUTS = ("x_prompt", "x_sample", "cache_a_kv1", "cache_a_kv2", "cache_a_kv3", "state_b_s", "state_b_conv", "state_c_pool",
          "norm1", "norm2", "norm_f", "a_w_in", "a_w_out", "b_w_in", "b_conv", "b_a_log", "b_dt_bias", "b_norm", "b_w_out",
          "c_w", "c_scale", "mlp_w1", "mlp_w2")
KV1, KV2, KV3 = (128, 2, 6, 64), (SEQ, 2, 6, 64), (SEQ, 2, 6, 64)
OUTPUTS = (("y_prompt", (1, SEQ, D)), ("y_sample", (DEC_B, DEC_T, D)),
           ("new_a_kv1_p", (2, 1) + KV1), ("new_a_kv2_p", (2, 1) + KV2), ("new_a_kv3_p", (2, 1) + KV3),
           ("new_b_s_p", (1, 1, 8, P, P)), ("new_b_conv_p", (1, 1, 3, 3 * D)), ("new_c_pool_p", (1, 1, 15, D)),
           ("new_a_kv1_s", (2, DEC_B) + KV1), ("new_a_kv2_s", (2, DEC_B) + KV2), ("new_a_kv3_s", (2, DEC_B) + KV3),
           ("new_b_s_s", (1, DEC_B, 8, P, P)), ("new_b_conv_s", (1, DEC_B, 3, 3 * D)), ("new_c_pool_s", (1, DEC_B, 15, D)))


def kernel(**inputs):
    import concourse.bacc as bacc
    from concourse.bass_utils import run_bass_kernel_spmd

    nc = bacc.Bacc("TRN2", target_bir_lowering=False, num_devices=1)
    arrays = {name: np.ascontiguousarray(inputs[name]) for name in INPUTS}
    arrays.update(constants())
    aps = {name: nc.dram_tensor(name, a.shape, F32, kind="ExternalInput").ap() for name, a in arrays.items()}
    for name, shape in OUTPUTS:
        aps[name] = nc.dram_tensor(name, shape, F32, kind="ExternalOutput").ap()
    build_step(nc, aps)
    results = run_bass_kernel_spmd(nc, [arrays], core_ids=[0]).results[0]
    return tuple(results[name] for name, _ in OUTPUTS)
```

```python
from contextlib import ExitStack

import numpy as np
import concourse.bass as bass
from concourse import mybir

F32 = mybir.dt.float32
F32R = mybir.dt.float32r
ALU = mybir.AluOpType
ACT = mybir.ActivationFunctionType
AX = mybir.AxisListType.X

P = 128
D = 1024
KD = D // P
SEQ = 512
DEC_B = 8
DEC_T = 4
NS = DEC_B * DEC_T
TOK = SEQ + NS
HALF = TOK // 2
QT = SEQ // P
DEPTH = 4
FQ = 4
EPS = 1e-6
SLOTS = 4
RAW = 2
KV_SLOTS = 5
KMAX = 9


COPY_PIECES = [(g, 127 * i, 127) for g in (2, 3) for i in range(4)] + [(1, 0, 124)]
COPIES = len(COPY_PIECES)


def build_step(nc, aps):
    layers = range(DEPTH)
    phases = []
    for l in layers:
        if l % 3 == 0:
            phases += [("a_in", l, 27), ("a_out", l, 8)]
        elif l % 3 == 1:
            phases += [("b_in", l, 32), ("b_out", l, 8)]
        phases.append(("mlp", l, 64))
    base, used = {}, {}
    total, per_slot = 0, [0] * RAW
    order = []
    raw_last = [None] * RAW
    found = {}
    for name, l, tiles in phases:
        base[name, l], used[name, l] = total, list(per_slot)
        found[name, l] = list(raw_last)
        order.append((name, l, tiles))
        for pos in range(tiles):
            per_slot[pos % RAW] += 1
            raw_last[pos % RAW] = total + pos
        total += tiles

    class WeightTile:

        def __init__(self, name, l, pos, q=0):
            tiles = dict(((a, b), c) for a, b, c in order)[name, l]
            if isinstance(q, int) and pos + 16 * q >= tiles:
                at = [(a, b) for a, b, _ in order].index((name, l)) + 1
                pos, q = pos + 16 * q - tiles, 0
                name, l = order[at][:2] if at < len(order) else (None, None)
            self.name, self.l, self.pos, self.q = name, l, pos, q
            if name is None:
                return
            self.slot = pos % SLOTS
            self.n = base[name, l] + pos + 16 * q
            self.first = base[name, l] + pos
            self.raw = pos % RAW
            self.landed = 16 * (used[name, l][self.raw] + pos // RAW + 1 + 8 * q)
            before = found[name, l][self.raw]
            self.raw_free = self.n - RAW + 1 if pos >= RAW else None if before is None else before + 1
            self.kt = KMAX if name == "a_out" else KD

    norms = [2 * l + s for l in layers for s in (0, 1)] + [2 * DEPTH]
    norm_no = {m: i for i, m in enumerate(norms)}
    split_norms = [m for m in norms if m != 2 * DEPTH and not (m % 2 == 0 and (m // 2) % 3 == 2)]
    split_no = {m: i for i, m in enumerate(split_norms)}

    with ExitStack() as ctx:
        def sb(name, shape, dt=F32):
            return ctx.enter_context(nc.sbuf_tensor(name, shape, dt))

        def sem(name):
            return ctx.enter_context(nc.semaphore(name))

        x = sb("x", [P, KD, TOK])
        w_raw = sb("w_raw", [P, RAW, KMAX, P])
        w_hi = sb("w_hi", [P, SLOTS, KMAX, P], F32R)
        w_lo = sb("w_lo", [P, SLOTS, KMAX, P], F32R)
        work = {}
        with ExitStack() as place:
            for name in ("e1", "e2", "eg", "kbe", "kd", "vb", "T", "U", "Z"):
                work[f"b_{name}"] = place.enter_context(nc.sbuf_tensor(f"b_{name}", [P, 2, 4, P], F32))
            work["b_dmask"] = place.enter_context(nc.sbuf_tensor("b_dmask", [P, 4, P], F32))
        with ExitStack() as place:
            work["s_kv"] = place.enter_context(nc.sbuf_tensor("s_kv", [P, KV_SLOTS, 4, 384], F32))
        act_hi = sb("act_hi", [P, KMAX, TOK], F32R)
        act_lo = sb("act_lo", [P, KMAX, TOK], F32R)
        R = sb("R", [P, TOK])
        ident = sb("ident", [P, P])
        ones = sb("ones", [P, P])
        gains = sb("gains", [P, 2 * DEPTH + 2, KD])
        gain_rows = sb("gain_rows", [(2 * DEPTH + 2) * KD, P])
        sumsq = sb("sumsq", [P, TOK])
        sq = sb("sq", [P, TOK])
        std = sb("std", [P, QT + 1])
        rstd = sb("rstd", [P, QT + 1])
        diag = sb("diag", [P, QT + 1, P])
        eps_col = sb("eps_col", [P, 1])
        with ExitStack() as local:
            def lsb(name, shape, dt=F32):
                return local.enter_context(nc.sbuf_tensor(name, shape, dt))
            h_hi = lsb("h_hi", [P, KD, TOK], F32R)
            h_lo = lsb("h_lo", [P, KD, TOK], F32R)
            relu_t = lsb("relu_t", [P, 2, TOK])
            h32 = lsb("h32", [P, 2, TOK])
        with ExitStack() as local:
            x_in = lsb("x_in", [P, QT + 1, D])
        with ExitStack() as local:
            y_T = lsb("y_T", [P, 2, TOK])
            y_out = lsb("y_out", [P, QT + 1, D])

        acc = ctx.enter_context(nc.psum_tensor("acc", [P, 2, 2, 512], F32))
        misc = [ctx.enter_context(nc.psum_tensor(f"misc{i}", [P, 512], F32)) for i in range(4)]

        w_landed = [sem(f"w_landed{i}") for i in range(RAW)]
        w_hi_done, w_split, acc_ready, evac_done = sem("w_hi_done"), sem("w_split"), sem("acc_ready"), sem("evac_done")
        const_in, x_landed, gain_T, gains_done, consts_set = (
            sem("const_in"), sem("x_landed"), sem("gain_T"), sem("gains_done"), sem("consts_set"))
        x_T, c_added = sem("x_T"), sem("c_added")
        x_ready, xg_hi, xg_ready = sem("x_ready"), sem("xg_hi"), sem("xg_ready")
        sq_done, norm_sum = sem("sq_done"), sem("norm_sum")
        std_ready, rstd_ready, diag_ready, rbc_ready, r_ready = (
            sem("std_ready"), sem("rstd_ready"), sem("diag_ready"), sem("rbc_ready"), sem("r_ready"))
        h_hi_done, h32_done, h_ready = sem("h_hi_done"), sem("h32_done"), sem("h_ready")
        in_used = sem("in_used")
        y_ready, y_T_done, y_copied, stored = sem("y_ready"), sem("y_T_done"), sem("y_copied"), sem("stored")
        caches_copied = sem("caches_copied")

        def weights_of(t):
            if t.name == "mlp":
                if t.pos % 16 < 8:
                    col = (t.pos // 16 * 8 + t.pos % 16) * P
                    w = aps["mlp_w1"][t.l].rearrange("(k p) n -> p k n", p=P)
                    return w[:, :, bass.ds(t.q * D + col, P)]
                w = aps["mlp_w2"][t.l].rearrange("(f k p) n -> p f k n", p=P, k=KD)
                qq = t.q + t.pos // 16
                return w[:, bass.ds(qq, 1), :, (t.pos % 16 - 8) * P:(t.pos % 16 - 7) * P].rearrange("p f k n -> p (f k) n")
            w = aps[t.name[0] + "_w_" + t.name[2:]][t.l // 3]
            return w.rearrange("(k p) n -> p k n", p=P)[:, :, t.pos * P:(t.pos + 1) * P]

        def sp_weights(sp, t):
            if t.name is None:
                return
            if t.raw_free is not None:
                sp.wait_ge(w_split, t.raw_free)
            sp.dma_start(w_raw[:, t.raw, 0:t.kt, :], weights_of(t)).then_inc(w_landed[t.raw], 16)

        def act_split(act, t):
            if t.name is None:
                return
            act.wait_ge(w_landed[t.raw], t.landed)
            if t.first >= SLOTS - 1:
                act.wait_ge(acc_ready, t.n - 2)
            nc.scalar.activation(w_hi[:, t.slot, 0:t.kt, :], w_raw[:, t.raw, 0:t.kt, :], ACT.Copy).then_inc(w_hi_done, 1)

        def dve_split(dve, t):
            if t.name is None:
                return
            dve.wait_ge(w_hi_done, t.n + 1)
            nc.vector.tensor_tensor(w_lo[:, t.slot, 0:t.kt, :], w_raw[:, t.raw, 0:t.kt, :],
                                    w_hi[:, t.slot, 0:t.kt, :].bitcast(F32), ALU.subtract).then_inc(w_split, 1)

        def pe_tile(pe, t, hi, lo, k_ready=None, between=None, k_used=None):
            pe.wait_ge(w_split, t.n + 1)
            if t.first >= 2:
                pe.wait_ge(evac_done, t.n - 1)
            for k in range(t.kt):
                if k_ready is not None:
                    pe.wait_ge(k_ready[0], k_ready[1] + k + 1)
                if k == 3 and between is not None:
                    between()
                for i, (w, a) in enumerate(((w_hi, hi), (w_hi, lo), (w_lo, hi))):
                    for s in range(2):
                        last = nc.tensor.matmul(acc[:, t.first % 2, s, 0:HALF], w[:, t.slot, k, :],
                                                a[:, k, s * HALF:(s + 1) * HALF],
                                                start=(k == 0 and i == 0), stop=(k == t.kt - 1 and i == 2))
                if k_used is not None and k < KD - 1:
                    last.then_inc(k_used, 1)
            last.then_inc(acc_ready, 1)

        def acc_of(t):
            return acc[:, t.first % 2, :, 0:HALF]

        def halves(ap):
            return ap.rearrange("p (s n) -> p s n", s=2)

        def gain_row(m):
            return m if m == 2 * DEPTH else m // 2 + DEPTH * (m % 2)

        def x_from(m):
            if m == norms[0]:
                return x_ready, 0
            l = layers[(norm_no[m] - 1) // 2]
            if m % 2 == 0:
                return evac_done, base["mlp", l] + 56
            if l % 3 == 2:
                return c_added, 0
            return evac_done, base["ab"[l % 3] + "_out", l]

        def gains_after_mixer(act, l):
            n = [j for j in layers if j % 3 != 2].index(l)
            for k in range(KD):
                if k < KD - 1:
                    act.wait_ge(in_used, (KD - 1) * n + k + 1)
                else:
                    act.wait_ge(evac_done, base["ab"[l % 3] + "_out", l] + KD)
                act_gain(act, 2 * l + 1, k)

        def act_gain(act, m, k):
            act.wait_ge(x_from(m)[0], x_from(m)[1] + k + 1)
            nc.scalar.activation(act_hi[:, k, :], x[:, k, :], ACT.Copy, scale=gains[:, gain_row(m), k:k + 1]).then_inc(xg_hi, 1)

        def dve_gain(dve, m, k):
            dve.wait_ge(xg_hi, 8 * split_no[m] + k + 1)
            nc.vector.scalar_tensor_tensor(act_lo[:, k, :], x[:, k, :], gains[:, gain_row(m), k:k + 1],
                                           act_hi[:, k, :].bitcast(F32), ALU.mult, ALU.subtract).then_inc(xg_ready, 1)

        def pool_sumsq(pool, m, k):
            i = norm_no[m]
            pool.wait_ge(x_from(m)[0], x_from(m)[1] + k + 1)
            if k == 0:
                if i > 0:
                    pool.wait_ge(norm_sum, i)
                nc.gpsimd.tensor_tensor(sumsq[:, :], x[:, 0, :], x[:, 0, :], ALU.mult).then_inc(sq_done, 1)
                return
            n = 15 * i + 2 * k - 1
            pool.wait_ge(sq_done, n)
            nc.gpsimd.tensor_tensor(sq[:, :], x[:, k, :], x[:, k, :], ALU.mult).then_inc(sq_done, 1)
            pool.wait_ge(sq_done, n + 1)
            last = nc.gpsimd.tensor_tensor(sumsq[:, :], sumsq[:, :], sq[:, :], ALU.add)
            last.then_inc(sq_done, 1)

        def pe_norm_sum(pe, m):
            i = norm_no[m]
            pe.wait_ge(sq_done, 15 * (i + 1))
            if i > 0:
                pe.wait_ge(r_ready, i)
            for j in range(QT + 1):
                rows = P if j < QT else NS
                last = nc.tensor.matmul(misc[0][0:rows, j:j + 1], sumsq[:, j * P:j * P + rows], ones[:, 0:1],
                                        start=True, stop=True)
            last.then_inc(norm_sum, 1)

        def act_norm_std(act, m):
            i = norm_no[m]
            act.wait_ge(norm_sum, i + 1)
            if i > 0:
                act.wait_ge(rstd_ready, i)
            nc.scalar.activation(std[:, 0:QT], misc[0][:, 0:QT], ACT.Sqrt, scale=1.0 / D, bias=eps_col[:, 0:1])
            nc.scalar.activation(std[0:NS, QT:QT + 1], misc[0][0:NS, QT:QT + 1], ACT.Sqrt, scale=1.0 / D,
                                 bias=eps_col[0:NS, 0:1]).then_inc(std_ready, 1)

        def dve_norm_diag(dve, m):
            i = norm_no[m]
            dve.wait_ge(std_ready, i + 1)
            nc.vector.reciprocal(rstd[:, :], std[:, :]).then_inc(rstd_ready, 1)
            dve.wait_ge(rstd_ready, i + 1)
            if i > 0:
                dve.wait_ge(rbc_ready, i)
            nc.vector.tensor_tensor(diag[:, :, :], ident[:, :].unsqueeze(1).to_broadcast([P, QT + 1, P]),
                                    rstd[:, :].unsqueeze(2).to_broadcast([P, QT + 1, P]), ALU.mult).then_inc(diag_ready, 1)

        def pe_norm_bcast(pe, m):
            pe.wait_ge(diag_ready, norm_no[m] + 1)
            for j in range(QT):
                nc.tensor.matmul(misc[1][:, j * P:(j + 1) * P], ones[:, :], diag[:, j, :], start=True, stop=True)
            nc.tensor.matmul(misc[0][:, 64:64 + NS], ones[0:NS, :], diag[0:NS, QT, 0:NS], start=True, stop=True).then_inc(rbc_ready, 1)

        def act_norm_R(act, m):
            act.wait_ge(rbc_ready, norm_no[m] + 1)
            nc.scalar.activation(R[:, 0:SEQ], misc[1][:, :], ACT.Copy)
            nc.scalar.activation(R[:, SEQ:TOK], misc[0][:, 64:64 + NS], ACT.Copy).then_inc(r_ready, 1)

        def mlp_positions(eng, step):
            step(0, 0)
            step(1, 0)
            with eng.Fori(0, FQ - 1) as q:
                for p in range(2, 18):
                    step(p, q)
            for p in range(2, 16):
                step(p, FQ - 1)

        def mlp_no(l):
            return l

        def cache_copy(sp, l, p, q):
            c = (p - 2) // 2 if p % 2 == 0 else COPIES - 1 if p == 17 else None
            if c is None:
                return
            a, b = mlp_no(l) // 2, DEC_B // 2 * (mlp_no(l) % 2) + q
            g, first, rows = COPY_PIECES[c]
            old = aps[f"cache_a_kv{g}"][a].rearrange("b l s h d -> b l (s h d)")
            new = aps[f"new_a_kv{g}_s"][a].rearrange("b l s h d -> b l (s h d)")
            sp.dma_start(new[bass.ds(b, 1), first:first + rows, :],
                         old[bass.ds(b, 1), first + DEC_T:first + DEC_T + rows, :]).then_inc(caches_copied, 16)

        def sp_mlp(sp, l):
            def step(p, q):
                sp_weights(sp, WeightTile("mlp", l, p, q))
                cache_copy(sp, l, p, q)
            with sp.Fori(0, FQ - 1) as q:
                for p in range(2, 18):
                    step(p, q)
            for p in range(2, 18):
                step(p, FQ - 1)

        def h_count(l, p, q):
            return 32 * mlp_no(l) + 8 * q + (p // 16) * 8 + p % 16

        def pe_mlp(pe, l):
            m = 2 * l + 1

            def step(p, q):
                t = WeightTile("mlp", l, p, q)
                if p % 16 < 8:
                    first = p == 0 and isinstance(q, int)
                    between = (lambda: pe_norm_bcast(pe, m)) if p == 1 and isinstance(q, int) else None
                    pe_tile(pe, t, act_hi, act_lo, k_ready=(xg_ready, 8 * split_no[m]) if first else None, between=between)
                    if first:
                        pe_norm_sum(pe, m)
                else:
                    pe_tile(pe, t, h_hi, h_lo, k_ready=(h_ready, 32 * mlp_no(l) + 8 * q) if p == 8 else None)
            mlp_positions(pe, step)

        def act_mlp(act, l, m_next):
            m = 2 * l + 1

            def step(p, q):
                act_split(act, WeightTile("mlp", l, p + 2, q))
                t = WeightTile("mlp", l, p, q)
                if p == 0 and isinstance(q, int):
                    act_norm_std(act, m)
                    act_norm_R(act, m)
                if p % 16 < 8:
                    act.wait_ge(evac_done, t.n + 1)
                    nc.scalar.activation(h_hi[:, p % 16, :], relu_t[:, p % 2, :], ACT.Square).then_inc(h_hi_done, 1)
                elif isinstance(q, int) and m_next in split_norms:
                    act_gain(act, m_next, p % 16 - 8)
            mlp_positions(act, step)

        def dve_mlp(dve, l, m_next):
            m = 2 * l + 1

            def step(p, q):
                dve_split(dve, WeightTile("mlp", l, p + 2, q))
                t = WeightTile("mlp", l, p, q)
                if p == 0 and isinstance(q, int):
                    dve_norm_diag(dve, m)
                    dve.wait_ge(r_ready, norm_no[m] + 1)
                dve.wait_ge(acc_ready, t.n + 1)
                if p % 16 < 8:
                    if mlp_no(l) or p >= 2:
                        dve.wait_ge(h_ready, h_count(l, p, q) - 1)
                    nc.vector.scalar_tensor_tensor(halves(relu_t[:, p % 2, :]), acc_of(t), 0.0, halves(R[:, :]),
                                                   ALU.max, ALU.mult).then_inc(evac_done, 1)
                    return
                k = p % 16 - 8
                nc.vector.tensor_tensor(halves(x[:, k, :]), acc_of(t), halves(x[:, k, :]), ALU.add).then_inc(evac_done, 1)
                if isinstance(q, int) and m_next in split_norms:
                    dve_gain(dve, m_next, k)
            mlp_positions(dve, step)

        def pool_mlp(pool, l, m_next):
            def step(p, q):
                t = WeightTile("mlp", l, p, q)
                if p % 16 < 8:
                    n = h_count(l, p, q)
                    pool.wait_ge(evac_done, t.n + 1)
                    if mlp_no(l) or p >= 2:
                        pool.wait_ge(h_ready, n - 1)
                    nc.gpsimd.tensor_tensor(h32[:, p % 2, :], relu_t[:, p % 2, :], relu_t[:, p % 2, :], ALU.mult).then_inc(h32_done, 1)
                    pool.wait_ge(h32_done, n + 1)
                    pool.wait_ge(h_hi_done, n + 1)
                    nc.gpsimd.tensor_tensor(h_lo[:, p % 16, :], h32[:, p % 2, :], h_hi[:, p % 16, :].bitcast(F32),
                                            ALU.subtract).then_inc(h_ready, 1)
                elif isinstance(q, int):
                    pool_sumsq(pool, m_next, p % 16 - 8)
            mlp_positions(pool, step)

        mixers = {}
        dve_steps, act_steps, pool_steps = sem("dve_steps"), sem("act_steps"), sem("pool_steps")
        c_stored = sem("c_stored")
        steps = {"dve": 0, "act": 0, "pool": 0}

        def chain(eng, ins, name="dve"):
            s = {"dve": dve_steps, "act": act_steps, "pool": pool_steps}[name]
            ins.then_inc(s, 1)
            steps[name] += 1
            eng.wait_ge(s, steps[name])

        def lsb(name, shape, dt=F32):
            return local.enter_context(nc.sbuf_tensor(name, shape, dt))

        def place_free(eng, l):
            if l == layers[0]:
                eng.wait_ge(x_T, KD)
                eng.wait_ge(x_ready, KD)
            else:
                eng.wait_ge(evac_done, base["mlp", l - 1] + 64)

        WINDOWS = (2, 4, 8, 16)
        PRE = 15
        CP = PRE + SEQ
        CS = PRE + DEC_T
        CW = CP + DEC_B * CS
        PREV_ROWS = DEC_B * PRE
        TAIL = PRE + NS
        with ExitStack() as local:
            c_x = lsb("c_x", [P, KD, CW])
            c_sum = lsb("c_sum", [P, 2, CW])
            c_d = lsb("c_d", [P, 2, TOK])
            c_w_raw = lsb("c_w_raw", [P, KD, 256])
            c_w_hi = lsb("c_w_hi", [P, KD, 256], F32R)
            c_w_lo = lsb("c_w_lo", [P, KD, 256], F32R)
            c_prev = lsb("c_prev", [PREV_ROWS, D])
            c_inv = lsb("c_inv", [P, len(WINDOWS), 16])
            c_tail = lsb("c_tail", [TAIL, D])
        c_landed, c_zero, c_prev_T, c_prev_done = sem("c_landed"), sem("c_zero"), sem("c_prev_T"), sem("c_prev_done")
        c_h, c_wh, c_d_done, c_d_hi, c_d_ready, c_w_ready = (sem("c_h"), sem("c_wh"), sem("c_d_done"), sem("c_d_hi"),
                                                             sem("c_d_ready"), sem("c_w_ready"))
        c_y, c_tail_T, c_tail_done = sem("c_y"), sem("c_tail_T"), sem("c_tail_done")

        class MixC:

            @staticmethod
            def sp(sp, l):
                place_free(sp, l)
                sp.dma_start(c_prev[:, :], aps["state_c_pool"][0].rearrange("b j d -> (b j) d")).then_inc(c_landed, 16)
                sp.dma_start(c_inv[:, :, :], aps["c_pool_inv"]).then_inc(c_landed, 16)
                sp.dma_start(c_w_raw[:, :, :], aps["c_w"][0].rearrange("g (k p) e -> p (g k) e", p=P)).then_inc(c_landed, 16)
                sp.dma_start(aps["new_c_pool_s"][0, :, 0:PRE - DEC_T, :], aps["state_c_pool"][0, :, DEC_T:PRE, :]).then_inc(c_stored, 16)
                sp.wait_ge(c_tail_done, 2)
                sp.dma_start(aps["new_c_pool_p"][0, 0], c_tail[0:PRE, :]).then_inc(c_stored, 16)
                for b in range(DEC_B):
                    sp.dma_start(aps["new_c_pool_s"][0, b, PRE - DEC_T:PRE, :],
                                 c_tail[PRE + b * DEC_T:PRE + (b + 1) * DEC_T, :]).then_inc(c_stored, 16)
                sp.wait_ge(c_stored, 16 * (2 + DEC_B))

            @staticmethod
            def pool(pool, l):
                place_free(pool, l)
                nc.gpsimd.memset(c_x[:, :, 0:PRE], 0.0).then_inc(c_zero, 1)
                nc.gpsimd.memset(c_sum[:, :, 0:PRE + 1], 0.0).then_inc(c_zero, 1)
                for k in range(KD):
                    pool_sumsq(pool, 2 * l + 1, k)

            @staticmethod
            def pe(pe, l):
                pe_norm_sum(pe, 2 * l)
                pe.wait_ge(c_landed, 48)
                for k in range(KD):
                    place_free(pe, l)
                    nc.tensor.transpose(acc[:, k // 4, 0, (k % 4) * P:(k % 4) * P + PREV_ROWS], c_prev[:, k * P:(k + 1) * P],
                                        ident[0:PREV_ROWS, 0:PREV_ROWS]).then_inc(c_prev_T, 1)
                pe_norm_bcast(pe, 2 * l)

                def products(g):
                    if g == 0:
                        pe.wait_ge(c_w_ready, KD)
                        pe.wait_ge(c_prev_done, KD)
                    for o in (2 * g, 2 * g + 1):
                        if o >= 2:
                            pe.wait_ge(c_added, o - 1)
                        for k in (2 * g, 2 * g + 1):
                            pe.wait_ge(c_d_ready, k + 1)
                            for i, (w, a) in enumerate(((c_w_hi, act_hi), (c_w_hi, act_lo), (c_w_lo, act_hi))):
                                for s in range(2):
                                    last = nc.tensor.matmul(acc[:, (base["mlp", l] + o) % 2, s, 0:HALF], w[:, k, (o % 2) * P:(o % 2 + 1) * P],
                                                            a[:, k, s * HALF:(s + 1) * HALF],
                                                            start=(k == 2 * g and i == 0), stop=(k == 2 * g + 1 and i == 2))
                        last.then_inc(c_y, 1)

                for k in range(KD):
                    pe.wait_ge(c_h, k + 1)
                    nc.tensor.transpose(misc[2 + k // 4][0:TAIL, (k % 4) * P:(k % 4 + 1) * P],
                                        c_d[:, k % 2, 0:TAIL], ident[:, :]).then_inc(c_tail_T, 1)
                    if k % 2:
                        products(k // 2)
                pe.wait_ge(c_added, KD - 1)

            @staticmethod
            def act(act, l):
                act_norm_std(act, 2 * l)
                act.wait_ge(c_landed, 48)
                for k in range(KD):
                    act.wait_ge(c_prev_T, 4 * (k // 4) + 4)
                    nc.scalar.activation(c_x[:, k, CP:].rearrange("p (b j) -> p b j", j=CS)[:, :, 0:PRE],
                                         acc[:, k // 4, 0, (k % 4) * P:(k % 4) * P + PREV_ROWS].rearrange("p (b j) -> p b j", j=PRE),
                                         ACT.Copy).then_inc(c_prev_done, 1)
                act_norm_R(act, 2 * l)
                for k in range(KD):
                    nc.scalar.activation(c_w_hi[:, k, :], c_w_raw[:, k, :], ACT.Copy).then_inc(c_wh, 1)

                def gains_of(first):
                    for k in (first, first + 1):
                        act.wait_ge(c_y, first + 2)
                        act_gain(act, 2 * l + 1, k)

                for k in range(KD):
                    act.wait_ge(c_d_done, k + 1)
                    nc.scalar.activation(act_hi[:, k, :], c_d[:, k % 2, :], ACT.Copy).then_inc(c_d_hi, 1)
                    if k % 2 == 0 and k:
                        gains_of(k - 2)
                for half in range(2):
                    act.wait_ge(c_tail_T, 4 * half + 4)
                    nc.scalar.activation(c_tail[:, half * 512:(half + 1) * 512], misc[2 + half][0:TAIL, :], ACT.Copy).then_inc(c_tail_done, 1)
                gains_of(KD - 2)

            @staticmethod
            def dve(dve, l):
                dve_norm_diag(dve, 2 * l)
                dve.wait_ge(r_ready, norm_no[2 * l] + 1)
                dve.wait_ge(c_zero, 2)
                dve.wait_ge(c_prev_done, KD)
                row = gain_row(2 * l)

                def add_to_x(first):
                    for o in (first, first + 1):
                        dve.wait_ge(c_y, o + 1)
                        nc.vector.scalar_tensor_tensor(halves(x[:, o, :]), acc[:, (base["mlp", l] + o) % 2, :, 0:HALF],
                                                       gains[:, 2 * DEPTH + 1, o:o + 1], halves(x[:, o, :]), ALU.mult, ALU.add).then_inc(c_added, 1)

                for k in range(KD):
                    g, b = k // 2, k % 2
                    cur = c_x[:, k, :]
                    if k >= 2:
                        dve.wait_ge(c_d_ready, k - 1)
                    nc.vector.scalar_tensor_tensor(cur[:, PRE:CP], x[:, k, 0:SEQ], gains[:, row, k:k + 1], R[:, 0:SEQ],
                                                   ALU.mult, ALU.mult)
                    chain(dve, nc.vector.scalar_tensor_tensor(
                        cur[:, CP:].rearrange("p (b j) -> p b j", j=CS)[:, :, PRE:], x[:, k, SEQ:TOK].rearrange("p (b t) -> p b t", t=DEC_T),
                        gains[:, row, k:k + 1], R[:, SEQ:TOK].rearrange("p (b t) -> p b t", t=DEC_T), ALU.mult, ALU.mult))
                    nc.vector.tensor_copy(c_d[:, b, 0:PRE], cur[:, CP - PRE:CP])
                    nc.vector.tensor_copy(c_d[:, b, PRE:TAIL].rearrange("p (b t) -> p b t", t=DEC_T),
                                          cur[:, CP:].rearrange("p (b j) -> p b j", j=CS)[:, :, PRE:]).then_inc(c_h, 1)
                    src = cur
                    for i in range(g + 1):
                        step = 1 << i
                        dst = c_sum[:, i % 2, :]
                        chain(dve, nc.vector.tensor_tensor(dst[:, 2 * step - 1:CW], src[:, 2 * step - 1:CW],
                                                           src[:, step - 1:CW - step], ALU.add))
                        src = dst
                    dve.wait_ge(c_tail_T, k + 1)
                    w = WINDOWS[g]
                    nc.vector.scalar_tensor_tensor(c_d[:, b, 16:SEQ], src[:, PRE + 16:CP], 1.0 / w, cur[:, PRE + 16:CP],
                                                   ALU.mult, ALU.subtract)
                    nc.vector.scalar_tensor_tensor(c_d[:, b, SEQ:TOK].rearrange("p (b t) -> p b t", t=DEC_T),
                                                   src[:, CP:].rearrange("p (b j) -> p b j", j=CS)[:, :, PRE:], 1.0 / w,
                                                   cur[:, CP:].rearrange("p (b j) -> p b j", j=CS)[:, :, PRE:], ALU.mult, ALU.subtract)
                    chain(dve, nc.vector.tensor_tensor(c_d[:, b, 0:16], src[:, PRE:PRE + 16], c_inv[:, g, :], ALU.mult))
                    nc.vector.tensor_tensor(c_d[:, b, 0:16], c_d[:, b, 0:16], cur[:, PRE:PRE + 16], ALU.subtract).then_inc(c_d_done, 1)
                    if k == 0:
                        for j in range(KD):
                            dve.wait_ge(c_wh, j + 1)
                            nc.vector.tensor_tensor(c_w_lo[:, j, :], c_w_raw[:, j, :], c_w_hi[:, j, :].bitcast(F32), ALU.subtract).then_inc(c_w_ready, 1)
                    dve.wait_ge(c_d_hi, k + 1)
                    nc.vector.tensor_tensor(act_lo[:, k, :], c_d[:, b, :], act_hi[:, k, :].bitcast(F32), ALU.subtract).then_inc(c_d_ready, 1)
                    if k % 2 == 0 and k:
                        add_to_x(k - 2)
                    elif k >= 3:
                        for j in (k - 3, k - 2):
                            dve_gain(dve, 2 * l + 1, j)
                add_to_x(KD - 2)
                for k in (KD - 2, KD - 1):
                    dve_gain(dve, 2 * l + 1, k)

        mixers[2] = MixC

        NG, HG, HD = 3, 6, 64
        PAIRS = HG // 2
        GW = HG * HD
        FT = NG * PAIRS
        A_TILES = 3 * PAIRS
        CACHE = (128, 512, 512)
        SCALE = HD ** -0.5
        BATCH = DEC_B // 2
        S_OFF, S_LEN = (0, 160, 704), (128, 512, 128)
        S_ALL = 864
        with ExitStack() as local:
            a_o = lsb("a_o", [P, NG, QT, GW])
            a_qbd = lsb("a_qbd", [P, FT, DEC_B, 32])
            a_kn = lsb("a_kn", [P, FT, NS])
            a_vn = lsb("a_vn", [NS, NG, GW])
            a_st = lsb("a_st", [P, NG, QT, 2 * HG])
            a_stx0 = lsb("a_stx0", [P, QT, 2 * HG])
            a_stx1 = lsb("a_stx1", [P, QT, 4 * HG])
            a_e = lsb("a_e", [P, 3, NG, QT * HG])
            a_t = lsb("a_t", [P, 3, QT * HG])
            a_f = lsb("a_f", [P, 3, NG, QT * HG])
            a_sst = lsb("a_sst", [P, 2, NG, 2])
            with ExitStack() as local:
                a_qk = lsb("a_qk", [P, 2 * PAIRS, TOK])
                a_v = lsb("a_v", [P, PAIRS, TOK])
                a_vtok = lsb("a_vtok", [P, QT, GW])
                a_ktok = lsb("a_ktok", [P, QT + 1, GW])
                a_cos = lsb("a_cos", [P, TOK])
                a_sin = lsb("a_sin", [P, TOK])
                a_sw = lsb("a_sw", [P, TOK])
                a_rc = lsb("a_rc", [P, TOK])
                a_p = lsb("a_p", [P, 2, QT, 2 * P])
                a_pt = lsb("a_pt", [P, 2, QT, P])
                a_mask = lsb("a_mask", [P, 3, P])
            with ExitStack() as local:
                s_kT = lsb("s_kT", [P, 2, PAIRS, 512])
                s_p = lsb("s_p", [P, 2, S_ALL])
                s_pt = lsb("s_pt", [P, 2, 9, P])
                s_mask = lsb("s_mask", [P, 2, S_ALL])
        s_kv = work["s_kv"]
        a_landed, a_zero, a_swapped, a_rope = sem("a_landed"), sem("a_zero"), sem("a_swapped"), sem("a_rope")
        a_kT, a_vT, a_kcopy, a_vcopy = sem("a_kT"), sem("a_vT"), sem("a_kcopy"), sem("a_vcopy")
        a_kout, a_vout, a_nout = sem("a_kout"), sem("a_vout"), sem("a_nout")
        a_scores, a_masked, a_nb, a_probs, a_ptT, a_ptc, a_pv, a_ocopy = (
            sem("a_scores"), sem("a_masked"), sem("a_nb"), sem("a_probs"), sem("a_ptT"), sem("a_ptc"), sem("a_pv"), sem("a_ocopy"))
        a_qcopy, a_bounce, a_back = sem("a_qcopy"), sem("a_bounce"), sem("a_back")
        a_dif, a_exp, a_scaled, a_oT, a_ohi, a_olo = sem("a_dif"), sem("a_exp"), sem("a_scaled"), sem("a_oT"), sem("a_ohi"), sem("a_olo")
        s_landed = [sem(f"s_landed{i}") for i in range(KV_SLOTS)]
        s_kTp, s_kTc, s_unit, s_masked, s_nb, s_probs, s_pscaled = (
            sem("s_kTp"), sem("s_kTc"), sem("s_unit"), sem("s_masked"), sem("s_nb"), sem("s_probs"), sem("s_pscaled"))
        s_ptT, s_ptc, s_oc, s_oT, s_hi, s_lo = sem("s_ptT"), sem("s_ptc"), sem("s_oc"), sem("s_oT"), sem("s_hi"), sem("s_lo")

        a_layers = [l for l in layers if l % 3 == 0]
        K_ITEMS = [(g, b) for g in range(NG) for b in range(QT + 1) if g > 0 or b >= QT - 1]
        def units_of(g, batch):
            bs = list(range(BATCH * batch, BATCH * (batch + 1)))
            return [(g, batch, [b]) for b in bs] if g == 1 else [(g, batch, bs)]
        K_UNITS = [u for g in range(NG) for batch in range(2) for u in units_of(g, batch)]
        V_UNITS = [u for batch in range(2) for g in range(NG) for u in units_of(g, batch)]
        S_ITEMS = [(batch, g) for batch in range(2) for g in range(NG)]
        UNITS = [(0, u) for u in K_UNITS] + [(1, u) for u in V_UNITS]
        unit_landed, landed_count = {}, [0] * KV_SLOTS
        for n in range(len(a_layers)):
            for i, (_, u) in enumerate(UNITS):
                landed_count[i % KV_SLOTS] += 64 if u[0] == 2 else 16
                unit_landed[n, i] = landed_count[i % KV_SLOTS]
        scratch0 = nc.dram_tensor("scratch0", [2, SEQ, 2 * HG], F32, kind="Internal").ap()
        scratch1 = nc.dram_tensor("scratch1", [2, SEQ, 4 * HG], F32, kind="Internal").ap()

        def cols(g, b):
            if b == QT:
                return slice(SEQ, TOK)
            return slice(b * P, (b + 1) * P) if g == 0 else slice(b, SEQ, QT)

        def a_no(l):
            return a_layers.index(l)

        class MixA:

            @staticmethod
            def sp(sp, l):
                a, n = l // 3, a_no(l)
                place_free(sp, l)
                sp.dma_start(a_cos[:, :], aps["c_cos"]).then_inc(a_landed, 16)
                sp.dma_start(a_sin[:, :], aps["c_sin"]).then_inc(a_landed, 16)
                sp.dma_start(a_mask[:, :, :], aps["c_mask"]).then_inc(a_landed, 16)
                for g in range(NG):
                    for p in range(A_TILES * g + 2, A_TILES * (g + 1) + 2):
                        sp_weights(sp, WeightTile("a_in", l, p))
                    new_p, new_s = aps[f"new_a_kv{g + 1}_p"], aps[f"new_a_kv{g + 1}_s"]
                    L = CACHE[g]
                    for b in range(QT + 1):
                        rows = P if b < QT else NS
                        if b == QT:
                            dst = new_s[a, :, L - DEC_T:L].rearrange("b t c h d -> b t c (h d)")
                        elif g == 0:
                            dst = new_p[a, 0].rearrange("i c h d -> i c (h d)")
                        else:
                            dst = new_p[a, 0].rearrange("(i r) c h d -> r i c (h d)", r=QT)[b]
                        if (g, b) in K_ITEMS:
                            i = K_ITEMS.index((g, b))
                            sp.wait_ge(a_kcopy, n * len(K_ITEMS) + i + 1)
                            if b < QT:
                                sp.dma_start(dst[:, 0, :], a_ktok[:, b, :]).then_inc(a_kout, 16)
                            else:
                                for s in range(DEC_B):
                                    sp.dma_start(dst[s, :, 0, :], a_ktok[s * DEC_T:(s + 1) * DEC_T, b, :]).then_inc(a_kout, 16)
                        sp.wait_ge(a_vcopy, 5 * (3 * n + g) + b + 1)
                        if b == QT:
                            for s in range(DEC_B):
                                sp.dma_start(dst[s, :, 1, :], a_vn[s * DEC_T:(s + 1) * DEC_T, g, :]).then_inc(a_nout, 16)
                        elif g > 0 or b == QT - 1:
                            sp.dma_start(dst[:, 1, :], a_vtok[:, b, :]).then_inc(a_vout, 16)
                sp.wait_ge(a_ocopy, 18 * (n + 1))
                sp.wait_ge(a_vout, 16 * 9 * (n + 1))
                sp.wait_ge(a_kout, K_OUT[NG] * (n + 1))
                sp.dma_start(s_mask[:, :, :], aps["c_smask"]).then_inc(a_landed, 16)
                sp.wait_ge(a_probs, 18 * (n + 1))
                sp.dma_start(scratch0[a].rearrange("(b p) c -> p b c", p=P), a_st[:, 0, :, :]).then_inc(a_bounce, 16)
                for g in (1, 2):
                    sp.dma_start(scratch1[a].rearrange("(i r) c -> i r c", r=QT)[:, :, (g - 1) * 12:g * 12], a_st[:, g, :, :]).then_inc(a_bounce, 16)
                sp.wait_ge(a_bounce, 48 * (n + 1))
                sp.dma_start(a_stx0[:, :, :], scratch0[a].rearrange("(i r) c -> i r c", r=QT)).then_inc(a_back, 16)
                sp.dma_start(a_stx1[:, :, :], scratch1[a].rearrange("(b p) c -> p b c", p=P)).then_inc(a_back, 16)
                for p in range(2, 10):
                    sp_weights(sp, WeightTile("a_out", l, p))
                sp.wait_ge(a_nout, 16 * 3 * DEC_B * (n + 1))

            @staticmethod
            def pool(pool, l):
                a, n = l // 3, a_no(l)
                place_free(pool, l)
                nc.gpsimd.memset(a_qbd[:, :, :, :], 0.0).then_inc(a_zero, 1)
                nc.gpsimd.memset(a_p[:, :, 0, 0:P], -1e30).then_inc(a_zero, 1)
                pool.wait_ge(evac_done, base["a_in", l] + NG * A_TILES)
                for i, (kv, (g, batch, bs)) in enumerate(UNITS):
                    if i >= KV_SLOTS:
                        pool.wait_ge(s_unit, n * len(UNITS) + i - KV_SLOTS + 1)
                    cache = aps[f"cache_a_kv{g + 1}"][a]
                    dst, landed = s_kv[:, i % KV_SLOTS, :, :], s_landed[i % KV_SLOTS]
                    if g == 0:
                        pool.dma_start(dst, cache[bs[0]:bs[-1] + 1, :, kv].rearrange("b k h d -> k b (h d)")).then_inc(landed, 16)
                    elif g == 1:
                        pool.dma_start(dst, cache[bs[0], :, kv].rearrange("(p j) h d -> p j (h d)", j=4)).then_inc(landed, 16)
                    else:
                        src = cache[bs[0]:bs[-1] + 1, :, kv].rearrange("b (k r) h d -> r k b (h d)", r=16)
                        for r in range(DEC_T):
                            pool.dma_start(dst[32 * r:32 * r + 32], src[r]).then_inc(landed, 16)
                for k in range(KD):
                    pool_sumsq(pool, 2 * l + 1, k)

            @staticmethod
            def pe(pe, l):
                n, m = a_no(l), 2 * l
                for g in range(NG):
                    G = 3 * n + g
                    for j in range(A_TILES):
                        t = WeightTile("a_in", l, A_TILES * g + j)
                        first = t.pos == 0
                        pe_tile(pe, t, act_hi, act_lo, k_ready=(xg_ready, 8 * split_no[m]) if first else None,
                                between=(lambda: pe_norm_bcast(pe, m)) if t.pos == 1 else None)
                        if first:
                            pe_norm_sum(pe, m)
                    pe.wait_ge(evac_done, base["a_in", l] + A_TILES * (g + 1))
                    pe.wait_ge(a_rope, 6 * (G + 1))
                    for b in range(QT + 1):
                        rows = P if b < QT else NS
                        if (g, b) in K_ITEMS:
                            i = K_ITEMS.index((g, b))
                            if i + n * len(K_ITEMS) >= 2:
                                pe.wait_ge(a_kcopy, n * len(K_ITEMS) + i - 1)
                            for p in range(PAIRS):
                                last = nc.tensor.transpose(acc[0:rows, i % 2, 0, p * P:(p + 1) * P], a_qk[:, PAIRS + p, cols(g, b)], ident[:, :])
                            last.then_inc(a_kT, 1)
                        v = 5 * G + b
                        if v >= 2:
                            pe.wait_ge(a_vcopy, v - 1)
                        for p in range(PAIRS):
                            last = nc.tensor.transpose(acc[0:rows, v % 2, 1, p * P:(p + 1) * P], a_v[:, p, cols(g, b)], ident[:, :])
                        last.then_inc(a_vT, 1)
                    pe.wait_ge(a_kcopy, n * len(K_ITEMS) + K_ITEMS.index((g, QT)) + 1)
                    pe.wait_ge(a_vcopy, 5 * (G + 1))

                    def scores(h):
                        H = 6 * G + h
                        r = slice((h % 2) * HD, (h % 2 + 1) * HD)
                        if h >= 2:
                            pe.wait_ge(a_masked, H - 1)
                        for b in range(QT):
                            last = nc.tensor.matmul(acc[:, h % 2, 0, b * P:(b + 1) * P], a_qk[r, h // 2, cols(g, b)],
                                                    a_qk[r, PAIRS + h // 2, cols(g, b)], start=True, stop=True)
                        if g == 0:
                            for b in range(1, QT):
                                last = nc.tensor.matmul(acc[:, h % 2, 1, b * P:(b + 1) * P], a_qk[r, h // 2, cols(g, b)],
                                                        a_qk[r, PAIRS + h // 2, cols(g, b - 1)], start=True, stop=True)
                        last.then_inc(a_scores, 1)

                    def turn(h):
                        H = 6 * G + h
                        pe.wait_ge(a_probs, H + 1)
                        if H >= 1:
                            pe.wait_ge(a_ptc, H)
                        for b in range(QT):
                            last = nc.tensor.transpose(misc[2][:, b * P:(b + 1) * P], a_p[:, h % 2, b, P:2 * P], ident[:, :])
                        if g == 0:
                            for b in range(1, QT):
                                last = nc.tensor.transpose(misc[3][:, b * P:(b + 1) * P], a_p[:, h % 2, b, 0:P], ident[:, :])
                        last.then_inc(a_ptT, 1)

                    def values(h):
                        H = 6 * G + h
                        pe.wait_ge(a_ptc, H + 1)
                        if H >= 2:
                            pe.wait_ge(a_ocopy, H - 1)
                        hc = slice(h * HD, (h + 1) * HD)
                        for b in range(QT):
                            prev = g == 0 and b > 0
                            out = misc[h % 2][:, b * HD:(b + 1) * HD]
                            if prev:
                                nc.tensor.matmul(out, a_pt[:, 1, b, :], a_vtok[:, b - 1, hc], start=True, stop=False)
                            last = nc.tensor.matmul(out, a_pt[:, 0, b, :], a_vtok[:, b, hc], start=not prev, stop=True)
                        last.then_inc(a_pv, 1)

                    for i in range(HG + 2):
                        if i < HG:
                            scores(i)
                        if 1 <= i <= HG:
                            turn(i - 1)
                        if i >= 2:
                            values(i - 2)
                pe.wait_ge(a_qcopy, 7 * 3 * (n + 1))
                pe.wait_ge(a_ocopy, 18 * (n + 1))
                pe.wait_ge(a_zero, 2 * (n + 1))

                def unit_wait(i):
                    pe.wait_ge(s_landed[i % KV_SLOTS], unit_landed[n, i])

                def turn_keys(i):
                    unit_wait(i)
                    if i + n >= 1:
                        pe.wait_ge(s_kTc, 3 * (12 * n + i))
                    for p in range(PAIRS):
                        for j in range(4):
                            last = nc.tensor.transpose(misc[1 + p][:, j * P:(j + 1) * P], s_kv[:, i % KV_SLOTS, j, p * P:(p + 1) * P], ident[:, :])
                        last.then_inc(s_kTp, 1)

                def sample_scores(i):
                    g, batch, bs = K_UNITS[i]
                    pe.wait_ge(s_kTc, 3 * (12 * n + i + 1))
                    k = 2 * g + batch
                    if bs[0] == BATCH * batch and g > 0:
                        pe.wait_ge(s_masked, 6 * n + k - 1)
                    for b in bs:
                        rows = slice(32 * (b % BATCH), 32 * (b % BATCH) + 32)
                        keys = slice(0, 512) if g == 1 else slice((b % BATCH) * P, (b % BATCH + 1) * P)
                        for p in range(PAIRS):
                            nc.tensor.matmul(acc[rows, batch, 0, 0:S_LEN[g]], a_qbd[:, 3 * g + p, b, :], s_kT[:, i % 2, p, keys],
                                             start=(p == 0), stop=(p == PAIRS - 1))
                        for p in range(PAIRS):
                            last = nc.tensor.matmul(acc[rows, batch, 1, 0:NS], a_qbd[:, 3 * g + p, b, :], a_kn[:, 3 * g + p, :],
                                                    start=(p == 0), stop=(p == PAIRS - 1))
                    last.then_inc(s_unit, 1)

                turn_keys(0)
                for i in range(12):
                    if i < 11:
                        turn_keys(i + 1)
                    sample_scores(i)
                for batch in range(2):
                    pe.wait_ge(s_pscaled, 2 * n + batch + 1)
                    if batch + n:
                        pe.wait_ge(s_ptc, 2 * n + batch)
                    if batch == 0:
                        pe.wait_ge(s_kTc, 36 * (n + 1))
                    starts = [0] + [S_OFF[1] + j * P for j in range(4)] + [S_OFF[2]]
                    for j, c in enumerate(starts):
                        nc.tensor.transpose(misc[1 + j // 4][:, (j % 4) * P:(j % 4 + 1) * P], s_p[:, batch, c:c + P], ident[:, :])
                    for g in range(NG):
                        j = 6 + g
                        c = S_OFF[g] + S_LEN[g]
                        last = nc.tensor.transpose(misc[1 + j // 4][0:NS, (j % 4) * P:(j % 4 + 1) * P], s_p[:, batch, c:c + NS], ident[:, :])
                    last.then_inc(s_ptT, 1)
                for i, (g, batch, bs) in enumerate(V_UNITS):
                    unit_wait(12 + i)
                    pe.wait_ge(s_ptc, 2 * n + batch + 1)
                    if bs[0] == BATCH * batch:
                        nc.tensor.matmul(sample_bank(batch, g)[:, 0:GW], s_pt[0:NS, batch, 6 + g, :], a_vn[0:NS, g, :], start=True, stop=False)
                    for b in bs:
                        rows = slice(32 * (b % BATCH), 32 * (b % BATCH) + 32)
                        tiles = [(j, 1 + j) for j in range(4)] if g == 1 else [(b % BATCH, 0 if g == 0 else 5)]
                        for q, (src, pt) in enumerate(tiles):
                            last = nc.tensor.matmul(sample_bank(batch, g)[rows, 0:GW], s_pt[:, batch, pt, rows],
                                                    s_kv[:, (12 + i) % KV_SLOTS, src, :], start=False, stop=(q == len(tiles) - 1))
                    last.then_inc(s_unit, 1)
                for i, (batch, g) in enumerate(S_ITEMS):
                    pe.wait_ge(s_oc, 6 * n + i + 1)
                    if i >= 2:
                        pe.wait_ge(s_lo, 12 * n + 2 * i - 2)
                    for p in range(PAIRS):
                        last = nc.tensor.transpose(misc[2 + i % 2][:, p * P:(p + 1) * P], s_kT[:, batch, g, p * P:(p + 1) * P], ident[:, :])
                    last.then_inc(s_oT, 1)
                for f in range(FT):
                    pe.wait_ge(a_scaled, 3 * n + f // 3 + 1)
                    if f >= 2:
                        pe.wait_ge(a_olo, 9 * n + f - 1)
                    for b in range(QT):
                        last = nc.tensor.transpose(misc[f % 2][:, b * P:(b + 1) * P], a_o[:, f // 3, b, (f % 3) * P:(f % 3 + 1) * P], ident[:, :])
                    last.then_inc(a_oT, 1)
                pe.wait_ge(a_olo, 9 * (n + 1))
                pe.wait_ge(s_lo, 12 * (n + 1))
                for o in range(KD):
                    pe_tile(pe, WeightTile("a_out", l, o), act_hi, act_lo, k_used=in_used if o == KD - 1 else None)

            @staticmethod
            def act(act, l):
                n, m = a_no(l), 2 * l
                for g in range(NG):
                    G = 3 * n + g
                    for j in range(A_TILES):
                        t = WeightTile("a_in", l, A_TILES * g + j)
                        act_split(act, WeightTile("a_in", l, t.pos + 2))
                        if t.pos == 0:
                            act_norm_std(act, m)
                            act_norm_R(act, m)
                        if j < 2 * PAIRS:
                            act.wait_ge(acc_ready, t.n + 1)
                            if t.n >= 1:
                                act.wait_ge(evac_done, t.n)
                            for q in range(4):
                                last = nc.scalar.activation(halves(a_sw[32 * (q ^ 1):32 * (q ^ 1) + 32, :]),
                                                            acc[32 * q:32 * q + 32, t.first % 2, :, 0:HALF], ACT.Copy)
                            last.then_inc(a_swapped, 1)
                    for b in range(QT + 1):
                        if (g, b) not in K_ITEMS:
                            continue
                        i = K_ITEMS.index((g, b))
                        rows = P if b < QT else NS
                        act.wait_ge(a_kT, n * len(K_ITEMS) + i + 1)
                        if G > 0 and i == K_ITEMS.index(next(item for item in K_ITEMS if item[0] == g)):
                            act.wait_ge(a_kout, K_OUT[g] + K_OUT[NG] * n)
                        nc.scalar.activation(a_ktok[0:rows, b, :], acc[0:rows, i % 2, 0, 0:GW], ACT.Copy).then_inc(a_kcopy, 1)
                    for i in range(HG + 1):
                        H = 6 * G + i
                        if i < HG:
                            act.wait_ge(a_nb, H + 1)
                            for b in range(QT):
                                lo = 0 if g == 0 and b > 0 else P
                                last = nc.scalar.activation(a_p[:, i % 2, b, lo:2 * P], a_p[:, i % 2, b, lo:2 * P], ACT.Exp, scale=SCALE,
                                                            bias=a_st[:, g, b, i:i + 1], accum_out=a_st[:, g, b, HG + i:HG + i + 1])
                            last.then_inc(a_probs, 1)
                        if i >= 1:
                            act.wait_ge(a_ptT, H)
                            if H >= 2:
                                act.wait_ge(a_pv, H - 1)
                            last = nc.scalar.activation(a_pt[:, 0, :, :], misc[2][:, :].rearrange("p (b n) -> p b n", n=P), ACT.Copy)
                            if g == 0:
                                last = nc.scalar.activation(a_pt[:, 1, 1:QT, :], misc[3][:, P:].rearrange("p (b n) -> p b n", n=P), ACT.Copy)
                            last.then_inc(a_ptc, 1)

                def sample_exp(k):
                    g, batch = k // 2, k % 2
                    act.wait_ge(s_nb, 6 * n + k + 1)
                    part = s_p[:, batch, S_OFF[g]:S_OFF[g] + S_LEN[g] + NS]
                    nc.scalar.activation(part, part, ACT.Exp, scale=SCALE, bias=a_sst[:, 0, g, batch:batch + 1],
                                         accum_out=a_sst[:, 1, g, batch:batch + 1]).then_inc(s_probs, 1)

                def last_of(i):
                    return i == 11 or K_UNITS[i + 1][:2] != K_UNITS[i][:2]

                act.wait_ge(a_vout, 16 * 9 * (n + 1))
                act.wait_ge(a_kout, K_OUT[NG] * (n + 1))
                for i in range(13):
                    if i < 12:
                        for p in range(PAIRS):
                            act.wait_ge(s_kTp, 3 * (12 * n + i) + p + 1)
                            if i >= 2:
                                act.wait_ge(s_unit, 24 * n + i - 1)
                            nc.scalar.activation(s_kT[:, i % 2, p, :], misc[1 + p][:, :], ACT.Copy).then_inc(s_kTc, 1)
                    if i >= 1 and last_of(i - 1):
                        sample_exp(2 * K_UNITS[i - 1][0] + K_UNITS[i - 1][1])

                def combine_exp(c, w):
                    act.wait_ge(a_dif, 3 * n + c + 1)
                    nc.scalar.activation(a_e[:, c, :, 0:w], a_e[:, c, :, 0:w], ACT.Exp).then_inc(a_exp, 1)

                combine_exp(0, 2)
                for batch in range(2):
                    act.wait_ge(s_ptT, 2 * n + batch + 1)
                    nc.scalar.activation(s_pt[:, batch, 0:4, :], misc[1][:, :].rearrange("p (j n) -> p j n", n=P), ACT.Copy)
                    nc.scalar.activation(s_pt[:, batch, 4:6, :], misc[2][:, 0:2 * P].rearrange("p (j n) -> p j n", n=P), ACT.Copy)
                    nc.scalar.activation(s_pt[0:NS, batch, 6:8, :], misc[2][0:NS, 2 * P:4 * P].rearrange("p (j n) -> p j n", n=P), ACT.Copy)
                    nc.scalar.activation(s_pt[0:NS, batch, 8, :], misc[3][0:NS, 0:P], ACT.Copy).then_inc(s_ptc, 1)
                combine_exp(1, QT * HG)
                combine_exp(2, QT * HG)
                for i, (batch, g) in enumerate(S_ITEMS):
                    done = max(j for j, u in enumerate(V_UNITS) if u[:2] == (g, batch)) + 1
                    act.wait_ge(s_unit, len(UNITS) * n + 12 + done)
                    nc.scalar.activation(s_kT[:, batch, g, 0:GW], sample_bank(batch, g)[:, 0:GW], ACT.Copy).then_inc(s_oc, 1)
                for i, (batch, g) in enumerate(S_ITEMS):
                    act.wait_ge(s_oT, 6 * n + i + 1)
                    for s in range(2):
                        nc.scalar.activation(sample_cols(act_hi, s, batch, g), sample_out(s, i), ACT.Copy).then_inc(s_hi, 1)
                for f in range(FT):
                    act.wait_ge(a_oT, 9 * n + f + 1)
                    nc.scalar.activation(prompt_cols(act_hi, f), misc[f % 2][:, :].rearrange("p (b i) -> p b i", i=P), ACT.Copy).then_inc(a_ohi, 1)
                for o in range(KD):
                    act_split(act, WeightTile("a_out", l, o + 2))
                gains_after_mixer(act, l)

            @staticmethod
            def dve(dve, l):
                n, m = a_no(l), 2 * l
                for g in range(NG):
                    G = 3 * n + g
                    for j in range(A_TILES):
                        t = WeightTile("a_in", l, A_TILES * g + j)
                        dve_split(dve, WeightTile("a_in", l, t.pos + 2))
                        if t.pos == 0:
                            dve_norm_diag(dve, m)
                            dve.wait_ge(r_ready, norm_no[m] + 1)
                            dve.wait_ge(a_landed, 64 * n + 48)
                            chain(dve, nc.vector.tensor_tensor(a_cos[:, :], a_cos[:, :], R[:, :], ALU.mult))
                            chain(dve, nc.vector.tensor_tensor(a_sin[:, :], a_sin[:, :], R[:, :], ALU.mult))
                        dve.wait_ge(acc_ready, t.n + 1)
                        if j < 2 * PAIRS:
                            dve.wait_ge(a_swapped, 6 * G + j + 1)
                            nc.vector.tensor_tensor(halves(a_rc[:, :]), acc_of(t), halves(a_cos[:, :]), ALU.mult)
                            nc.vector.tensor_tensor(a_qk[:, j, :], a_sw[:, :], a_sin[:, :], ALU.mult).then_inc(evac_done, 1)
                            dve.wait_ge(evac_done, t.n + 1)
                            nc.vector.tensor_tensor(a_qk[:, j, :], a_qk[:, j, :], a_rc[:, :], ALU.add).then_inc(a_rope, 1)
                            dve.wait_ge(a_rope, 6 * G + j + 1)
                        else:
                            nc.vector.tensor_tensor(halves(a_v[:, j - 2 * PAIRS, :]), acc_of(t), halves(R[:, :]), ALU.mult).then_inc(evac_done, 1)
                    for b in range(QT + 1):
                        v = 5 * G + b
                        dve.wait_ge(a_vT, v + 1)
                        if b == 0 and 0 < g:
                            dve.wait_ge(a_vout, 16 * (9 * n + (1, 5)[g - 1]))
                        if b < QT:
                            nc.vector.tensor_copy(a_vtok[:, b, :], acc[:, v % 2, 1, 0:GW]).then_inc(a_vcopy, 1)
                        else:
                            nc.vector.tensor_copy(a_vn[0:NS, g, :], acc[0:NS, v % 2, 1, 0:GW]).then_inc(a_vcopy, 1)
                    dve.wait_ge(a_zero, 2 * (n + 1))
                    for p in range(PAIRS):
                        for s in range(2):
                            r = slice(HD * s, HD * (s + 1))
                            c = (2 * p + s) * DEC_T
                            nc.vector.tensor_copy(a_qbd[r, 3 * g + p, :, c:c + DEC_T],
                                                  a_qk[r, p, SEQ:TOK].rearrange("p (b t) -> p b t", t=DEC_T)).then_inc(a_qcopy, 1)
                    nc.vector.tensor_copy(a_kn[:, 3 * g:3 * g + 3, :], a_qk[:, PAIRS:2 * PAIRS, SEQ:TOK]).then_inc(a_qcopy, 1)
                    mask = a_mask[:, (0, 0, 2)[g], :].unsqueeze(1)
                    for i in range(HG + 2):
                        H = 6 * G + i
                        if i < HG:
                            dve.wait_ge(a_scores, H + 1)
                            if H >= 2:
                                dve.wait_ge(a_ptT, H - 1)
                            last = nc.vector.tensor_tensor(a_p[:, i % 2, :, P:2 * P], acc[:, i % 2, 0, :].rearrange("p (b k) -> p b k", k=P),
                                                           mask.to_broadcast([P, QT, P]), ALU.add)
                            if g == 0:
                                last = nc.vector.tensor_tensor(a_p[:, i % 2, 1:QT, 0:P], acc[:, i % 2, 1, P:].rearrange("p (b k) -> p b k", k=P),
                                                               a_mask[:, 1, :].unsqueeze(1).to_broadcast([P, QT - 1, P]), ALU.add)
                            last.then_inc(a_masked, 1)
                            dve.wait_ge(a_masked, H + 1)
                            chain(dve, nc.vector.tensor_reduce(a_t[:, 0, 0:QT], a_p[:, i % 2, :, (0 if g == 0 else P):2 * P], AX, ALU.max))
                            nc.vector.tensor_scalar(a_st[:, g, :, i], a_t[:, 0, 0:QT], -SCALE, None, ALU.mult).then_inc(a_nb, 1)
                            dve.wait_ge(a_nb, H + 1)
                        if i >= 2:
                            dve.wait_ge(a_pv, H - 1)
                            h = i - 2
                            nc.vector.tensor_copy(a_o[:, g, :, h * HD:(h + 1) * HD],
                                                  misc[h % 2][:, 0:QT * HD].rearrange("p (b d) -> p b d", d=HD)).then_inc(a_ocopy, 1)
                for k in range(6):
                    g, batch = k // 2, k % 2
                    units = [i for i, u in enumerate(K_UNITS) if u[:2] == (g, batch)]
                    dve.wait_ge(s_unit, 24 * n + units[-1] + 1)
                    if k == 0:
                        dve.wait_ge(a_landed, 64 * (n + 1))
                    o, L = S_OFF[g], S_LEN[g]
                    nc.vector.tensor_tensor(s_p[:, batch, o:o + L], acc[:, batch, 0, 0:L], s_mask[:, batch, o:o + L], ALU.add)
                    nc.vector.tensor_tensor(s_p[:, batch, o + L:o + L + NS], acc[:, batch, 1, 0:NS], s_mask[:, batch, o + L:o + L + NS],
                                            ALU.add).then_inc(s_masked, 1)
                    dve.wait_ge(s_masked, 6 * n + k + 1)
                    chain(dve, nc.vector.tensor_reduce(a_t[:, 0, 0:1], s_p[:, batch, o:o + L + NS], AX, ALU.max))
                    nc.vector.tensor_scalar(a_sst[:, 0, g, batch:batch + 1], a_t[:, 0, 0:1], -SCALE, None, ALU.mult).then_inc(s_nb, 1)
                    dve.wait_ge(s_nb, 6 * n + k + 1)

                def combine(c, w, nb, l_sum, shape):
                    lowest, den = shape(a_t[:, c, 0:w]), shape(a_t[:, (c + 1) % 3, 0:w])
                    e = [shape(a_e[:, c, g, 0:w]) for g in range(NG)]
                    f = [shape(a_f[:, c, g, 0:w]) for g in range(NG)]
                    chain(dve, nc.vector.tensor_tensor(lowest, nb[0], nb[1], ALU.min))
                    chain(dve, nc.vector.tensor_tensor(lowest, lowest, nb[2], ALU.min))
                    for g in range(NG):
                        last = nc.vector.tensor_tensor(e[g], lowest, nb[g], ALU.subtract)
                    last.then_inc(a_dif, 1)
                    dve.wait_ge(a_exp, 3 * n + c + 1)
                    for g in range(NG):
                        last = nc.vector.tensor_tensor(f[g], e[g], l_sum[g], ALU.mult)
                    chain(dve, last)
                    chain(dve, nc.vector.tensor_tensor(den, f[0], f[1], ALU.add))
                    chain(dve, nc.vector.tensor_tensor(den, den, f[2], ALU.add))
                    chain(dve, nc.vector.reciprocal(den, den))
                    for g in range(NG):
                        last = nc.vector.tensor_tensor(f[g], e[g], den, ALU.mult)
                    chain(dve, last)

                dve.wait_ge(s_probs, 6 * (n + 1))
                combine(0, 2, [a_sst[:, 0, g, :] for g in range(NG)], [a_sst[:, 1, g, :] for g in range(NG)], lambda ap: ap)
                for batch in range(2):
                    for g in range(NG):
                        part = s_p[:, batch, S_OFF[g]:S_OFF[g] + S_LEN[g] + NS]
                        last = nc.vector.tensor_scalar(part, part, a_f[:, 0, g, batch:batch + 1], None, ALU.mult)
                    last.then_inc(s_pscaled, 1)
                dve.wait_ge(a_back, 32 * (n + 1))
                grid = lambda ap: ap.rearrange("p (b h) -> p b h", h=HG)
                st = [[a_st[:, g, :, s * HG:(s + 1) * HG] for g in range(NG)] for s in range(2)]
                x0 = [a_stx0[:, :, s * HG:(s + 1) * HG] for s in range(2)]
                x1 = [[a_stx1[:, :, (2 * g + s) * HG:(2 * g + s + 1) * HG] for g in range(2)] for s in range(2)]
                combine(1, QT * HG, [st[0][0]] + x1[0], [st[1][0]] + x1[1], grid)
                combine(2, QT * HG, [x0[0]] + st[0][1:], [x0[1]] + st[1][1:], grid)
                for g in range(NG):
                    o = a_o[:, g, :, :].rearrange("p b (h d) -> p (b h) d", d=HD)
                    nc.vector.tensor_tensor(o, o, a_f[:, 1 if g == 0 else 2, g, :].unsqueeze(2).to_broadcast([P, QT * HG, HD]),
                                            ALU.mult).then_inc(a_scaled, 1)
                for i, (batch, g) in enumerate(S_ITEMS):
                    for s in range(2):
                        dve.wait_ge(s_hi, 12 * n + 2 * i + s + 1)
                        nc.vector.tensor_tensor(sample_cols(act_lo, s, batch, g), sample_out(s, i),
                                                sample_cols(act_hi, s, batch, g).bitcast(F32), ALU.subtract).then_inc(s_lo, 1)
                for f in range(FT):
                    dve.wait_ge(a_ohi, 9 * n + f + 1)
                    nc.vector.tensor_tensor(prompt_cols(act_lo, f), misc[f % 2][:, :].rearrange("p (b i) -> p b i", i=P),
                                            prompt_cols(act_hi, f).bitcast(F32), ALU.subtract).then_inc(a_olo, 1)
                for o in range(KD):
                    t = WeightTile("a_out", l, o)
                    dve_split(dve, WeightTile("a_out", l, o + 2))
                    dve.wait_ge(acc_ready, t.n + 1)
                    nc.vector.tensor_tensor(halves(x[:, o, :]), acc_of(t), halves(x[:, o, :]), ALU.add).then_inc(evac_done, 1)
                for k in range(KD):
                    dve_gain(dve, 2 * l + 1, k)

        def sample_bank(batch, g):
            return acc[:, batch, g, :] if g < 2 else misc[batch]

        def sample_out(s, i):
            bank = misc[2 + i % 2][HD * s:HD * (s + 1), :]
            return bass.AP(bank.tensor, bank.offset + s * DEC_T, [bank.ap[0], [P + 2 * DEC_T, PAIRS], [32, BATCH], [1, DEC_T]])

        def sample_cols(buf, s, batch, g):
            c = SEQ + batch * BATCH * DEC_T
            return buf[HD * s:HD * (s + 1), 3 * g:3 * g + 3, c:c + BATCH * DEC_T].rearrange("p f (b t) -> p f b t", t=DEC_T)

        def prompt_cols(buf, f):
            if f < PAIRS:
                return buf[:, f, 0:SEQ].rearrange("p (b i) -> p b i", i=P)
            return buf[:, f, 0:SEQ].rearrange("p (i b) -> p b i", b=QT)

        K_OUT = [16 * sum(DEC_B if b == QT else 1 for g, b in K_ITEMS if g < before) for before in range(NG + 1)]
        mixers[0] = MixA

        HB_, CHUNK, CONV = 8, 64, 4
        QKV = 3 * HB_
        XS = CONV - 1 + DEC_T
        XP = CONV - 1 + SEQ
        XW = XP + DEC_B * XS
        XF = XW - (CONV - 1)
        LEVELS = 6
        TAILB = (CONV - 1) * (1 + DEC_B)
        with ExitStack() as local:
            b_qkv = lsb("b_qkv", [P, QKV, TOK])
            b_z = lsb("b_z", [P, HB_, TOK])
            b_ab = lsb("b_ab", [P, QT + 1, 2 * HB_])
            b_g = lsb("b_g", [P, QT + 1, HB_])
            b_beta = lsb("b_beta", [P, QT + 1, HB_])
            b_G = lsb("b_G", [P, QT + 1, HB_])
            b_be = lsb("b_be", [P, QT + 1, HB_])
            b_kdf = lsb("b_kdf", [P, QT + 1, HB_])
            b_tmp = lsb("b_tmp", [P, 2, QT + 1, HB_])
            b_dl = lsb("b_dl", [P, 2 * QT + DEC_B, HB_])
            b_gm = lsb("b_gm", [NS, DEC_B, HB_])
            b_par = lsb("b_par", [P, 2 * HB_])
            b_rn = lsb("b_rn", [P, QT + 1, 2 * HB_])
            b_cw = lsb("b_cw", [P, CONV * QKV + 1])
            b_tri = lsb("b_tri", [P, 4, P])
            b_bmask = lsb("b_bmask", [NS, DEC_B])
            eps_l2 = lsb("eps_l2", [P, 1])
            with ExitStack() as local:
                b_xp = lsb("b_xp", [P, 2, XW])
                b_xc = lsb("b_xc", [P, 2, XW])
                b_cst = lsb("b_cst", [P, QKV, DEC_B, CONV - 1])
                b_rows = lsb("b_rows", [CONV * QKV + 1, P])
                b_tail = lsb("b_tail", [P, 2, TAILB])
                b_tailT = lsb("b_tailT", [TAILB, 2, 512])
                b_sq = lsb("b_sq", [P, TOK])
                b_wab = lsb("b_wab", [P, KD, 2 * HB_])
                b_wab_hi = lsb("b_wab_hi", [P, KD, 2 * HB_], F32R)
                b_wab_lo = lsb("b_wab_lo", [P, KD, 2 * HB_], F32R)
            with ExitStack() as local:
                b_S = lsb("b_S", [P, HB_, P])
                b_M = lsb("b_M", [P, 2, 2, 4, P])
                b_lvl = lsb("b_lvl", [P, LEVELS, P])
            with ExitStack() as local:
                b_h32 = lsb("b_h32", [P, 2, TOK])
                b_osq = lsb("b_osq", [P, 2, TOK])
        names = ("e1", "e2", "eg", "kbe", "kd", "vb", "T", "U", "Z")
        b_w = {nm: work[f"b_{nm}"] for nm in names}
        b_dmask = work["b_dmask"]
        b_vmask = b_M[0:NS, :, :, :, :].rearrange("p a c h n -> p (a c h n)")[:, 0:DEC_B * P]
        b_late = b_M[0:NS, :, :, :, :].rearrange("p a c h n -> p (a c h n)")[:, DEC_B * P:]
        b_ub = b_late[:, 0:4 * NS].rearrange("p (q n) -> p q n", q=2)
        b_ot = b_late[:, 4 * NS:4 * NS + 2 * P].rearrange("p (q n) -> p q n", q=2)
        b_own = b_w["e1"][:, :, :, :].rearrange("p a h n -> p a (h n)")
        b_landed, b_clanded, b_zero = sem("b_landed"), sem("b_clanded"), sem("b_zero")
        b_setup_pe, b_setup_act = sem("b_setup_pe"), sem("b_setup_act")
        b_pre, b_conv, b_tailc, b_silu, b_sqd, b_sum = sem("b_pre"), sem("b_conv"), sem("b_tailc"), sem("b_silu"), sem("b_sqd"), sem("b_sum")
        b_tlT, b_tlc, b_tlout = sem("b_tlT"), sem("b_tlc"), [sem("b_tlout0"), sem("b_tlout1")]
        b_wabr = sem("b_wabr")
        b_gate_pe, b_gate_act, b_gate_dve = sem("b_gate_pe"), sem("b_gate_act"), sem("b_gate_dve")
        b_bc, b_qk = sem("b_bc"), sem("b_qk")
        b_kvT, b_kv, b_kk, b_e, b_ex, b_a, b_att = (
            sem("b_kvT"), sem("b_kv"), sem("b_kk"), sem("b_e"), sem("b_ex"), sem("b_a"), sem("b_att"))
        b_m, b_zp, b_zc, b_delta, b_tu, b_wT, b_wc = (
            sem("b_m"), sem("b_zp"), sem("b_zc"), sem("b_delta"), sem("b_tu"), sem("b_wT"), sem("b_wc"))
        b_vn, b_vnc, b_ob, b_s, b_oc = sem("b_vn"), sem("b_vnc"), sem("b_ob"), sem("b_s"), sem("b_oc")
        b_sin, b_sout, b_pout = [sem(f"b_sin{i}") for i in range(4)], sem("b_sout"), sem("b_pout")
        b_zm, b_vTc, b_vm, b_su, b_sd = sem("b_zm"), sem("b_vTc"), sem("b_vm"), sem("b_su"), sem("b_sd")
        b_osqd, b_os, b_obc, b_on, b_zo, b_ohi, b_olo = (
            sem("b_osqd"), sem("b_os"), sem("b_obc"), sem("b_on"), sem("b_zo"), sem("b_ohi"), sem("b_olo"))

        def width(i):
            return P if i < QT else NS

        def tcols(i):
            return slice(i * P, i * P + width(i))

        def levels_of(i):
            return LEVELS if i < QT else 2

        def lev(i, k, hb):
            return 12 * i + 2 * k + hb

        def heads(ap):
            return ap.rearrange("p (h n) -> p h n", h=4)

        def sample_state(h):
            return b_qkv[:, HB_:, :].rearrange("p k t -> p (k t)")[:, h * DEC_B * P:(h + 1) * DEC_B * P].rearrange("p (b e) -> p b e", b=DEC_B)

        b_state = b_qkv[0:DEC_B * (CONV - 1), 3 * QKV // 4:QKV, :].rearrange("p k t -> p (k t)")[:, 0:QKV * P]

        def own_columns(q, part):
            block = b_own[:, q, :]
            return bass.AP(block.tensor, block.offset + part * NS, [block.ap[0], [2 * NS + DEC_T, DEC_B], [1, DEC_T]])

        class MixB:

            @staticmethod
            def sp(sp, l):
                place_free(sp, l)
                sp.dma_start(b_rows[0:CONV * QKV, :], aps["b_conv"][0].rearrange("j (k p) -> (j k) p", p=P)).then_inc(b_landed, 16)
                sp.dma_start(b_rows[CONV * QKV:, :], aps["b_norm"]).then_inc(b_landed, 16)
                sp.dma_start(b_par[:, 0:HB_], aps["b_dt_bias"].partition_broadcast(P)).then_inc(b_landed, 16)
                sp.dma_start(b_par[:, HB_:], aps["b_a_log"].partition_broadcast(P)).then_inc(b_landed, 16)
                sp.dma_start(b_tri[:, :, :], aps["c_tri"]).then_inc(b_landed, 16)
                sp.dma_start(b_bmask[:, :], aps["c_bmask"]).then_inc(b_landed, 16)
                sp.dma_start(b_wab[:, :, :], aps["b_w_in"][0].rearrange("(k p) n -> p k n", p=P)[:, :, 4 * HB_ * P:]).then_inc(b_landed, 16)
                sp.dma_start(b_state, aps["state_b_conv"][0].rearrange("b j c -> (b j) c")).then_inc(b_clanded, 16)
                for j in range(32):
                    sp_weights(sp, WeightTile("b_in", l, j + 2))
                    if j >= 4 and j % 4 == 2 and j < 28:
                        c = j // 4 - 1
                        sp.wait_ge(b_tlc, c + 1)
                        cs = slice(c * 512, (c + 1) * 512)
                        sp.dma_start(aps["new_b_conv_p"][0, 0, :, cs], b_tailT[0:3, c % 2, :]).then_inc(b_tlout[c % 2], 16)
                        sp.dma_start(aps["new_b_conv_s"][0].rearrange("b j c -> (b j) c")[:, cs], b_tailT[3:TAILB, c % 2, :]).then_inc(b_tlout[c % 2], 16)
                sp.wait_ge(b_gate_dve, 7)
                for i in range(2):
                    sp.wait_ge(b_tlout[i], 96)
                sp.wait_ge(b_qk, 16)
                sp.dma_start(b_lvl[:, :, :], aps["c_lvl"]).then_inc(b_clanded, 16)
                sp.dma_start(b_dmask[:, :, :], aps["c_dmask"]).then_inc(b_clanded, 16)
                states = aps["state_b_s"][0].rearrange("b h d e -> h d b e")
                new_states = aps["new_b_s_s"][0].rearrange("b h d e -> h d b e")
                sp.wait_ge(b_s, 16)
                sp.dma_start(aps["new_b_s_p"][0, 0].rearrange("h d e -> d h e"), b_S[:, :, :]).then_inc(b_pout, 16)
                sp.wait_ge(b_kk, 2 * (QT + 1))
                for h in range(HB_):
                    if h >= 4:
                        sp.wait_ge(b_sin[h % 4], 16 * (h // 4))
                    sp.dma_start(sample_state(h), states[h]).then_inc(b_sin[h % 4], 16)
                for h in range(HB_):
                    sp.wait_ge(b_sd, h + 1)
                    sp.dma_start(new_states[h], sample_state(h)).then_inc(b_sout, 16)
                sp.wait_ge(b_pout, 16)
                for p in range(2, 10):
                    sp_weights(sp, WeightTile("b_out", l, p))
                sp.wait_ge(b_sout, 16 * HB_)

            @staticmethod
            def pool(pool, l):
                place_free(pool, l)
                for i in range(2):
                    nc.gpsimd.memset(b_xp[:, i, 0:CONV - 1], 0.0).then_inc(b_zero, 1)
                nc.gpsimd.memset(eps_l2[:, :], 1e-6).then_inc(b_zero, 1)
                for j in range(2 * HB_):
                    pool.wait_ge(b_silu, j + 1)
                    if j >= 1:
                        pool.wait_ge(b_sum, j)
                    nc.gpsimd.tensor_tensor(b_sq[:, :], b_qkv[:, j, :], b_qkv[:, j, :], ALU.mult).then_inc(b_sqd, 1)
                pool.wait_ge(b_qk, 16)
                pool.wait_ge(b_gate_dve, 7)
                for i in range(2):
                    pool.wait_ge(b_tlout[i], 96)
                nc.gpsimd.memset(b_S[:, :, :], 0.0).then_inc(b_zero, 1)
                pool.wait_ge(b_clanded, 16 * 3)
                for i in range(QT + 1):
                    w = width(i)
                    for k in range(levels_of(i)):
                        for hb in range(2):
                            pool.wait_ge(b_a, 2 * i + hb + 1)
                            if k >= 2:
                                pool.wait_ge(b_tu, lev(i, k - 2, hb) + 1)
                            nc.gpsimd.tensor_tensor(b_M[0:w, hb, k % 2, :, 0:w], b_w["e1"][0:w, hb, :, 0:w],
                                                    b_lvl[0:w, k, 0:w].unsqueeze(1).to_broadcast([w, 4, w]), ALU.mult).then_inc(b_m, 1)
                pool.wait_ge(b_m, LEVELS * 2 * QT + 4)
                nc.gpsimd.memset(b_own[:, :, :], 0.0).then_inc(b_zero, 1)
                pool.wait_ge(b_wT, 2 * (QT + 1))
                nc.gpsimd.memset(b_ub[:, :, :], 0.0).then_inc(b_zero, 1)
                pool.wait_ge(b_oc, 16 + HB_)
                for h in range(HB_):
                    nc.gpsimd.tensor_tensor(b_z[:, h, :], b_z[:, h, :], b_qkv[:, h, :], ALU.mult).then_inc(b_zo, 1)
                for k in range(KD):
                    pool_sumsq(pool, 2 * l + 1, k)

            @staticmethod
            def pe(pe, l):
                m = 2 * l
                def setup():
                    pe.wait_ge(b_landed, 7 * 16)
                    nc.tensor.transpose(misc[1][:, 0:CONV * QKV + 1], b_rows[:, :], ident[0:CONV * QKV + 1, 0:CONV * QKV + 1]).then_inc(b_setup_pe, 1)
                    pe.wait_ge(b_clanded, 16)
                    R24 = DEC_B * (CONV - 1)
                    for j in range(QKV):
                        nc.tensor.transpose(misc[2 + j // 12][:, (j % 12) * R24:(j % 12 + 1) * R24], b_state[:, j * P:(j + 1) * P],
                                            ident[0:R24, 0:R24]).then_inc(b_setup_pe, 1)

                def tail(j):
                    pe.wait_ge(b_tailc, j + 1)
                    if j == 0:
                        pe.wait_ge(b_setup_act, 3)
                    if j >= 8:
                        pe.wait_ge(b_tlc, j // 4 - 1)
                    nc.tensor.transpose(misc[2 + (j // 4) % 2][0:TAILB, (j % 4) * P:(j % 4 + 1) * P], b_tail[:, j % 2, :], ident[:, :]).then_inc(b_tlT, 1)

                def sums(sq, first, bank, col):
                    for i in range(QT + 1):
                        last = nc.tensor.matmul(bank[0:width(i), first + i * 2 * HB_ + col:first + i * 2 * HB_ + col + 1],
                                                sq[:, tcols(i)], ones[:, 0:1], start=True, stop=True)
                    return last

                for j in range(32):
                    t = WeightTile("b_in", l, j)
                    pe_tile(pe, t, act_hi, act_lo, k_ready=(xg_ready, 8 * split_no[m]) if j == 0 else None,
                            between=(lambda: (pe.wait_ge(b_setup_act, 1), pe_norm_bcast(pe, m))) if j == 1 else None)
                    if j == 0:
                        pe_norm_sum(pe, m)
                        setup()
                    if 1 <= j <= QKV:
                        tail(j - 1)
                    if 2 <= j < 2 * HB_ + 2:
                        pe.wait_ge(b_sqd, j - 1)
                        sums(b_sq, 128, misc[0], j - 2).then_inc(b_sum, 1)
                pe.wait_ge(b_wabr, 1)
                for i in range(QT + 1):
                    for k in range(KD):
                        for q, (a, w) in enumerate(((act_hi, b_wab_hi), (act_lo, b_wab_hi), (act_hi, b_wab_lo))):
                            last = nc.tensor.matmul(misc[1][0:width(i), i * 2 * HB_:(i + 1) * 2 * HB_], a[:, k, tcols(i)], w[:, k, :],
                                                    start=(k == 0 and q == 0), stop=(k == KD - 1 and q == 2))
                last.then_inc(b_gate_pe, 1)
                pe.wait_ge(b_gate_dve, 1)
                pe.wait_ge(evac_done, base["b_in", l] + 32)
                for j in range(2 * HB_):
                    if j >= 2:
                        pe.wait_ge(b_qk, j - 1)
                    for i in range(QT + 1):
                        w = width(i)
                        last = nc.tensor.matmul(acc[:, j % 2, i // QT, (i % QT) * P:(i % QT) * P + w],
                                                b_rn[0:w, i, j:j + 1].to_broadcast([w, P]), ident[0:w, 0:w], start=True, stop=True)
                    last.then_inc(b_bc, 1)
                pe.wait_ge(b_gate_dve, 4)
                pe.wait_ge(b_gate_dve, 5)
                pe.wait_ge(b_tlc, 6)
                for i in range(QT + 1):
                    w, o = width(i), 0 if i < QT else 2
                    for s in range(2):
                        nc.tensor.matmul(misc[2][0:w, (s * 5 + i) * HB_:(s * 5 + i + 1) * HB_], b_tri[0:w, o + s, 0:w], b_g[0:w, i, :],
                                         start=True, stop=True)
                    if i < QT:
                        for s in range(2):
                            nc.tensor.matmul(misc[2][:, 128 + (2 * i + s) * HB_:128 + (2 * i + s + 1) * HB_],
                                             b_tri[:, 1, CHUNK * s:CHUNK * s + 1].to_broadcast([P, P]), b_g[:, i, :], start=True, stop=True)
                nc.tensor.matmul(misc[2][:, 192:256], ones[0:NS, :], b_gm[:, :, :].rearrange("p b h -> p (b h)"), start=True, stop=True).then_inc(b_gate_pe, 1)
                pe.wait_ge(b_gate_dve, 7)
                pe.wait_ge(b_qk, 16)
                pe.wait_ge(b_zero, 4)
                for i in range(QT + 1):
                    w, tc = width(i), tcols(i)
                    for hb in range(2):
                        u = 2 * i + hb
                        if i >= 1:
                            pe.wait_ge(b_oc, 4 * (i - 1) + 2 + hb + 1)
                            pe.wait_ge(b_s, 4 * (i - 1) + 2 + hb + 1)
                        for h in range(4):
                            nc.tensor.transpose(acc[0:w, hb, 0, h * P:(h + 1) * P], b_qkv[:, HB_ + 4 * hb + h, tc], ident[:, :])
                        for h in range(4):
                            last = nc.tensor.transpose(acc[0:w, hb, 1, h * P:(h + 1) * P], b_qkv[:, 2 * HB_ + 4 * hb + h, tc], ident[:, :])
                        last.then_inc(b_kvT, 1)
                    for hb in range(2):
                        u = 2 * i + hb
                        for h in range(4):
                            kT = b_qkv[:, HB_ + 4 * hb + h, tc]
                            nc.tensor.matmul(misc[2 * hb][0:w, h * P:h * P + w], kT, kT, start=True, stop=True)
                        for h in range(4):
                            nc.tensor.matmul(misc[2 * hb + 1][0:w, h * P:h * P + w], b_qkv[:, HB_ + 4 * hb + h, tc],
                                             b_qkv[:, 4 * hb + h, tc], start=True, stop=True)
                        pe.wait_ge(b_kv, u + 1)
                        for h in range(4):
                            hh = 4 * hb + h
                            last = nc.tensor.matmul(acc[:, hb, 0, h * P:h * P + w], b_g[0:w, i, hh:hh + 1].to_broadcast([w, P]),
                                                    b_tri[0:w, 0 if i < QT else 2, 0:w], start=True, stop=True)
                        last.then_inc(b_kk, 1)
                    for k in range(levels_of(i)):
                        for hb in range(2):
                            pe.wait_ge(b_m, lev(i, k, hb) + 1)
                            if k == 0:
                                pe.wait_ge(b_att, 2 * i + hb + 1)
                            else:
                                pe.wait_ge(b_tu, lev(i, k - 1, hb) + 1)
                            for h in range(4):
                                last = nc.tensor.matmul(misc[2 * hb][0:w, h * P:h * P + w], b_M[0:w, hb, k % 2, h, 0:w],
                                                        ident[0:w, 0:w] if k == 0 else b_w["U"][0:w, hb, h, 0:w], start=True, stop=True)
                            last.then_inc(b_zp, 1)
                        if k == 0:
                            continue
                        for hb in range(2):
                            pe.wait_ge(b_zc, lev(i, k, hb) + 1)
                            for h in range(4):
                                last = nc.tensor.matmul(misc[2 * hb + 1][0:w, h * P:h * P + w], b_w["T"][0:w, hb, h, 0:w],
                                                        b_w["Z"][0:w, hb, h, 0:w], start=True, stop=True)
                            if k < levels_of(i) - 1:
                                for h in range(4):
                                    last = nc.tensor.matmul(acc[0:w, hb, 0, h * P:h * P + w], b_w["Z"][0:w, hb, h, 0:w],
                                                            b_w["T"][0:w, hb, h, 0:w], start=True, stop=True)
                            last.then_inc(b_delta, 1)
                    for hb in range(2):
                        pe.wait_ge(b_tu, lev(i, levels_of(i) - 1, hb) + 1)
                        for h in range(4):
                            last = nc.tensor.matmul(misc[2 * hb][:, h * P:h * P + w], b_w["kbe"][0:w, hb, h, :], b_w["U"][0:w, hb, h, 0:w],
                                                    start=True, stop=True)
                        last.then_inc(b_wT, 1)
                    if i < QT:
                        for n in range(2):
                            c = 4 * i + 2 * n
                            r = slice(CHUNK * n, CHUNK * (n + 1))
                            for hb in range(2):
                                pe.wait_ge(b_wc, 2 * i + hb + 1)
                                if c >= 2:
                                    pe.wait_ge(b_s, c - 2 + hb + 1)
                                for h in range(4):
                                    out = misc[2 * hb + 1][r, h * P:(h + 1) * P]
                                    nc.tensor.matmul(out, b_w["U"][:, hb, h, r], b_w["vb"][:, hb, h, :], start=True, stop=False)
                                    last = nc.tensor.matmul(out, b_w["Z"][:, hb, h, r], b_S[:, 4 * hb + h, :], start=False, stop=True)
                                last.then_inc(b_vn, 1)
                            for hb in range(2):
                                pe.wait_ge(b_vnc, c + hb + 1)
                                if n == 1:
                                    pe.wait_ge(b_oc, c - 2 + hb + 1)
                                for h in range(4):
                                    out = acc[:, hb, 0, h * CHUNK:(h + 1) * CHUNK]
                                    nc.tensor.matmul(out, b_S[:, 4 * hb + h, :], b_w["eg"][:, hb, h, r], start=True, stop=False)
                                    nc.tensor.matmul(out, b_w["T"][r, hb, h, :], b_w["e2"][r, hb, h, r], start=False, stop=True)
                                for h in range(4):
                                    last = nc.tensor.matmul(acc[:, hb, 1, h * P:(h + 1) * P], b_w["kd"][r, hb, h, :], b_w["T"][r, hb, h, :],
                                                            start=True, stop=True)
                                last.then_inc(b_ob, 1)
                def old_state(h):
                    pe.wait_ge(b_zm, h + 1)
                    pe.wait_ge(b_sin[h % 4], 16 * (h // 4 + 1))
                    if h >= 2:
                        pe.wait_ge(b_vTc, h - 1)
                    out = acc[0:2 * NS, h % 2, 0, 0:P]
                    nc.tensor.matmul(out, b_ub[:, h % 2, :], b_w["vb"][0:NS, h // 4, h % 4, :], start=True, stop=False)
                    for b in range(DEC_B):
                        last = nc.tensor.matmul(out, b_own[:, h % 2, 2 * NS * b:2 * NS * (b + 1)], sample_state(h)[:, b, :],
                                                start=False, stop=(b == DEC_B - 1))
                    last.then_inc(b_vn, 1)

                pe.wait_ge(b_wc, 2 * QT + 2)
                pe.wait_ge(b_oc, 16)
                pe.wait_ge(b_s, 16)
                old_state(0)
                for h in range(HB_):
                    hb, hh = h // 4, h % 4
                    if h + 1 < HB_:
                        old_state(h + 1)
                    pe.wait_ge(b_vTc, h + 1)
                    if h >= 2:
                        pe.wait_ge(b_oc, 16 + h - 1)
                    nc.tensor.matmul(acc[:, h % 2, 1, 0:NS], b_ot[:, h % 2, :], ident[0:NS, 0:NS], start=True, stop=False)
                    nc.tensor.matmul(acc[:, h % 2, 1, 0:NS], b_w["T"][0:NS, hb, hh, :], b_w["e2"][0:NS, hb, hh, 0:NS],
                                     start=False, stop=True).then_inc(b_ob, 1)
                    pe.wait_ge(b_vm, h + 1)
                    if h >= 2:
                        pe.wait_ge(b_sd, h - 1)
                    for s in range(2):
                        last = nc.tensor.matmul(misc[2 * (h % 2) + s][:, :], b_w["kd"][0:NS, hb, hh, :], b_vmask[:, s * 512:(s + 1) * 512],
                                                start=True, stop=True)
                    last.then_inc(b_su, 1)
                pe.wait_ge(b_sd, HB_)
                for h in range(HB_):
                    pe.wait_ge(b_osqd, h + 1)
                    sums(b_osq[:, h % 2, :], 0, misc[2], h).then_inc(b_os, 1)
                pe.wait_ge(b_gate_dve, 8)
                for h in range(HB_):
                    if h >= 2:
                        pe.wait_ge(b_on, h - 1)
                    for i in range(QT + 1):
                        w = width(i)
                        last = nc.tensor.matmul(acc[:, h % 2, i // QT, (i % QT) * P:(i % QT) * P + w],
                                                b_rn[0:w, i, h:h + 1].to_broadcast([w, P]), ident[0:w, 0:w], start=True, stop=True)
                    last.then_inc(b_obc, 1)
                pe.wait_ge(b_on, HB_)
                for o in range(KD):
                    pe_tile(pe, WeightTile("b_out", l, o), act_hi, act_lo, k_ready=(b_olo, 0) if o == 0 else None,
                            k_used=in_used if o == KD - 1 else None)

            @staticmethod
            def act(act, l):
                m = 2 * l
                def sample_of(ap, lo, hi):
                    return ap[:, XP:XW].rearrange("p (b j) -> p b j", j=XS)[:, :, lo:hi]

                act_split(act, WeightTile("b_in", l, 2))
                for j in range(32):
                    if j == 0:
                        act_norm_std(act, m)
                        act.wait_ge(b_setup_pe, 1)
                        nc.scalar.activation(b_cw[:, :], misc[1][:, 0:CONV * QKV + 1], ACT.Copy).then_inc(b_setup_act, 1)
                        for s in range(2):
                            act.wait_ge(b_setup_pe, 12 * (s + 1) + 1)
                            nc.scalar.activation(b_cst[:, 12 * s:12 * s + 12, :, :],
                                                 misc[2 + s][:, 0:288].rearrange("p (k b j) -> p k b j", k=12, b=DEC_B), ACT.Copy).then_inc(b_setup_act, 1)
                        act.wait_ge(b_landed, 7 * 16)
                        nc.scalar.activation(b_wab_hi[:, :, :], b_wab[:, :, :], ACT.Copy).then_inc(b_setup_act, 1)
                        act.wait_ge(b_setup_act, 3)
                        act_norm_R(act, m)
                    if j < QKV:
                        xp = b_xp[:, j % 2, :]
                        if j >= 2:
                            act.wait_ge(b_conv, j - 1)
                        nc.scalar.activation(sample_of(xp, 0, CONV - 1), b_cst[:, j, :, :], ACT.Copy).then_inc(b_pre, 1)
                        act.wait_ge(evac_done, base["b_in", l] + j + 1)
                        if j >= 2:
                            act.wait_ge(b_tlT, j - 1)
                        nc.scalar.activation(b_tail[:, j % 2, 0:3], xp[:, SEQ:XP], ACT.Copy)
                        nc.scalar.activation(b_tail[:, j % 2, 3:].rearrange("p (b j) -> p b j", b=DEC_B), sample_of(xp, DEC_T, XS), ACT.Copy).then_inc(b_tailc, 1)
                        act_split(act, WeightTile("b_in", l, j + 3))
                        act.wait_ge(b_conv, j + 1)
                        xc = b_xc[:, j % 2, :]
                        nc.scalar.activation(b_qkv[:, j, 0:SEQ], xc[:, 0:SEQ], ACT.Silu)
                        nc.scalar.activation(b_qkv[:, j, SEQ:].rearrange("p (b t) -> p b t", t=DEC_T), sample_of(xc, 0, DEC_T), ACT.Silu).then_inc(b_silu, 1)
                        if j % 4 == 0 and j:
                            tail_out(act, j // 4 - 1)
                    else:
                        if j == QKV:
                            tail_out(act, 5)
                        act.wait_ge(evac_done, base["b_in", l] + j + 1)
                        if j < 31:
                            act_split(act, WeightTile("b_in", l, j + 3))
                        nc.scalar.activation(b_z[:, j - QKV, :], b_z[:, j - QKV, :], ACT.Silu)
                act.wait_ge(b_sum, 16)
                act.wait_ge(b_zero, 3)
                for i in range(QT + 1):
                    w = width(i)
                    last = nc.scalar.activation(b_rn[0:w, i, :], misc[0][0:w, 128 + 16 * i:144 + 16 * i], ACT.Sqrt, bias=eps_l2[0:w, 0:1])
                last.then_inc(b_gate_act, 1)
                act.wait_ge(b_gate_dve, 2)
                nc.scalar.activation(b_tmp[:, :, :, :], b_tmp[:, :, :, :], ACT.Exp)
                nc.scalar.activation(b_par[:, HB_:], b_par[:, HB_:], ACT.Exp).then_inc(b_gate_act, 1)
                act.wait_ge(b_gate_dve, 3)
                nc.scalar.activation(b_tmp[:, 0, :, :], b_tmp[:, 0, :, :], ACT.Ln).then_inc(b_gate_act, 1)
                act.wait_ge(b_gate_pe, 2)
                nc.scalar.activation(b_dl[:, :, :], misc[2][:, 128:256].rearrange("p (c h) -> p c h", h=HB_), ACT.Exp)
                nc.scalar.activation(b_tmp[:, 1, 0:QT, :], misc[2][:, 40:72].rearrange("p (i h) -> p i h", h=HB_), ACT.Copy)
                nc.scalar.activation(b_tmp[0:NS, 1, QT, :], misc[2][0:NS, 72:80], ACT.Copy)
                nc.scalar.activation(b_G[:, 0:QT, :], misc[2][:, 0:32].rearrange("p (i h) -> p i h", h=HB_), ACT.Copy)
                nc.scalar.activation(b_G[0:NS, QT, :], misc[2][0:NS, 32:40], ACT.Copy).then_inc(b_gate_act, 1)
                act.wait_ge(b_gate_dve, 6)
                act.wait_ge(b_gate_act, 4)
                nc.scalar.activation(b_kdf[:, :, :], b_tmp[:, 1, :, :], ACT.Exp)
                nc.scalar.activation(b_be[:, :, :], b_G[:, :, :], ACT.Exp).then_inc(b_gate_act, 1)
                for i in range(QT + 1):
                    w = width(i)
                    for hb in range(2):
                        u = 2 * i + hb
                        act.wait_ge(b_e, 2 * u + 1)
                        nc.scalar.activation(b_w["e1"][0:w, hb, :, 0:w], b_w["e1"][0:w, hb, :, 0:w], ACT.Exp, scale=-1.0).then_inc(b_ex, 1)
                        act.wait_ge(b_e, 2 * u + 2)
                        nc.scalar.activation(b_w["e2"][0:w, hb, :, 0:w], b_w["e2"][0:w, hb, :, 0:w], ACT.Exp).then_inc(b_ex, 1)
                        nc.scalar.activation(b_w["eg"][:, hb, :, 0:w], heads(acc[:, hb, 0, :])[:, :, 0:w], ACT.Exp).then_inc(b_ex, 1)
                    for k in range(levels_of(i)):
                        for hb in range(2):
                            act.wait_ge(b_zp, lev(i, k, hb) + 1)
                            nc.scalar.activation(b_w["Z"][0:w, hb, :, 0:w], heads(misc[2 * hb][0:w, :])[:, :, 0:w], ACT.Copy).then_inc(b_zc, 1)
                    for hb in range(2):
                        act.wait_ge(b_wT, 2 * i + hb + 1)
                        nc.scalar.activation(b_w["Z"][:, hb, :, 0:w], heads(misc[2 * hb][:, :])[:, :, 0:w], ACT.Copy, scale=-1.0).then_inc(b_wc, 1)
                    if i < QT:
                        for n in range(2):
                            c = 4 * i + 2 * n
                            r = slice(CHUNK * n, CHUNK * (n + 1))
                            for hb in range(2):
                                act.wait_ge(b_vn, c + hb + 1)
                                nc.scalar.activation(b_w["T"][r, hb, :, :], heads(misc[2 * hb + 1][r, :]), ACT.Copy).then_inc(b_vnc, 1)
                            for hb in range(2):
                                act.wait_ge(b_ob, c + hb + 1)
                                o = i * P + n * CHUNK
                                nc.scalar.activation(b_qkv[:, 4 * hb:4 * hb + 4, o:o + CHUNK],
                                                     acc[:, hb, 0, 0:4 * CHUNK].rearrange("p (h c) -> p h c", h=4), ACT.Copy).then_inc(b_oc, 1)
                def v_new_copy(h):
                    act.wait_ge(b_vn, 16 + h + 1)
                    nc.scalar.activation(b_w["T"][0:NS, h // 4, h % 4, :], acc[0:NS, h % 2, 0, 0:P], ACT.Copy)
                    nc.scalar.activation(b_ot[:, h % 2, :], acc[NS:2 * NS, h % 2, 0, 0:P], ACT.Copy).then_inc(b_vTc, 1)

                v_new_copy(0)
                for h in range(HB_):
                    if h + 1 < HB_:
                        v_new_copy(h + 1)
                    act.wait_ge(b_ob, 16 + h + 1)
                    nc.scalar.activation(b_qkv[:, h, SEQ:TOK], acc[:, h % 2, 1, 0:NS], ACT.Copy).then_inc(b_oc, 1)
                act.wait_ge(b_oc, 16 + HB_)
                act.wait_ge(b_pout, 16)
                act.wait_ge(b_su, HB_)
                for h in range(HB_):
                    if h >= 2:
                        act.wait_ge(b_os, h - 1)
                    nc.scalar.activation(b_osq[:, h % 2, :], b_qkv[:, h, :], ACT.Square).then_inc(b_osqd, 1)
                act.wait_ge(b_os, HB_)
                for i in range(QT + 1):
                    w = width(i)
                    last = nc.scalar.activation(b_rn[0:w, i, 0:HB_], misc[2][0:w, 16 * i:16 * i + HB_], ACT.Sqrt, scale=1.0 / P, bias=eps_l2[0:w, 0:1])
                last.then_inc(b_gate_act, 1)
                for h in range(HB_):
                    act.wait_ge(b_on, h + 1)
                    nc.scalar.activation(act_hi[:, h, :], b_h32[:, h % 2, :], ACT.Copy).then_inc(b_ohi, 1)
                for o in range(KD):
                    act_split(act, WeightTile("b_out", l, o + 2))
                gains_after_mixer(act, l)

            @staticmethod
            def dve(dve, l):
                m = 2 * l
                sub = lambda ap, lo, hi: ap[:, XP:XW].rearrange("p (b j) -> p b j", j=XS)[:, :, lo:hi]
                for j in range(32):
                    t = WeightTile("b_in", l, j)
                    dve_split(dve, WeightTile("b_in", l, j + 2))
                    if j == 0:
                        dve_norm_diag(dve, m)
                        dve.wait_ge(r_ready, norm_no[m] + 1)
                        dve.wait_ge(b_setup_act, 4)
                        nc.vector.tensor_tensor(b_wab_lo[:, :, :], b_wab[:, :, :], b_wab_hi[:, :, :].bitcast(F32), ALU.subtract).then_inc(b_wabr, 1)
                        dve.wait_ge(b_setup_act, 1)
                        dve.wait_ge(b_zero, 3)
                    dve.wait_ge(acc_ready, t.n + 1)
                    if j >= QKV:
                        nc.vector.tensor_tensor(halves(b_z[:, j - QKV, :]), acc_of(t), halves(R[:, :]), ALU.mult).then_inc(evac_done, 1)
                        continue
                    xp, xc = b_xp[:, j % 2, :], b_xc[:, j % 2, :]
                    if j >= 2:
                        dve.wait_ge(b_tailc, j - 1)
                        dve.wait_ge(b_silu, j - 1)
                    pre = CONV - 1
                    nc.vector.tensor_tensor(xp[:, pre:pre + HALF], acc[:, t.first % 2, 0, 0:HALF], R[:, 0:HALF], ALU.mult)
                    nc.vector.tensor_tensor(xp[:, pre + HALF:XP], acc[:, t.first % 2, 1, 0:SEQ - HALF], R[:, HALF:SEQ], ALU.mult)
                    nc.vector.tensor_tensor(sub(xp, pre, XS), acc[:, t.first % 2, 1, SEQ - HALF:HALF].rearrange("p (b t) -> p b t", t=DEC_T),
                                            R[:, SEQ:TOK].rearrange("p (b t) -> p b t", t=DEC_T), ALU.mult).then_inc(evac_done, 1)
                    dve.wait_ge(evac_done, t.n + 1)
                    dve.wait_ge(b_pre, j + 1)
                    chain(dve, nc.vector.tensor_scalar(xc[:, 0:XF], xp[:, 0:XF], b_cw[:, j:j + 1], None, ALU.mult))
                    for q in range(1, CONV):
                        ins = nc.vector.scalar_tensor_tensor(xc[:, 0:XF], xp[:, q:q + XF], b_cw[:, QKV * q + j:QKV * q + j + 1], xc[:, 0:XF],
                                                             ALU.mult, ALU.add)
                        if q < CONV - 1:
                            chain(dve, ins)
                    ins.then_inc(b_conv, 1)
                dve.wait_ge(b_gate_act, 1)
                chain(dve, nc.vector.memset(b_tmp[:, :, :, :], 0.0))
                for i in range(QT + 1):
                    w = width(i)
                    last = nc.vector.reciprocal(b_rn[0:w, i, :], b_rn[0:w, i, :])
                chain(dve, last)
                chain(dve, nc.vector.memset(b_ab[:, :, :], 0.0))
                for i in range(QT + 1):
                    w = width(i)
                    last = nc.vector.tensor_scalar(b_rn[0:w, i, 0:HB_], b_rn[0:w, i, 0:HB_], float(P) ** -0.5, None, ALU.mult)
                last.then_inc(b_gate_dve, 1)
                dve.wait_ge(b_gate_pe, 1)
                for i in range(QT + 1):
                    w = width(i)
                    last = nc.vector.tensor_scalar(b_ab[0:w, i, :], misc[1][0:w, 16 * i:16 * i + 16], rstd[0:w, i:i + 1], None, ALU.mult)
                chain(dve, last)
                a5, b5 = b_ab[:, :, 0:HB_], b_ab[:, :, HB_:]
                chain(dve, nc.vector.tensor_tensor(a5, a5, b_par[:, 0:HB_].unsqueeze(1).to_broadcast([P, QT + 1, HB_]), ALU.add))
                nc.vector.scalar_tensor_tensor(b_tmp[:, 0, :, :], a5, -1.0, a5, ALU.mult, ALU.min)
                nc.vector.tensor_scalar(b_tmp[:, 1, :, :], b5, -1.0, None, ALU.mult).then_inc(b_gate_dve, 1)
                dve.wait_ge(b_gate_act, 2)
                chain(dve, nc.vector.tensor_scalar(b_tmp[:, :, :, :], b_tmp[:, :, :, :], 1.0, None, ALU.add))
                nc.vector.reciprocal(b_beta[:, :, :], b_tmp[:, 1, :, :]).then_inc(b_gate_dve, 1)
                dve.wait_ge(b_gate_act, 3)
                chain(dve, nc.vector.scalar_tensor_tensor(b_g[:, :, :], a5, 0.0, b_tmp[:, 0, :, :], ALU.max, ALU.add))
                chain(dve, nc.vector.scalar_tensor_tensor(b_g[:, :, :], b_g[:, :, :], -1.0,
                                                          b_par[:, HB_:].unsqueeze(1).to_broadcast([P, QT + 1, HB_]), ALU.mult, ALU.mult))
                nc.vector.tensor_tensor(b_gm[:, :, :], b_g[0:NS, QT, :].unsqueeze(1).to_broadcast([NS, DEC_B, HB_]),
                                        b_bmask[:, :].unsqueeze(2).to_broadcast([NS, DEC_B, HB_]), ALU.mult).then_inc(b_gate_dve, 1)
                dve.wait_ge(b_gate_dve, 4)
                nc.vector.memset(b_G[:, :, :], 0.0).then_inc(b_gate_dve, 1)
                for j in range(2 * HB_):
                    dve.wait_ge(b_bc, j + 1)
                    nc.vector.tensor_tensor(b_qkv[:, j, 0:SEQ], b_qkv[:, j, 0:SEQ], acc[:, j % 2, 0, :], ALU.mult)
                    nc.vector.tensor_tensor(b_qkv[:, j, SEQ:TOK], b_qkv[:, j, SEQ:TOK], acc[:, j % 2, 1, 0:NS], ALU.mult).then_inc(b_qk, 1)
                dve.wait_ge(b_gate_act, 4)
                nc.vector.tensor_tensor(b_tmp[:, 1, :, :], b_tmp[:, 1, :, :], b_G[:, :, :], ALU.subtract).then_inc(b_gate_dve, 1)
                dve.wait_ge(b_gate_act, 5)
                nc.vector.tensor_tensor(b_be[:, :, :], b_be[:, :, :], b_beta[:, :, :], ALU.mult).then_inc(b_gate_dve, 1)
                dve.wait_ge(b_gate_dve, 7)
                dve.wait_ge(b_clanded, 16 * 3)
                for i in range(QT + 1):
                    w = width(i)
                    o = 0 if i < QT else 2
                    for hb in range(2):
                        u = 2 * i + hb
                        hs = slice(4 * hb, 4 * hb + 4)
                        dve.wait_ge(b_kvT, u + 1)
                        per = lambda f: f[0:w, i, hs].unsqueeze(2).to_broadcast([w, 4, P])
                        nc.vector.tensor_tensor(b_w["kbe"][0:w, hb], heads(acc[0:w, hb, 0, :]), per(b_be), ALU.mult)
                        nc.vector.tensor_tensor(b_w["kd"][0:w, hb], heads(acc[0:w, hb, 0, :]), per(b_kdf), ALU.mult)
                        nc.vector.tensor_tensor(b_w["vb"][0:w, hb], heads(acc[0:w, hb, 1, :]), per(b_beta), ALU.mult).then_inc(b_kv, 1)
                    for hb in range(2):
                        dve.wait_ge(b_kk, 2 * i + hb + 1)
                        for h in range(4):
                            last = nc.vector.scalar_tensor_tensor(b_w["e1"][0:w, hb, h, 0:w], acc[0:w, hb, 0, h * P:h * P + w],
                                                                  b_G[0:w, i, 4 * hb + h:4 * hb + h + 1], b_dmask[0:w, o, 0:w], ALU.subtract, ALU.add)
                        last.then_inc(b_e, 1)
                        for h in range(4):
                            last = nc.vector.scalar_tensor_tensor(b_w["e2"][0:w, hb, h, 0:w], acc[0:w, hb, 0, h * P:h * P + w],
                                                                  b_G[0:w, i, 4 * hb + h:4 * hb + h + 1], b_dmask[0:w, o + 1, 0:w], ALU.subtract, ALU.add)
                        last.then_inc(b_e, 1)
                    for hb in range(2):
                        u = 2 * i + hb
                        dve.wait_ge(b_ex, 3 * u + 1)
                        for h in range(4):
                            last = nc.vector.scalar_tensor_tensor(b_w["e1"][0:w, hb, h, 0:w], misc[2 * hb][0:w, h * P:h * P + w],
                                                                  b_beta[0:w, i, 4 * hb + h:4 * hb + h + 1], b_w["e1"][0:w, hb, h, 0:w],
                                                                  ALU.mult, ALU.mult)
                        last.then_inc(b_a, 1)
                        dve.wait_ge(b_ex, 3 * u + 3)
                        nc.vector.tensor_tensor(b_w["e2"][0:w, hb, :, 0:w], heads(misc[2 * hb + 1][0:w, :])[:, :, 0:w],
                                                b_w["e2"][0:w, hb, :, 0:w], ALU.mult)
                        nc.vector.tensor_tensor(b_w["eg"][:, hb, :, 0:w], b_qkv[:, 4 * hb:4 * hb + 4, tcols(i)],
                                                b_w["eg"][:, hb, :, 0:w], ALU.mult).then_inc(b_att, 1)
                    eye = ident[0:w, 0:w].unsqueeze(1).to_broadcast([w, 4, w])
                    for k in range(levels_of(i)):
                        for hb in range(2):
                            T, U, Z = (b_w[nm][0:w, hb, :, 0:w] for nm in "TUZ")
                            if k == 0:
                                dve.wait_ge(b_zc, lev(i, k, hb) + 1)
                                dve.wait_ge(b_m, lev(i, k, hb) + 1)
                                nc.vector.tensor_tensor(U, eye, Z, ALU.subtract)
                                nc.vector.tensor_tensor(T, eye, b_M[0:w, hb, 0, :, 0:w], ALU.subtract).then_inc(b_tu, 1)
                            else:
                                dve.wait_ge(b_delta, 10 * i + 2 * (k - 1) + hb + 1)
                                if k == 1:
                                    dve.wait_ge(b_tu, lev(i, k, hb) - 1)
                                last = nc.vector.tensor_tensor(U, U, heads(misc[2 * hb + 1][0:w, :])[:, :, 0:w], ALU.subtract)
                                if k < levels_of(i) - 1:
                                    last = nc.vector.tensor_tensor(T, T, heads(acc[0:w, hb, 0, :])[:, :, 0:w], ALU.subtract)
                                last.then_inc(b_tu, 1)
                    if i < QT:
                        for n in range(2):
                            for hb in range(2):
                                c = 4 * i + 2 * n + hb
                                dve.wait_ge(b_ob, c + 1)
                                for h in range(4):
                                    S = b_S[:, 4 * hb + h, :]
                                    last = nc.vector.scalar_tensor_tensor(S, S, b_dl[:, 2 * i + n, 4 * hb + h:4 * hb + h + 1],
                                                                          acc[:, hb, 1, h * P:(h + 1) * P], ALU.mult, ALU.add)
                                last.then_inc(b_s, 1)
                dve.wait_ge(b_zero, 6)
                dve.wait_ge(b_wc, 2 * QT + 2)

                def own(h):
                    hb, hh = h // 4, h % 4
                    for part, nm in enumerate(("Z", "eg")):
                        nc.vector.tensor_copy(own_columns(h % 2, part), b_w[nm][:, hb, hh, 0:NS].rearrange("p (b t) -> p b t", t=DEC_T))
                    nc.vector.tensor_copy(b_ub[:, h % 2, 0:NS], b_w["U"][0:NS, hb, hh, 0:NS]).then_inc(b_zm, 1)

                def state_out(h):
                    dve.wait_ge(b_su, h + 1)
                    for b in range(DEC_B):
                        S = sample_state(h)[:, b, :]
                        last = nc.vector.scalar_tensor_tensor(S, S, b_dl[:, 2 * QT + b, h:h + 1],
                                                              misc[2 * (h % 2) + b // 4][:, (b % 4) * P:(b % 4 + 1) * P], ALU.mult, ALU.add)
                    last.then_inc(b_sd, 1)

                own(0)
                own(1)
                for h in range(HB_):
                    dve.wait_ge(b_vTc, h + 1)
                    if h >= 1:
                        dve.wait_ge(b_su, h)
                    nc.vector.tensor_tensor(b_vmask[:, :].rearrange("p (b e) -> p b e", b=DEC_B),
                                            b_w["T"][0:NS, h // 4, h % 4, :].unsqueeze(1).to_broadcast([NS, DEC_B, P]),
                                            b_bmask[:, :].unsqueeze(2).to_broadcast([NS, DEC_B, P]), ALU.mult).then_inc(b_vm, 1)
                    if h >= 1:
                        state_out(h - 1)
                    if h + 2 < HB_:
                        own(h + 2)
                state_out(HB_ - 1)
                dve.wait_ge(b_gate_act, 6)
                for i in range(QT + 1):
                    w = width(i)
                    last = nc.vector.reciprocal(b_rn[0:w, i, 0:HB_], b_rn[0:w, i, 0:HB_])
                last.then_inc(b_gate_dve, 1)
                nw = b_cw[:, CONV * QKV:CONV * QKV + 1]
                for h in range(HB_):
                    dve.wait_ge(b_obc, h + 1)
                    if h >= 2:
                        dve.wait_ge(b_olo, h - 1)
                    o32 = b_h32[:, h % 2, :]
                    dve.wait_ge(b_zo, h + 1)
                    nc.vector.scalar_tensor_tensor(o32[:, 0:SEQ], b_z[:, h, 0:SEQ], nw, acc[:, h % 2, 0, :], ALU.mult, ALU.mult)
                    nc.vector.scalar_tensor_tensor(o32[:, SEQ:TOK], b_z[:, h, SEQ:TOK], nw, acc[:, h % 2, 1, 0:NS], ALU.mult, ALU.mult).then_inc(b_on, 1)
                    dve.wait_ge(b_ohi, h + 1)
                    nc.vector.tensor_tensor(act_lo[:, h, :], o32, act_hi[:, h, :].bitcast(F32), ALU.subtract).then_inc(b_olo, 1)
                for o in range(KD):
                    t = WeightTile("b_out", l, o)
                    dve_split(dve, WeightTile("b_out", l, o + 2))
                    dve.wait_ge(acc_ready, t.n + 1)
                    nc.vector.tensor_tensor(halves(x[:, o, :]), acc_of(t), halves(x[:, o, :]), ALU.add).then_inc(evac_done, 1)
                for k in range(KD):
                    dve_gain(dve, 2 * l + 1, k)

        def tail_out(act, c):
            act.wait_ge(b_tlT, 4 * c + 4)
            if c >= 2:
                act.wait_ge(b_tlout[c % 2], 32 * (c // 2))
            nc.scalar.activation(b_tailT[:, c % 2, :], misc[2 + c % 2][0:TAILB, :], ACT.Copy).then_inc(b_tlc, 1)

        mixers[1] = MixB

        block = ctx.enter_context(nc.Block())
        first_norm = norms[0]

        def next_norm(l):
            return 2 * (l + 1)

        @block.sync
        def _(sp):
            sp.dma_start(ident[:, :], aps["c_ident"]).then_inc(const_in, 16)
            sp.dma_start(gain_rows[0:DEPTH * KD, :], aps["norm1"].rearrange("l (k p) -> (l k) p", p=P)).then_inc(const_in, 16)
            sp.dma_start(gain_rows[DEPTH * KD:2 * DEPTH * KD, :], aps["norm2"].rearrange("l (k p) -> (l k) p", p=P)).then_inc(const_in, 16)
            sp.dma_start(gain_rows[2 * DEPTH * KD:(2 * DEPTH + 1) * KD, :], aps["norm_f"].rearrange("(k p) -> k p", p=P)).then_inc(const_in, 16)
            sp.dma_start(gain_rows[(2 * DEPTH + 1) * KD:, :], aps["c_scale"][0].rearrange("(k p) -> k p", p=P)).then_inc(const_in, 16)
            for j in range(QT):
                sp.dma_start(x_in[:, j, :], aps["x_prompt"][0, j * P:(j + 1) * P, :]).then_inc(x_landed, 16)
            sp.dma_start(x_in[0:NS, QT, :], aps["x_sample"].rearrange("b t d -> (b t) d")).then_inc(x_landed, 16)
            for p in range(2):
                sp_weights(sp, WeightTile(order[0][0], order[0][1], p))
            for l in layers:
                mixers[l % 3].sp(sp, l)
                sp_mlp(sp, l)
            sp.wait_ge(y_copied, 2 * KD)
            for j in range(QT):
                sp.dma_start(aps["y_prompt"][0, j * P:(j + 1) * P, :], y_out[:, j, :]).then_inc(stored, 16)
            sp.dma_start(aps["y_sample"].rearrange("b t d -> (b t) d"), y_out[0:NS, QT, :]).then_inc(stored, 16)
            sp.wait_ge(stored, 16 * (QT + 1))
            sp.wait_ge(caches_copied, 16 * COPIES * FQ * len(layers))

        @block.gpsimd
        def _(pool):
            nc.gpsimd.memset(ones[:, :], 1.0)
            nc.gpsimd.memset(std[:, :], 1.0)
            nc.gpsimd.memset(eps_col[:, :], EPS).then_inc(consts_set, 1)
            for k in range(KD):
                pool_sumsq(pool, first_norm, k)
            for l in layers:
                mixers[l % 3].pool(pool, l)
                pool_mlp(pool, l, next_norm(l))

        @block.scalar
        def _(act):
            act.wait_ge(gain_T, 1)
            nc.scalar.activation(gains[:, :, :], misc[2][:, 0:(2 * DEPTH + 2) * KD].rearrange("p (m k) -> p m k", k=KD),
                                 ACT.Copy).then_inc(gains_done, 1)
            act.wait_ge(gains_done, 1)
            act.wait_ge(consts_set, 1)
            for k in range(KD):
                if first_norm in split_norms:
                    act_gain(act, first_norm, k)
                if k < 2:
                    act_split(act, WeightTile(order[0][0], order[0][1], k))
            for l in layers:
                mixers[l % 3].act(act, l)
                act_mlp(act, l, next_norm(l))
            act_norm_std(act, 2 * DEPTH)
            act_norm_R(act, 2 * DEPTH)
            for k in range(KD):
                act.wait_ge(y_T_done, k + 1)
                nc.scalar.activation(y_out[:, 0:QT, k * P:(k + 1) * P],
                                     acc[:, k % 2, 0, :].rearrange("p (j n) -> p j n", n=P), ACT.Copy).then_inc(y_copied, 1)
                nc.scalar.activation(y_out[0:NS, QT, k * P:(k + 1) * P], acc[0:NS, k % 2, 1, 0:P], ACT.Copy).then_inc(y_copied, 1)

        @block.vector
        def _(dve):
            dve.wait_ge(gains_done, 1)
            for k in range(KD + 1):
                if k < KD:
                    dve.wait_ge(x_T, k + 1)
                    nc.vector.tensor_copy(x[:, k, 0:SEQ], acc[:, k % 2, 0, :])
                    nc.vector.tensor_copy(x[:, k, SEQ:TOK], acc[:, k % 2, 1, 0:NS]).then_inc(x_ready, 1)
                if k >= 1 and first_norm in split_norms:
                    dve_gain(dve, first_norm, k - 1)
                if k < 2:
                    dve_split(dve, WeightTile(order[0][0], order[0][1], k))
            for l in layers:
                mixers[l % 3].dve(dve, l)
                dve_mlp(dve, l, next_norm(l))
            dve_norm_diag(dve, 2 * DEPTH)
            dve.wait_ge(r_ready, len(norms))
            for k in range(KD):
                if k >= 2:
                    dve.wait_ge(y_T_done, k - 1)
                nc.vector.scalar_tensor_tensor(y_T[:, k % 2, :], x[:, k, :], gains[:, 2 * DEPTH, k:k + 1], R[:, :],
                                               ALU.mult, ALU.mult).then_inc(y_ready, 1)

        @block.tensor
        def _(pe):
            pe.wait_ge(const_in, 80)
            rows = (2 * DEPTH + 2) * KD
            nc.tensor.transpose(misc[2][:, 0:rows], gain_rows[:, :], ident[0:rows, 0:rows]).then_inc(gain_T, 1)
            pe.wait_ge(x_landed, 16 * (QT + 1))
            for k in range(KD):
                if k >= 2:
                    pe.wait_ge(x_ready, k - 1)
                for j in range(QT):
                    nc.tensor.transpose(acc[:, k % 2, 0, j * P:(j + 1) * P], x_in[:, j, k * P:(k + 1) * P], ident[:, :])
                nc.tensor.transpose(acc[:, k % 2, 1, 0:NS], x_in[0:NS, QT, k * P:(k + 1) * P],
                                    ident[0:NS, 0:NS]).then_inc(x_T, 1)
            pe.wait_ge(consts_set, 1)
            pe.wait_ge(x_ready, KD)
            for l in layers:
                mixers[l % 3].pe(pe, l)
                pe_mlp(pe, l)
            pe_norm_sum(pe, 2 * DEPTH)
            pe_norm_bcast(pe, 2 * DEPTH)
            pe.wait_ge(evac_done, total)
            for k in range(KD):
                pe.wait_ge(y_ready, k + 1)
                if k >= 2:
                    pe.wait_ge(y_copied, 2 * (k - 1))
                for j in range(QT):
                    nc.tensor.transpose(acc[:, k % 2, 0, j * P:(j + 1) * P], y_T[:, k % 2, j * P:(j + 1) * P], ident[:, :])
                nc.tensor.transpose(acc[0:NS, k % 2, 1, 0:P], y_T[:, k % 2, SEQ:TOK], ident[:, :]).then_inc(y_T_done, 1)


def constants():
    f = np.float32
    c = {"c_ident": np.eye(P, dtype=f)}
    inv = [[f(1) / f(min(w, t + 1)) for t in range(16)] for w in (2, 4, 8, 16)]
    c["c_pool_inv"] = np.broadcast_to(np.array(inv, f), (P, 4, 16)).copy()
    pos = np.concatenate([np.arange(SEQ), np.tile(SEQ + np.arange(DEC_T), DEC_B)]).astype(f)
    half = 32
    freq = (f(10000.0) ** (-np.arange(half, dtype=f) / f(half))).astype(f)
    ang = (pos[None, :] * freq[:, None]).astype(f)
    cos, sin = np.cos(ang).astype(f), np.sin(ang).astype(f)
    c["c_cos"] = np.tile(cos, (4, 1))
    c["c_sin"] = np.tile(np.concatenate([-sin, sin]), (2, 1))
    i, j = np.arange(P)[:, None], np.arange(P)[None, :]
    allowed = np.stack([j <= i, j >= i, (j <= i) & (i % 4 == j % 4)], axis=1)
    c["c_mask"] = np.where(allowed, f(0), f(-1e30)).astype(f)
    row = np.arange(P)
    t, real = row % 4, row % 32 < 24
    k = np.arange(P)
    cached = [k[None, :] >= t[:, None],
              np.repeat(np.arange(4), P)[None, :] == t[:, None],
              (k // 32)[None, :] == t[:, None]]
    new = np.arange(NS)
    both = []
    for batch in range(2):
        mine = (new // 4)[None, :] == (4 * batch + row // 32)[:, None]
        parts = []
        for g in range(3):
            when = (new % 4)[None, :] <= t[:, None] if g == 0 else (new % 4)[None, :] == t[:, None]
            parts += [cached[g], mine & when]
        both.append(np.concatenate(parts, axis=1) | ~real[:, None])
    c["c_smask"] = np.where(np.stack(both, axis=1), f(0), f(-1e30)).astype(f)
    s, q = np.arange(P)[:, None], np.arange(P)[None, :]
    tri, dmask = [], []
    for n in (64, DEC_T):
        same = s // n == q // n
        tri += [same & (s <= q), same]
        dmask += [np.where(same & (q < s), f(0), f(1e30)), np.where(same & (s <= q), f(0), f(-1e30))]
    c["c_tri"] = np.stack(tri, axis=1).astype(f)
    c["c_dmask"] = np.stack(dmask, axis=1).astype(f)
    lvl = [(s // (2 << k) == q // (2 << k)) & (s // (1 << k) % 2 == 1) & (q // (1 << k) % 2 == 0) for k in range(6)]
    c["c_lvl"] = np.stack(lvl, axis=1).astype(f)
    c["c_bmask"] = (np.arange(NS)[:, None] // DEC_T == np.arange(DEC_B)[None, :]).astype(f)
    return c


INPUTS = ("x_prompt", "x_sample", "cache_a_kv1", "cache_a_kv2", "cache_a_kv3", "state_b_s", "state_b_conv", "state_c_pool",
          "norm1", "norm2", "norm_f", "a_w_in", "a_w_out", "b_w_in", "b_conv", "b_a_log", "b_dt_bias", "b_norm", "b_w_out",
          "c_w", "c_scale", "mlp_w1", "mlp_w2")
KV1, KV2, KV3 = (128, 2, 6, 64), (SEQ, 2, 6, 64), (SEQ, 2, 6, 64)
OUTPUTS = (("y_prompt", (1, SEQ, D)), ("y_sample", (DEC_B, DEC_T, D)),
           ("new_a_kv1_p", (2, 1) + KV1), ("new_a_kv2_p", (2, 1) + KV2), ("new_a_kv3_p", (2, 1) + KV3),
           ("new_b_s_p", (1, 1, 8, P, P)), ("new_b_conv_p", (1, 1, 3, 3 * D)), ("new_c_pool_p", (1, 1, 15, D)),
           ("new_a_kv1_s", (2, DEC_B) + KV1), ("new_a_kv2_s", (2, DEC_B) + KV2), ("new_a_kv3_s", (2, DEC_B) + KV3),
           ("new_b_s_s", (1, DEC_B, 8, P, P)), ("new_b_conv_s", (1, DEC_B, 3, 3 * D)), ("new_c_pool_s", (1, DEC_B, 15, D)))


def kernel(**inputs):
    import concourse.bacc as bacc
    from concourse.bass_utils import run_bass_kernel_spmd

    nc = bacc.Bacc("TRN2", target_bir_lowering=False, num_devices=1)
    arrays = {name: np.ascontiguousarray(inputs[name]) for name in INPUTS}
    arrays.update(constants())
    aps = {name: nc.dram_tensor(name, a.shape, F32, kind="ExternalInput").ap() for name, a in arrays.items()}
    for name, shape in OUTPUTS:
        aps[name] = nc.dram_tensor(name, shape, F32, kind="ExternalOutput").ap()
    build_step(nc, aps)
    results = run_bass_kernel_spmd(nc, [arrays], core_ids=[0]).results[0]
    return tuple(results[name] for name, _ in OUTPUTS)
```
